# Optimizing a Trainium2 kernel written in Bass

```python
import math
import jax, jax.numpy as jnp
from jax import lax
import numpy as np

D_MODEL = 1024
BATCH = 1
SEQ = 512
DEPTH = 2
DEC_BATCH = 8
DEC_SEQ = 4
PAST_LEN = 4096
PAGE_SIZE = 128

CHUNK = 128
A_HEADS = 4
D_A = D_MODEL // 2
A_HEAD_DIM = D_A // A_HEADS
POOL_WINDOWS = (2, 4, 8, 16)
B_GROUPS = len(POOL_WINDOWS)
D_B = D_MODEL // 2
B_GROUP_DIM = D_B // B_GROUPS
POOL_HIST = max(POOL_WINDOWS) - 1
D_C = D_MODEL // 2
CONV_C = 31
D_D = D_MODEL // 2
CONV_D = 3
N_MEM = 256
MEM_HEADS = 4
MEM_HEAD_DIM = D_MODEL // MEM_HEADS
N_GROUPS = 4
EXPERTS_PER_GROUP = 4
N_EXPERTS = N_GROUPS * EXPERTS_PER_GROUP
TOP_K_INNER = 2
D_EXPERT = 512
DN_ALPHA = (2 * DEPTH) ** 0.25
DN_BETA = (8 * DEPTH) ** -0.25
N_EVEN = (DEPTH + 1) // 2
N_ODD = DEPTH // 2
LN_EPS = 1e-5

kernel_name = 'hybrid_gmlp_pool_conformer_shortconv_hmoe_step'

def layer_norm(x, g, b):
    xf = x.astype(jnp.float32)
    mu = jnp.mean(xf, axis=-1, keepdims=True)
    var = jnp.mean(jnp.square(xf - mu), axis=-1, keepdims=True)
    y = (xf - mu) * lax.rsqrt(var + LN_EPS) * g.astype(jnp.float32) + b.astype(jnp.float32)
    return y.astype(x.dtype)

def spatial_gate(u, v, w_s, b_s):
    n, t, _ = v.shape
    n_chunks = -(-t // CHUNK)
    pad = n_chunks * CHUNK - t
    vp = jnp.pad(v, ((0, 0), (0, pad), (0, 0))).reshape(n, n_chunks, CHUNK, A_HEADS, A_HEAD_DIM)
    causal = jnp.tril(jnp.ones((CHUNK, CHUNK), dtype=bool))
    w = jnp.where(causal[None], w_s, 0).astype(v.dtype)
    mixed = jnp.einsum('hts,ncshd->ncthd', w, vp) + b_s.T.astype(v.dtype)[None, None, :, :, None]
    mixed = mixed.reshape(n, n_chunks * CHUNK, D_A)[:, :t]
    return u * mixed

def multi_scale_pool(z, hist, positions):
    zp = jnp.concatenate([hist, z], axis=1)
    t = z.shape[1]
    cs = jnp.pad(jnp.cumsum(zp.astype(jnp.float32), axis=1), ((0, 0), (1, 0), (0, 0)))
    end = cs[:, POOL_HIST + 1:]
    outs = []
    for gi, w in enumerate(POOL_WINDOWS):
        lo, hi = gi * B_GROUP_DIM, (gi + 1) * B_GROUP_DIM
        start = cs[:, POOL_HIST + 1 - w: POOL_HIST + 1 - w + t, lo:hi]
        cnt = jnp.minimum(positions + 1, w).astype(jnp.float32)[None, :, None]
        outs.append((end[:, :, lo:hi] - start) / cnt)
    pooled = jnp.concatenate(outs, axis=-1).astype(z.dtype)
    return pooled - z, zp[:, -POOL_HIST:]

def causal_dwconv(z, hist, w):
    zp = jnp.concatenate([hist, z], axis=1)
    k, c = w.shape
    y = lax.conv_general_dilated(zp, w[:, None, :].astype(zp.dtype), window_strides=(1,), padding='VALID',
                                 dimension_numbers=('NWC', 'WIO', 'NWC'), feature_group_count=c)
    return y, zp[:, -(k - 1):]

def mixer_ab(x, pool_hist, positions, w_in, ln_v_g, ln_v_b, w_s, b_s, w_pool, pool_scale, w_out):
    h = jnp.einsum('ntd,de->nte', x, w_in)
    ua = jax.nn.gelu(h[..., :2 * D_A])
    u = ua[..., :D_A]
    v = layer_norm(ua[..., D_A:], ln_v_g, ln_v_b)
    z = h[..., 2 * D_A:]
    a_out = spatial_gate(u, v, w_s, b_s)
    pooled, new_hist = multi_scale_pool(z, pool_hist, positions)
    n, t, _ = z.shape
    b_out = jnp.einsum('ntgc,gcd->ntgd', pooled.reshape(n, t, B_GROUPS, B_GROUP_DIM), w_pool).reshape(n, t, D_B) * pool_scale
    y = jnp.einsum('nte,ed->ntd', jnp.concatenate([a_out, b_out], axis=-1), w_out)
    return y, v, new_hist

def mixer_cd(x, hist_c, hist_d, w_in, conv_c_w, conv_c_b, ln_c_g, ln_c_b, conv_d_w, w_out):
    h = jnp.einsum('ntd,de->nte', x, w_in)
    glu = h[..., :D_C] * jax.nn.sigmoid(h[..., D_C:2 * D_C])
    cc, new_hist_c = causal_dwconv(glu, hist_c, conv_c_w)
    c_out = jax.nn.silu(layer_norm(cc + conv_c_b, ln_c_g, ln_c_b))
    o = 2 * D_C
    gate_b = h[..., o:o + D_D]
    gate_c = h[..., o + D_D:o + 2 * D_D]
    xt = h[..., o + 2 * D_D:]
    cd, new_hist_d = causal_dwconv(gate_c * xt, hist_d, conv_d_w)
    d_out = gate_b * cd
    y = jnp.einsum('nte,ed->ntd', jnp.concatenate([c_out, d_out], axis=-1), w_out)
    return y, new_hist_c, new_hist_d

def mem_project(mem, w):
    n = mem.shape[0]
    return jnp.einsum('nmd,de->nme', mem, w).reshape(n, N_MEM, MEM_HEADS, MEM_HEAD_DIM)

def mem_attend(x, k, v, w_q, w_o):
    n, t, _ = x.shape
    q = jnp.einsum('ntd,de->nte', x, w_q).reshape(n, t, MEM_HEADS, MEM_HEAD_DIM)
    s = jnp.einsum('nthc,nmhc->nhtm', q, k).astype(jnp.float32) * (MEM_HEAD_DIM ** -0.5)
    p = jax.nn.softmax(s, axis=-1).astype(x.dtype)
    o = jnp.einsum('nhtm,nmhc->nthc', p, v).reshape(n, t, D_MODEL)
    return jnp.einsum('nte,ed->ntd', o, w_o)

def hier_moe(x, w_group, b_group, w_router, b_router, w_gate, w_up, w_down):
    n, t, d = x.shape
    xf = x.reshape(n * t, d)
    g_logits = jnp.einsum('md,dg->mg', xf, w_group).astype(jnp.float32) + b_group.astype(jnp.float32)
    g_prob = jax.nn.softmax(g_logits, axis=-1)
    g_sel = jnp.argmax(g_logits, axis=-1)
    g_w = jnp.take_along_axis(g_prob, g_sel[:, None], axis=-1)
    e_logits = (jnp.einsum('md,de->me', xf, w_router).astype(jnp.float32) + b_router.astype(jnp.float32))
    e_logits = e_logits.reshape(-1, N_GROUPS, EXPERTS_PER_GROUP)
    e_logits = jnp.take_along_axis(e_logits, g_sel[:, None, None], axis=1)[:, 0]
    top_v, top_i = lax.top_k(e_logits, TOP_K_INNER)
    top_w = jax.nn.softmax(top_v, axis=-1) * g_w
    expert_id = g_sel[:, None] * EXPERTS_PER_GROUP + top_i
    gates = jnp.sum(jax.nn.one_hot(expert_id, N_EXPERTS, dtype=jnp.float32) * top_w[..., None], axis=1)
    hg = jnp.einsum('md,edf->mef', xf, w_gate)
    hu = jnp.einsum('md,edf->mef', xf, w_up)
    hid = jax.nn.silu(hg) * hu * gates.astype(x.dtype)[..., None]
    y = jnp.einsum('mef,efd->md', hid, w_down)
    return y.reshape(n, t, d)

def setup_inputs(seed: int = 0) -> dict:
    key = jax.random.key(seed)
    ks = iter(jax.random.split(key, 48))

    def nrm(shape, scale):
        return jax.random.normal(next(ks), shape, jnp.float32) * scale

    def gain(shape):
        return 1.0 + nrm(shape, 0.1)

    dm = D_MODEL ** -0.5
    return {
        'x_prompt': nrm((BATCH, SEQ, D_MODEL), 1.0),
        'x_sample': nrm((DEC_BATCH, DEC_SEQ, D_MODEL), 1.0),
        'cache_mem_k': nrm((DEPTH, DEC_BATCH, N_MEM, MEM_HEADS, MEM_HEAD_DIM), 1.0),
        'cache_mem_v': nrm((DEPTH, DEC_BATCH, N_MEM, MEM_HEADS, MEM_HEAD_DIM), 1.0),
        'state_pool': nrm((N_EVEN, DEC_BATCH, POOL_HIST, D_B), 1.0),
        'state_conv_c': nrm((N_ODD, DEC_BATCH, CONV_C - 1, D_C), 0.5),
        'state_conv_d': nrm((N_ODD, DEC_BATCH, CONV_D - 1, D_D), 1.0),
        'mem_prompt': nrm((BATCH, N_MEM, D_MODEL), 1.0),
        'w_in_ab': nrm((N_EVEN, D_MODEL, 2 * D_A + D_B), dm),
        'ln_v_g': gain((N_EVEN, D_A)),
        'ln_v_b': nrm((N_EVEN, D_A), 0.02),
        'w_spatial': nrm((N_EVEN, A_HEADS, CHUNK, CHUNK), CHUNK ** -0.5),
        'b_spatial': gain((N_EVEN, A_HEADS, CHUNK)),
        'w_pool': nrm((N_EVEN, B_GROUPS, B_GROUP_DIM, B_GROUP_DIM), B_GROUP_DIM ** -0.5),
        'pool_scale': gain((N_EVEN, D_B)),
        'w_out_ab': nrm((N_EVEN, D_A + D_B, D_MODEL), (D_A + D_B) ** -0.5 * DN_BETA),
        'w_in_cd': nrm((N_ODD, D_MODEL, 2 * D_C + 3 * D_D), dm),
        'conv_c_w': nrm((N_ODD, CONV_C, D_C), CONV_C ** -0.5),
        'conv_c_b': nrm((N_ODD, D_C), 0.02),
        'ln_c_g': gain((N_ODD, D_C)),
        'ln_c_b': nrm((N_ODD, D_C), 0.02),
        'conv_d_w': nrm((N_ODD, CONV_D, D_D), CONV_D ** -0.5),
        'w_out_cd': nrm((N_ODD, D_C + D_D, D_MODEL), (D_C + D_D) ** -0.5 * DN_BETA),
        'w_q': nrm((DEPTH, D_MODEL, D_MODEL), dm),
        'w_k': nrm((DEPTH, D_MODEL, D_MODEL), dm),
        'w_v': nrm((DEPTH, D_MODEL, D_MODEL), dm * DN_BETA),
        'w_o': nrm((DEPTH, D_MODEL, D_MODEL), dm * DN_BETA),
        'w_group': nrm((DEPTH, D_MODEL, N_GROUPS), dm),
        'b_group': nrm((DEPTH, N_GROUPS), 0.01),
        'w_router': nrm((DEPTH, D_MODEL, N_EXPERTS), dm),
        'b_router': nrm((DEPTH, N_EXPERTS), 0.01),
        'w_gate': nrm((DEPTH, N_EXPERTS, D_MODEL, D_EXPERT), dm),
        'w_up': nrm((DEPTH, N_EXPERTS, D_MODEL, D_EXPERT), dm),
        'w_down': nrm((DEPTH, N_EXPERTS, D_EXPERT, D_MODEL), D_EXPERT ** -0.5 * DN_BETA),
        'ln_g': gain((DEPTH, 3, D_MODEL)),
        'ln_b': nrm((DEPTH, 3, D_MODEL), 0.02),
    }

def reference(x_prompt, x_sample, cache_mem_k, cache_mem_v, state_pool, state_conv_c, state_conv_d, mem_prompt,
              w_in_ab, ln_v_g, ln_v_b, w_spatial, b_spatial, w_pool, pool_scale, w_out_ab,
              w_in_cd, conv_c_w, conv_c_b, ln_c_g, ln_c_b, conv_d_w, w_out_cd,
              w_q, w_k, w_v, w_o, w_group, b_group, w_router, b_router, w_gate, w_up, w_down, ln_g, ln_b):
    n_p, t_p = x_prompt.shape[0], x_prompt.shape[1]
    t_s = x_sample.shape[1]
    pos_p = jnp.arange(t_p)
    pos_s = PAST_LEN + jnp.arange(t_s)
    hp, hs = x_prompt, x_sample
    mem_k_p, mem_v_p = [], []
    pool_p, pool_s, chunk_v_s = [], [], []
    conv_c_p, conv_c_s, conv_d_p, conv_d_s = [], [], [], []
    for l in range(DEPTH):
        if l % 2 == 0:
            i = l // 2
            wts = (w_in_ab[i], ln_v_g[i], ln_v_b[i], w_spatial[i], b_spatial[i], w_pool[i], pool_scale[i], w_out_ab[i])
            zero_pool = jnp.zeros((n_p, POOL_HIST, D_B), hp.dtype)
            mp, _, hist_p = mixer_ab(hp, zero_pool, pos_p, *wts)
            ms, v_rows, hist_s = mixer_ab(hs, state_pool[i], pos_s, *wts)
            pool_p.append(hist_p)
            pool_s.append(hist_s)
            chunk_v_s.append(v_rows)
        else:
            i = l // 2
            wts = (w_in_cd[i], conv_c_w[i], conv_c_b[i], ln_c_g[i], ln_c_b[i], conv_d_w[i], w_out_cd[i])
            zero_c = jnp.zeros((n_p, CONV_C - 1, D_C), hp.dtype)
            zero_d = jnp.zeros((n_p, CONV_D - 1, D_D), hp.dtype)
            mp, hc_p, hd_p = mixer_cd(hp, zero_c, zero_d, *wts)
            ms, hc_s, hd_s = mixer_cd(hs, state_conv_c[i], state_conv_d[i], *wts)
            conv_c_p.append(hc_p)
            conv_c_s.append(hc_s)
            conv_d_p.append(hd_p)
            conv_d_s.append(hd_s)
        hp = layer_norm(DN_ALPHA * hp + mp, ln_g[l, 0], ln_b[l, 0])
        hs = layer_norm(DN_ALPHA * hs + ms, ln_g[l, 0], ln_b[l, 0])
        kp = mem_project(mem_prompt, w_k[l])
        vp = mem_project(mem_prompt, w_v[l])
        mem_k_p.append(kp)
        mem_v_p.append(vp)
        hp = layer_norm(DN_ALPHA * hp + mem_attend(hp, kp, vp, w_q[l], w_o[l]), ln_g[l, 1], ln_b[l, 1])
        hs = layer_norm(DN_ALPHA * hs + mem_attend(hs, cache_mem_k[l], cache_mem_v[l], w_q[l], w_o[l]), ln_g[l, 1], ln_b[l, 1])
        moe_w = (w_group[l], b_group[l], w_router[l], b_router[l], w_gate[l], w_up[l], w_down[l])
        hp = layer_norm(DN_ALPHA * hp + hier_moe(hp, *moe_w), ln_g[l, 2], ln_b[l, 2])
        hs = layer_norm(DN_ALPHA * hs + hier_moe(hs, *moe_w), ln_g[l, 2], ln_b[l, 2])
    return (hp, hs, jnp.stack(mem_k_p), jnp.stack(mem_v_p), jnp.stack(pool_p), jnp.stack(conv_c_p), jnp.stack(conv_d_p),
            jnp.stack(chunk_v_s), jnp.stack(pool_s), jnp.stack(conv_c_s), jnp.stack(conv_d_s))


_drawn_inputs = setup_inputs


def setup_inputs(seed=0):
    import zlib

    import numpy as np

    out = dict(_drawn_inputs(seed))
    spreads = {}
    factors = {'ln_v_b': 2.734,
     'conv_c_b': 8.0,
     'ln_c_g': 3.112,
     'ln_c_b': 8.0,
     'b_group': 5.588,
     'b_router': 7.202}
    for name, (base, spread) in spreads.items():
        noise = np.random.default_rng([zlib.crc32(name.encode()), seed]).standard_normal(out[name].shape)
        drawn = base * np.exp(spread * noise) if base else spread * noise
        out[name] = __import__('jax').numpy.asarray(drawn.astype(out[name].dtype))
    for name, factor in factors.items():
        out[name] = (out[name] * factor).astype(out[name].dtype)
    return out
```

```python
from contextlib import ExitStack

import concourse.bass as bass
from concourse import mybir

ALU = mybir.AluOpType
ACT = mybir.ActivationFunctionType
AX = mybir.AxisListType.X
F32 = mybir.dt.float32
F32R = mybir.dt.float32r
BF16 = mybir.dt.bfloat16
U32 = mybir.dt.uint32
I32 = mybir.dt.int32

P = 128


def trunk_kernel(nc, a, outs):
    D = a["x_prompt"].shape[2]
    SEQ = a["x_prompt"].shape[1]
    NB, TS = a["x_sample"].shape[0], a["x_sample"].shape[1]
    DEPTH = a["w_q"].shape[0]
    NMEM = a["mem_prompt"].shape[1]
    HEADS, HD = a["cache_mem_k"].shape[3], a["cache_mem_k"].shape[4]
    EXPERTS, FF = a["w_gate"].shape[1], a["w_gate"].shape[3]
    GROUPS = a["w_group"].shape[2]
    PER = EXPERTS // GROUPS
    HIST = a["state_pool"].shape[2]
    HALF = D // 2
    TAPS_C, TAPS_D = a["conv_c_w"].shape[1], a["conv_d_w"].shape[1]
    HC, HDD = TAPS_C - 1, TAPS_D - 1
    KC = D // P
    G4 = HALF // P
    NS = NB * TS
    TOK = SEQ + NS
    TILES = SEQ // P + 1
    LASTT = TILES - 1
    MT = NMEM // P
    MOVE = TOK // 2
    PB = MOVE - NS
    ALPHA = (2 * DEPTH) ** 0.25
    EPS = 1e-5
    QSCALE = HD ** -0.5
    SLOTS = P
    LEVELS = -(-TOK // SLOTS) - 1
    FURTHER = 2 * TOK // SLOTS
    RING = 4
    UW = 2048
    ROUTE = GROUPS + EXPERTS
    assert (D, SEQ, NS, NMEM, FF, DEPTH, EXPERTS, HIST) == (1024, 512, 32, 256, 512, 2, 16, 15)

    (y_prompt, y_sample, o_memk, o_memv, o_pool_p, o_cc_p, o_cd_p, o_chunk, o_pool_s, o_cc_s, o_cd_s) = outs

    def rows(t):
        return P if t < LASTT else NS

    def cols(t):
        return slice(t * P, t * P + rows(t))

    UNITS, RAW, SPL, PLAIN = [], {}, {}, {}
    MOE_RAW, MOE_SPL = {}, {}
    count = {"raw": 0, "spl": 0, "plain": 0}

    LANDED = []
    landed_now = [0] * RING

    def lands(pieces):
        slot = len(LANDED) % RING
        landed_now[slot] += 16 * pieces
        LANDED.append(landed_now[slot])

    def plan(key, dst_split, src, wait_kv=False, pieces=1):
        RAW[key] = count["raw"]
        count["raw"] += 1
        lands(pieces)
        kind = "spl" if dst_split else "plain"
        (SPL if dst_split else PLAIN)[key] = count[kind]
        count[kind] += 1
        UNITS.append(("unit", key, src, wait_kv))

    def plan_rows(name, w):
        for q in range(4):
            plan((name, q), True, (lambda q: lambda s: [(s.rearrange("p (k n) -> p k n", k=2),
                 w[256 * q:256 * q + 256, :].rearrange("(k p) n -> p k n", p=P))])(q))

    def plan_cols(name, u, w, c0, c1):
        def src(s):
            v = s.rearrange("p (k n) -> p k n", k=KC)
            wv = w.rearrange("(k p) n -> p k n", p=P)
            if c1 == c0 + P:
                return [(v, wv[:, :, c0:c0 + 2 * P])]
            return [(v[:, :, 0:P], wv[:, :, c0:c0 + P]), (v[:, :, P:2 * P], wv[:, :, c1:c1 + P])]
        plan((name, u), True, src, pieces=1 if c1 == c0 + P else 2)

    def plan_memory(name, src_ap, wait_kv=False):
        plan(name, False, lambda s: [(s.rearrange("p (m n) -> p m n", m=MT),
             src_ap.rearrange("(m p) n -> p m n", p=P))], wait_kv)

    for l in range(DEPTH):
        plan_rows(f"wk{l}", a["w_k"][l])
        plan_rows(f"wv{l}", a["w_v"][l])
    for l in range(DEPTH):
        if l == 0:
            w = a["w_in_ab"][0]
            for u in range(2):
                plan_cols("wz", u, w, D + 256 * u, D + 256 * u + P)
            plan_rows("wuv", w[:, 0:D])
            plan_rows("wout0", a["w_out_ab"][0])
        else:
            w = a["w_in_cd"][0]
            for g in range(G4):
                plan_cols("wglu", g, w, g * P, HALF + g * P)
            for g in range(G4):
                plan_cols("wcx", g, w, 3 * HALF + g * P, 4 * HALF + g * P)
            for u in range(2):
                plan_cols("wgb", u, w, 2 * HALF + 256 * u, 2 * HALF + 256 * u + P)
            plan_rows("wout1", a["w_out_cd"][0])
        for u in range(4):
            plan_cols(f"wq{l}", u, a["w_q"][l], 256 * u, 256 * u + P)
        plan_memory(("k", l), o_memk[l, 0].rearrange("m h c -> m (h c)"), True)
        plan_memory(("v", l), o_memv[l, 0].rearrange("m h c -> m (h c)"), True)
        for b in range(NB):
            plan_memory(("ks", l, b), a["cache_mem_k"][l, b].rearrange("m h c -> m (h c)"))
        for b in range(NB):
            plan_memory(("vs", l, b), a["cache_mem_v"][l, b].rearrange("m h c -> m (h c)"))
        plan_rows(f"wo{l}", a["w_o"][l])
        MOE_RAW[l], MOE_SPL[l] = count["raw"], count["spl"]
        UNITS.append(("moe", l))
        count["raw"] += 6 * EXPERTS
        count["spl"] += 6 * EXPERTS
        for _ in range(6 * EXPERTS):
            lands(1)
    ring_release = []
    for u in UNITS:
        if u[0] == "unit":
            key = u[1]
            ring_release.append(("spl", SPL[key] + 1) if key in SPL else ("plain", PLAIN[key] + 1))
        else:
            ring_release += [("spl", MOE_SPL[u[1]] + j + 1) for j in range(6 * EXPERTS)]

    SHARED = {}

    def share(semaphore, stages):
        at = 0
        for name, n in stages:
            SHARED[name] = (semaphore, at)
            at += n

    LAYERED = dict(q_mm=KC // 2, q_copied=KC, kt_tr=NB + 1, kt_a=NB + 1, kt_b=NB + 1, score_mm=LASTT, prob_max=TILES,
                   prob_exp=TILES, prob_norm=TILES, prob_tr=TILES, pt_copied=LASTT, att_mm=LASTT - 1, att_hi=TILES,
                   att_lo=TILES, sscore_mm=NB, os_copied=1, os_tr=1, wr_hi=1, wr_lo=1, 
                   lg_copied=1, lg_zeroed=1, 
                   scaled=TILES, moe_combined=TILES, out_mm=LASTT, o_mm=LASTT)
    LAYERED.update({name: EXPERTS for name in ("hit", "tok_mm", "tok", "xg_tr", "xg_hi", "xg_lo", "hid", "hid_tr", "hid_hi",
                                               "hid_lo", "ye", "silu")})
    for name, n in LAYERED.items():
        stem, _, rest = name.partition("_")
        share(name, [(f"{stem}{l}_{rest}" if rest else f"{stem}{l}", n) for l in range(DEPTH)])
    for name, parts in (("routing_mm", ("lg{}_mm", "lg{}_tr", "rank{}_mm")), ("routed", ("member{}", "slots{}", "ranked{}", "listed{}")),
                        ("shifted", ("group{}_shift", "expert{}_shift")), ("exponential", ("group{}_exp", "expert{}_exp")),
                        ("only", ("q{}_only", "prob{}_only"))):
        share(name, [(part.format(l), 1) for l in range(DEPTH) for part in parts])
    for event in ("tr", "hi", "lo"):
        share("columns_" + event, [(f"mem_{event}", MT)] + [(f"{stage}_{event}", TILES)
                                                             for stage in ("x", "out0", "o0", "moe0", "out1", "o1")])
    for event in ("mv", "rstd"):
        share("norm_" + event, [(f"{stage}_{event}", TILES) for stage in ("v", "out0", "o0", "moe0", "c", "out1", "o1", "moe1")])
    for event in ("gain", "row"):
        share("norm_" + event, [(f"{stage}_{event}", TILES) for stage in ("v", "out0", "o0", "moe0", "out1", "o1", "moe1")])
    share("norm_res", [(f"{stage}_res", TILES) for stage in ("out0", "o0", "out1", "o1")])

    with ExitStack() as ctx:
        def sb(name, shape, dt=F32):
            return ctx.enter_context(nc.sbuf_tensor(name, shape, dt))

        SIGS = {}

        def sig(name):
            name = SHARED.get(name, (name, 0))[0]
            if name not in SIGS:
                SIGS[name] = ctx.enter_context(nc.semaphore("s_" + name))
            return SIGS[name]

        def past(name):
            return SHARED.get(name, (name, 0))[1]

        raw = [sb(f"raw{i}", [P, UW]) for i in range(RING)]
        whi = [sb(f"whi{i}", [P, UW], F32R) for i in range(RING)]
        wlo = [sb(f"wlo{i}", [P, UW], F32R) for i in range(RING)]
        h = sb("h", [P, TILES, D])
        xhi = sb("xhi", [P, KC, TOK], F32R)
        xlo = sb("xlo", [P, KC, TOK], F32R)
        gb = sb("gb", [P, 2, D])
        ARENA = 11008
        arena = sb("arena", [P, ARENA])
        ident = sb("ident", [P, P])
        iota = sb("iota", [P, P])
        before = sb("before", [P, P], BF16)
        ones = sb("ones", [P, P], BF16)
        tok2 = sb("tok2", [P, TILES, 2], BF16)
        valid = sb("valid", [P, TILES])
        minus_half = sb("minus_half", [P, 1])
        slot0 = sb("slot0", [P, EXPERTS])
        inv_count = sb("inv_count", [P, HIST + 1])
        b_rows = sb("b_rows", [P, G4])
        b_rows_s = sb("b_rows_s", [NS, G4])
        pool_scale = sb("pool_scale", [P, G4])
        CROWS = TAPS_C + TAPS_D + 3
        ccol = sb("ccol", [P, G4, CROWS])
        bn = sb("bn", [P, 2, 6])
        mv = sb("mv", [P, TILES, 2])
        ve = sb("ve", [P, TILES])
        rstd = sb("rstd", [P, TILES])
        flat = sb("flat", [P, 2, G4, NS])
        smax = sb("smax", [P, TILES, HEADS])
        ssum = sb("ssum", [P, TILES, HEADS])
        wrhi = sb("wrhi", [P, KC, ROUTE], F32R)
        wrlo = sb("wrlo", [P, KC, ROUTE], F32R)
        rbias = sb("rbias", [ROUTE, 1])
        lgt = sb("lgt", [P, TILES, ROUTE])
        chosen = sb("chosen", [P, TILES, 3, 4])
        picked = sb("picked", [P, TILES, 4])
        rt = sb("rt", [P, 8, TILES])
        rw = sb("rw", [P, TILES, 2])
        member = sb("member", [P, TILES, EXPERTS], BF16)
        rank = sb("rank", [P, TILES, EXPERTS])
        wait_mark = sb("wait_mark", [1, 3])
        blocks = sb("blocks", [1, 1], I32)
        block_expert = sb("block_expert", [1, FURTHER], I32)
        slot_f = sb("slot_f", [P, TILES, 2])
        slot_of = sb("slot_of", [P, TILES, 2], U32)
        tok_of = [sb(f"tok_of{i}", [P, 1], U32) for i in range(2)]
        ps = ctx.enter_context(nc.psum_tensor("ps", [P, 8, 512], F32))

        h_dram = nc.dram_tensor("h_rows", [TOK, D], F32, kind="Internal").ap()
        y_dram = nc.dram_tensor("expert_rows", [EXPERTS * SLOTS, D], F32, kind="Internal").ap()

        def area(at, n, pattern=None, p=P, **kw):
            v = arena[0:p, at:at + n]
            return v.rearrange(pattern, **kw) if pattern else v

        mem_rows = area(0, 2048, "p (m n) -> p m n", m=MT)
        kv_rows = [area(2048 + 1024 * i, 1024) for i in range(2)]
        ZW, SW = HIST + SEQ, HIST + TS
        ZL = ZW + NB * SW
        zT = area(0, G4 * ZL, "p (g n) -> p g n", g=G4)
        zsum = [area(2716 + ZL * i, ZL) for i in range(2)]
        pz = area(4074, G4 * TOK, "p (g n) -> p g n", g=G4)
        wp = area(6250, 512, "p (g n) -> p g n", g=G4)
        wsT = area(6762, 512, "p (g n) -> p g n", g=G4)
        wsS = area(7274, 128, "p (g n) -> p g n", NS, g=G4)
        pool_rows = area(7402, 512, p=NB * HIST)
        z_tail = area(7914, 512, p=HIST)
        z_new = area(8426, 512, p=NS)
        uv = [area(8938 + 1024 * i, 1024) for i in range(2)]
        ws_rows = area(8938, 512, "p (g n) -> p g n", g=G4)
        CW, CSW = HC + SEQ, HC + TS
        CL = CW + NB * CSW
        gluT = area(0, G4 * CL, "p (g n) -> p g n", g=G4)
        acc = area(3256, G4 * TOK, "p (g n) -> p g n", g=G4)
        c_rows = area(3256, 1024, "p (j n) -> p j n", 4 * HC, j=2)
        d_rows = area(4280, 512, p=NB * HDD)
        tap_rows = area(4792, 512, p=CROWS)
        DW, DSW = HDD + SEQ, HDD + TS
        DL = DW + NB * DSW
        cxT = area(5432, G4 * DL, "p (g n) -> p g n", g=G4)
        cd = area(7680, G4 * TOK, "p (g n) -> p g n", g=G4)
        gate_tmp = [area(9856 + TOK * i, TOK) for i in range(2)]
        ln_rows = [area(9856 + 512 * i, 512) for i in range(2)]
        tails = [gb[:, 0, 0:512], gb[:, 0, 512:1024], gb[:, 1, 0:512], gb[:, 1, 512:1024]]
        qT = area(0, KC * TOK, "p (k n) -> p k n", k=KC)
        KT = [area(4352 + 2048 * i, 2048, "p (k m) -> p k m", k=KC) for i in range(2)]
        prob = area(8448, 1024)
        probT = area(9472, 1024, "p (k n) -> p k n", k=KC)
        q_only = gb[:, :, :].rearrange("p a n -> p (a n)").rearrange("p (k b n) -> p k b n", k=KC, b=NB)
        p_only = area(0, 2048, "p (k b n) -> p k b n", k=KC, b=NB)
        xg = [area(1024 * i, 1024) for i in range(2)]
        silu = area(2048, 512)
        hid = area(2560, 512)
        both = area(2560, 2 * TILES * EXPERTS, "p (j t e) -> p j t e", j=2, t=TILES)
        ye = [area(3072 + 1024 * i, 1024) for i in range(2)]
        hit = [area(5120 + 320 * i, 320).bitcast(BF16).rearrange("p (t n) -> p t n", t=TILES) for i in range(2)]
        logitT = area(6400, 640, p=ROUTE)
        back = [[area(6400 + 2048 * i + 1024 * j, 1024) for j in range(2)] for i in range(2)]
        wr_rows = area(10496, KC * ROUTE, "p (k n) -> p k n", k=KC)
        xgT_hi = xhi[:, :, 0:P]
        xgT_lo = xlo[:, :, 0:P]
        hidT_hi = xhi[:, 0:4, P:2 * P]
        hidT_lo = xlo[:, 0:4, P:2 * P]
        kept = area(2720, TILES * EXPERTS, "p (t e) -> p t e", t=TILES)
        slot_value = area(2800, TILES * EXPERTS, "p (t e) -> p t e", t=TILES)
        gates = lgt[:, :, 0:EXPERTS]
        tok2_f = lgt[:, :, EXPERTS:EXPERTS + 2]
        is_of = area(10656, FURTHER * EXPERTS, "p (j e) -> p j e", j=FURTHER)
        first_rank = area(10784, FURTHER)
        nth = area(2880, FURTHER * EXPERTS, "p (j e) -> p j e", j=FURTHER)
        level = area(10800, LEVELS * EXPERTS, "p (r e) -> p r e", r=LEVELS)
        total = [area(10864 + 24 * i, EXPERTS // 2 + EXPERTS) for i in range(2)]
        own = area(10800, TILES * EXPERTS, "p (t e) -> p t e", t=TILES)
        own_rank = area(10912, TILES)
        own_gate = area(10920, TILES)
        spare = area(10928, 1)
        hit_f = area(5120, TILES * P, "p (t n) -> p t n", t=TILES)
        rowsT = area(4096, 1024, "p (k n) -> p k n", k=KC)
        hidT = area(1024, 512, "p (k n) -> p k n", k=4)
        y_hi = xhi[:, 0:4, 2 * P:4 * P]
        y_lo = xlo[:, 0:4, 2 * P:4 * P]
        hitT = xhi[:, 4:4 + (TILES + 1) // 2, 2 * P:4 * P]
        w_again = [area(6400 + 2048 * i, 2048) for i in range(2)]

        PAIR = [ps[:, 2 * i:2 * i + 2, :] for i in range(4)]
        A_, B_, C_, D_ = range(4)

        def pair_flat(i):
            return PAIR[i].rearrange("p b n -> p (b n)")

        def pair_chunks(i):
            return pair_flat(i).rearrange("p (k n) -> p k n", k=KC)

        block = ctx.enter_context(nc.Block())

        def wait_release(eng, i, shift=0):
            if i >= RING:
                kind, value = ring_release[i - RING]
                eng.wait_ge(sig("lo_made" if kind == "spl" else "plain_used"), value + shift)

        def chained(eng, name):
            n = [0]

            def link(ins):
                n[0] += 1
                ins.then_inc(sig(name), 1)
                eng.wait_ge(sig(name), n[0])
            return link

        def wait_product(eng, tag, t, name):
            if t == LASTT:
                eng.wait_ge(sig("split_used"), SPL[(name, 3)] + 1)
            else:
                eng.wait_ge(sig(tag + "_mm"), past(tag + "_mm") + t + 1)

        def wait_column(eng, tag, name, u, o):
            if o == 1:
                eng.wait_ge(sig("split_used"), SPL[(name, u)] + 1)
            else:
                eng.wait_ge(sig(tag + "_mm"), past(tag + "_mm") + u + 1)

        def first_unit(c):
            return 4 + 6 * (c - 1) if c else 0

        def unit_value(base, k, i):
            return base + k + 1 + 12 * i

        N_SMALL = {0: 5 + NB, 1: 7}
        GB_LOADS = {}
        for n_, key_ in enumerate(("lnv", "out0", "o0", "moe0", "out1", "o1", "moe1")):
            GB_LOADS[key_] = 32 * (n_ + 1)
        TAIL_SOURCES = ((HC, lambda g: gluT[:, g, CW - HC:CW]), (NS, lambda g: flat[:, 0, g, :]),
                        (HDD, lambda g: cxT[:, g, DW - HDD:DW]), (NB * HDD, lambda g: flat[:, 1, g, 0:NB * HDD]))

        def further_blocks(eng, l):
            eng.wait_ge(sig(f"listed{l}"), past(f"listed{l}") + 1)
            return eng.value_load(blocks[0:1, 0:1], min_val=0, max_val=FURTHER)

        def again(l, name):
            return sig(f"again{l}_{name}")

        @block.sync
        def _(sp):
            sp.dma_start(mem_rows, a["mem_prompt"][0].rearrange("(m p) n -> p m n", p=P)).then_inc(sig("mem_landed"), 16)
            i_raw = 0
            for u in UNITS:
                if u[0] == "unit":
                    _, key, src, wait_kv = u
                    if wait_kv:
                        for par in range(2):
                            sp.wait_ge(sig(f"kv_stored{par}"), 16 * 2 * DEPTH)
                    wait_release(sp, i_raw)
                    for dst, part in src(raw[i_raw % RING][:, :]):
                        sp.dma_start(dst, part).then_inc(sig(f"raw_landed{i_raw % RING}"), 16)
                    i_raw += 1
                    if key == ("wk0", 3):
                        sp.dma_start(h[:, 0:LASTT, :], a["x_prompt"][0].rearrange("(t p) n -> p t n", p=P)).then_inc(sig("x_landed"), 16)
                        sp.dma_start(h[0:NS, LASTT, :], a["x_sample"].rearrange("b t n -> (b t) n")).then_inc(sig("x_landed"), 16)
                    continue
                l, rb = u[1], i_raw
                w_gate = a["w_gate"][l].rearrange("e (u k p) n -> u e p k n", u=2, p=P)
                w_up = a["w_up"][l].rearrange("e (u k p) n -> u e p k n", u=2, p=P)
                w_down = a["w_down"][l].rearrange("e (u k p) n -> u e p k n", u=2, p=P)

                def expert_load(k, i, w, e):
                    wait_release(sp, rb + k, 12 * i)
                    slot = (rb + k) % RING
                    if isinstance(e, int):
                        src = w[e]
                    else:
                        src = w[bass.ds(e, 1)].rearrange("a p k n -> (a p) k n")
                    sp.dma_start(raw[slot][:, :].rearrange("p (k n) -> p k n", k=src.shape[1]), src).then_inc(sig(f"raw_landed{slot}"), 16)

                def load_step(c, i):
                    k, n = first_unit(c), c + 2 * i
                    if c < EXPERTS:
                        expert_load(k, i, w_gate[0], n)
                        expert_load(k + 1, i, w_gate[1], n)
                        expert_load(k + 2, i, w_up[0], n)
                        expert_load(k + 3, i, w_up[1], n)
                        k += 4
                    if c:
                        expert_load(k, i, w_down[0], n - 1)
                        expert_load(k + 1, i, w_down[1], n - 1)

                load_step(0, 0)
                for c in range(1, 3):
                    load_step(c, 0)
                with sp.Fori(0, EXPERTS // 2 - 3) as i:
                    load_step(3, i)
                    load_step(4, i)
                for c in range(EXPERTS - 3, EXPERTS + 1):
                    load_step(c, 0)
                i_raw += 6 * EXPERTS
                n = further_blocks(sp, l)
                with sp.Fori(0, FURTHER) as i:
                    with sp.If(n > i):
                        e = sp.value_load(block_expert[0:1, bass.ds(i, 1)], min_val=0, max_val=EXPERTS - 1)
                        for k, w in enumerate((w_gate, w_up, w_down)):
                            for q in range(2):
                                sp.wait_ge(again(l, "used"), max(2 * k + q, 1) + 6 * i)
                                src = w[q][bass.ds(e, 1)].rearrange("a p k n -> (a p) k n")
                                sp.dma_start(w_again[q].rearrange("p (k n) -> p k n", k=src.shape[1]), src).then_inc(again(l, f"landed{q}"), 16)

        @block.tensor
        def _(pe):
            def to_columns(tag, t, m, source, ready):
                ready()
                if t >= 2:
                    pe.wait_ge(sig(tag + "_lo"), past(tag + "_lo") + t - 1)
                pair = pair_chunks(C_ + t % 2)
                for k in range(KC):
                    mm = pe.transpose(pair[:, k, 0:m], source[0:m, k * P:(k + 1) * P], ident[0:m, 0:m])
                mm.then_inc(sig(tag + "_tr"), 1)

            def row_product(tag, t, m, lhs_cols, pair, name, first, last):
                for q in range(4):
                    s = SPL[(name, q)]
                    if first:
                        pe.wait_ge(sig("hi_made"), s + 1)
                        pe.wait_ge(sig("lo_made"), s + 1)
                    for kk in range(2):
                        k = 2 * q + kk
                        for n, (x, w) in enumerate(((xhi, whi), (xlo, whi), (xhi, wlo))):
                            for half in range(2):
                                at = kk * 1024 + 512 * half
                                mm = pe.matmul(ps[0:m, 2 * pair + half, :], x[:, k, lhs_cols], w[s % RING][:, at:at + 512],
                                               start=(k == 0 and n == 0), stop=(k == KC - 1 and n == 2))
                    if last:
                        mm.then_inc(sig("split_used"), 1)
                if not last:
                    mm.then_inc(sig(tag + "_mm"), 1)

            def column_product(tag, name, u, o, pair):
                s = SPL[(name, u)]
                if o == 0:
                    pe.wait_ge(sig("hi_made"), s + 1)
                    pe.wait_ge(sig("lo_made"), s + 1)
                for k in range(KC):
                    at = k * 256 + o * P
                    for n, (x, w) in enumerate(((xhi, whi), (xlo, whi), (xhi, wlo))):
                        for half in range(2):
                            mm = pe.matmul(ps[:, 2 * pair + half, 0:MOVE], w[s % RING][:, at:at + P],
                                           x[:, k, half * MOVE:(half + 1) * MOVE],
                                           start=(k == 0 and n == 0), stop=(k == KC - 1 and n == 2))
                mm.then_inc(sig("split_used" if o else tag + "_mm"), 1)

            def product_then_columns(tag, name, operands_ready):
                operands_ready()
                for t in range(TILES + 1):
                    if t < TILES:
                        if t >= 2:
                            pe.wait_ge(sig(tag + "_res"), past(tag + "_res") + t - 1)
                        row_product(tag, t, rows(t), cols(t), t % 2, name, t == 0, t == LASTT)
                    if t >= 1:
                        to_columns(tag, t - 1, rows(t - 1), h[:, t - 1, :],
                                   lambda: pe.wait_ge(sig(tag + "_row"), past(tag + "_row") + t))

            pe.wait_ge(sig("consts"), 9)
            for m in range(MT):
                to_columns("mem", m, P, mem_rows[:, m, :], lambda: pe.wait_ge(sig("mem_landed"), 16))
            pe.wait_ge(sig("mem_hi"), past("mem_hi") + MT)
            pe.wait_ge(sig("mem_lo"), past("mem_lo") + MT)
            n = 0
            for name in ("wk0", "wv0", "wk1", "wv1"):
                for m in range(MT):
                    if n >= 2:
                        pe.wait_ge(sig("kv_copied"), n - 1)
                    row_product("kv", m, P, slice(m * P, m * P + P), n % 2, name, m == 0, m == MT - 1)
                    n += 1

            pe.wait_ge(sig("small_landed0"), 16 * N_SMALL[0])
            for g in range(G4):
                mm = pe.transpose(ps[:, 4, g * P:(g + 1) * P], ws_rows[:, g, :], ident[:, :])
            mm.then_inc(sig("ws_tr"), 1)
            for g in range(G4):
                mm = pe.transpose(ps[:, 5, g * P:g * P + NB * HIST], pool_rows[:, g * P:(g + 1) * P], ident[0:NB * HIST, 0:NB * HIST])
            mm.then_inc(sig("hist_tr"), 1)
            pe.wait_ge(sig("ws_copied"), 1)
            pe.wait_ge(sig("hist_copied"), 1)
            for t in range(TILES):
                to_columns("x", t, rows(t), h[:, t, :], lambda: pe.wait_ge(sig("x_landed"), 32))
            pe.wait_ge(sig("x_hi"), past("x_hi") + TILES)
            pe.wait_ge(sig("x_lo"), past("x_lo") + TILES)
            pe.wait_ge(sig("kv_copied"), 2 * 2 * DEPTH)
            for u in range(2):
                for o in range(2):
                    if 2 * u + o >= 2:
                        pe.wait_ge(sig("z_copied"), 2 * u + o - 1)
                    column_product("z", "wz", u, o, o)
            pe.wait_ge(sig("z_copied"), 4)

            def mix(t):
                m = rows(t)
                pe.wait_ge(sig("v_row"), past("v_row") + t + 1)
                if t == 0:
                    pe.wait_ge(sig("ws_masked"), 1)
                if t == LASTT:
                    pe.wait_ge(sig("wss_landed"), 16 * NB)
                if t >= 2:
                    pe.wait_ge(sig("gated"), t - 1)
                for g in range(G4):
                    w = wsT[:, g, :] if t < LASTT else wsS[:, g, :]
                    mm = pe.matmul(ps[0:m, 4 + t % 2, g * P:(g + 1) * P], w, uv[t % 2][0:m, 512 + g * P:512 + (g + 1) * P],
                                   start=True, stop=True)
                mm.then_inc(sig("mixed"), 1)

            def gated_columns(t):
                m = rows(t)
                pe.wait_ge(sig("gated"), t + 1)
                if t >= 2:
                    pe.wait_ge(sig("a_lo"), t - 1)
                for g in range(G4):
                    mm = pe.transpose(ps[:, 6 + t % 2, g * P:g * P + m], uv[t % 2][0:m, g * P:(g + 1) * P], ident[0:m, 0:m])
                mm.then_inc(sig("a_tr"), 1)

            for t in range(TILES + 2):
                if t < TILES:
                    if t >= 2:
                        pe.wait_ge(sig("uv_gelu"), t - 1)
                    row_product("uv", t, rows(t), cols(t), t % 2, "wuv", t == 0, t == LASTT)
                if 1 <= t <= TILES:
                    mix(t - 1)
                if t >= 2:
                    gated_columns(t - 2)
            pe.wait_ge(sig("uv_gelu"), TILES)
            for g in range(G4):
                pe.wait_ge(sig("pooled"), g + 1)
                if g >= 2:
                    pe.wait_ge(sig("b_lo"), g - 1)
                pe.matmul(ps[:, 2 * (g % 2), :], wp[:, g, :], pz[:, g, 0:SEQ], start=True, stop=True)
                pe.matmul(ps[:, 2 * (g % 2) + 1, 0:NS], wp[:, g, :], pz[:, g, SEQ:TOK], start=True, stop=True).then_inc(sig("b_mm"), 1)
            pe.wait_ge(sig("a_lo"), TILES)
            for g in range(G4):
                mm = pe.transpose(ps[0:HIST, 4, g * P:(g + 1) * P], zT[:, g, ZW - HIST:ZW], ident[:, :])
            mm.then_inc(sig("z_back"), 1)
            pe.wait_ge(sig("z_flat"), 1)
            for g in range(G4):
                mm = pe.transpose(ps[0:NS, 5, g * P:(g + 1) * P], flat[:, 0, g, :], ident[:, :])
            mm.then_inc(sig("z_back"), 1)

            def out_before(l):
                def waits():
                    if l == 0:
                        pe.wait_ge(sig("b_hi"), G4)
                        pe.wait_ge(sig("b_lo"), G4)
                        pe.wait_ge(sig("a_hi"), TILES)
                        pe.wait_ge(sig("z_back_copied"), 2)
                    else:
                        pe.wait_ge(sig("c_hi"), TILES)
                        pe.wait_ge(sig("c_lo"), TILES)
                        pe.wait_ge(sig("d_hi"), 1)
                        pe.wait_ge(sig("d_lo"), 1)
                        pe.wait_ge(sig("tails_copied"), 4)
                return waits

            def attention(l):
                pe.wait_ge(sig(f"out{l}_hi"), past(f"out{l}_hi") + TILES)
                pe.wait_ge(sig(f"out{l}_lo"), past(f"out{l}_lo") + TILES)
                for u in range(4):
                    for o in range(2):
                        j = 2 * u + o
                        if j >= 2:
                            pe.wait_ge(sig(f"q{l}_copied"), past(f"q{l}_copied") + j - 1)
                        column_product(f"q{l}", f"wq{l}", u, o, o)
                pe.wait_ge(sig(f"q{l}_copied"), past(f"q{l}_copied") + KC)

                def key_columns(key, n):
                    i = RAW[key]
                    pe.wait_ge(sig(f"raw_landed{i % RING}"), LANDED[i])
                    rows_ = raw[i % RING][:, :].rearrange("p (m n) -> p m n", m=MT)
                    for m in range(MT):
                        if n:
                            pe.wait_ge(sig(f"kt{l}_{'ab'[m]}"), past(f"kt{l}_{'ab'[m]}") + n)
                        pair = pair_chunks(C_ + m)
                        for k in range(KC):
                            mm = pe.transpose(pair[:, k, :], rows_[:, m, k * P:(k + 1) * P], ident[:, :])
                        mm.then_inc(sig("plain_used" if m else f"kt{l}_tr"), 1)

                key_columns(("k", l), 0)
                iv = RAW[("v", l)]
                v_rows = raw[iv % RING][:, :].rearrange("p (m n) -> p m n", m=MT)

                def scores(t):
                    if t == 0:
                        pe.wait_ge(sig(f"kt{l}_a"), past(f"kt{l}_a") + 1)
                        pe.wait_ge(sig(f"kt{l}_b"), past(f"kt{l}_b") + 1)
                    if t >= 2:
                        pe.wait_ge(sig(f"prob{l}_exp"), past(f"prob{l}_exp") + t - 1)
                    pair = pair_flat(t % 2)
                    for j in range(KC):
                        hh, c = j // 2, j % 2
                        mm = pe.matmul(pair[:, hh * NMEM:(hh + 1) * NMEM], qT[:, j, cols(t)], KT[0][:, j, :],
                                       start=(c == 0), stop=(c == 1))
                    mm.then_inc(sig(f"score{l}_mm"), 1)

                def prob_columns(t, m):
                    pe.wait_ge(sig(f"prob{l}_norm"), past(f"prob{l}_norm") + t + 1)
                    if t >= 1:
                        pe.wait_ge(sig(f"pt{l}_copied"), past(f"pt{l}_copied") + t)
                    pair = pair_chunks(C_)
                    for k in range(KC):
                        mm = pe.transpose(pair[:, k, 0:m], prob[0:m, k * P:(k + 1) * P], ident[0:m, 0:m])
                    mm.then_inc(sig(f"prob{l}_tr"), 1)

                def mixed_values(t):
                    pe.wait_ge(sig(f"pt{l}_copied"), past(f"pt{l}_copied") + t + 1)
                    if t == 0:
                        pe.wait_ge(sig(f"raw_landed{iv % RING}"), LANDED[iv])
                    else:
                        pe.wait_ge(sig(f"att{l}_lo"), past(f"att{l}_lo") + t)
                    pair = pair_chunks(D_)
                    for j in range(KC):
                        for m in range(MT):
                            mm = pe.matmul(pair[:, j, :], v_rows[:, m, j * P:(j + 1) * P], probT[:, 2 * (j // 2) + m, :],
                                           start=(m == 0), stop=(m == MT - 1))
                    mm.then_inc(sig("plain_used" if t == LASTT - 1 else f"att{l}_mm"), 1)

                scores(0)
                for t in range(LASTT):
                    if t + 1 < LASTT:
                        scores(t + 1)
                    prob_columns(t, P)
                    mixed_values(t)
                for b in range(NB):
                    if b == 0:
                        pe.wait_ge(sig(f"att{l}_lo"), past(f"att{l}_lo") + LASTT)
                    key_columns(("ks", l, b), b + 1)
                    if b == 0:
                        pe.wait_ge(sig(f"q{l}_only"), past(f"q{l}_only") + 1)
                        pe.wait_ge(sig(f"prob{l}_norm"), past(f"prob{l}_norm") + LASTT)
                    pe.wait_ge(sig(f"kt{l}_a"), past(f"kt{l}_a") + b + 2)
                    pe.wait_ge(sig(f"kt{l}_b"), past(f"kt{l}_b") + b + 2)
                    pair = pair_flat(A_)
                    for j in range(KC):
                        hh, c = j // 2, j % 2
                        mm = pe.matmul(pair[0:NS, hh * NMEM:(hh + 1) * NMEM], q_only[:, j, b, :], KT[(b + 1) % 2][:, j, :],
                                       start=(b == 0 and j in (0, 4)), stop=(b == NB - 1 and c == 1), skip_group_check=True)
                    mm.then_inc(sig(f"sscore{l}_mm"), 1)
                prob_columns(LASTT, NS)
                for b in range(NB):
                    if b == 0:
                        pe.wait_ge(sig(f"prob{l}_only"), past(f"prob{l}_only") + 1)
                    i = RAW[("vs", l, b)]
                    pe.wait_ge(sig(f"raw_landed{i % RING}"), LANDED[i])
                    vb = raw[i % RING][:, :].rearrange("p (m n) -> p m n", m=MT)
                    for hh in range(HEADS):
                        for m in range(MT):
                            mm = pe.matmul(pair_flat(B_)[0:NS, hh * HD:(hh + 1) * HD], p_only[:, 2 * hh + m, b, :],
                                           vb[:, m, hh * HD:(hh + 1) * HD],
                                           start=(b == 0 and m == 0 and hh in (0, 2)), stop=(b == NB - 1 and m == 1),
                                           skip_group_check=True)
                    mm.then_inc(sig("plain_used"), 1)
                pe.wait_ge(sig(f"os{l}_copied"), past(f"os{l}_copied") + 1)
                for k in range(KC):
                    mm = pe.transpose(pair_chunks(C_)[:, k, 0:NS], prob[0:NS, k * P:(k + 1) * P], ident[0:NS, 0:NS])
                mm.then_inc(sig(f"os{l}_tr"), 1)

            def o_before(l):
                def waits():
                    pe.wait_ge(sig(f"att{l}_hi"), past(f"att{l}_hi") + TILES)
                    pe.wait_ge(sig(f"att{l}_lo"), past(f"att{l}_lo") + TILES)
                return waits

            def router(l):
                pe.wait_ge(sig(f"o{l}_hi"), past(f"o{l}_hi") + TILES)
                pe.wait_ge(sig(f"o{l}_lo"), past(f"o{l}_lo") + TILES)
                pe.wait_ge(sig(f"wr{l}_hi"), past(f"wr{l}_hi") + 1)
                pe.wait_ge(sig(f"wr{l}_lo"), past(f"wr{l}_lo") + 1)
                for k in range(KC):
                    for n, (x, w) in enumerate(((xhi, wrhi), (xlo, wrhi), (xhi, wrlo))):
                        for half in range(2):
                            mm = pe.matmul(ps[0:ROUTE, half, 0:MOVE], w[:, k, :], x[:, k, half * MOVE:(half + 1) * MOVE],
                                           start=(k == 0 and n == 0), stop=(k == KC - 1 and n == 2))
                mm.then_inc(sig(f"lg{l}_mm"), 1)
                pe.wait_ge(sig(f"lg{l}_copied"), past(f"lg{l}_copied") + 1)
                for t in range(TILES):
                    mm = pe.transpose(ps[:, 2, t * 32:t * 32 + ROUTE], logitT[:, t * P:(t + 1) * P], ident[0:ROUTE, 0:ROUTE])
                mm.then_inc(sig(f"lg{l}_tr"), 1)
                pe.wait_ge(sig(f"member{l}"), past(f"member{l}") + 1)
                for t in range(TILES + 1):
                    for tt in range(min(t + 1, TILES)):
                        mm = pe.matmul(ps[:, 3, t * EXPERTS:(t + 1) * EXPERTS], (before if tt == t else ones)[:, :], member[:, tt, :],
                                       start=(tt == 0), stop=(tt == min(t, LASTT)))
                mm.then_inc(sig(f"rank{l}_mm"), 1)

            def experts(l):
                sb_ = MOE_SPL[l]

                def find_tokens(c, i):
                    n = c + 2 * i
                    pe.wait_ge(sig(f"hit{l}"), past(f"hit{l}") + n + 1)
                    if c:
                        pe.wait_ge(sig(f"tok{l}"), past(f"tok{l}") + n)
                    for t in range(TILES):
                        mm = pe.matmul(ps[:, 7, 0:2], hit[c % 2][:, t, :], tok2[:, t, :], start=(t == 0), stop=(t == LASTT))
                    mm.then_inc(sig(f"tok{l}_mm"), 1)

                def gathered_columns(c, i):
                    n = c + 2 * i
                    pe.wait_ge(sig(f"gathered{c % 2}"), 16 * (l * EXPERTS // 2 + c // 2 + 1) + 16 * i)
                    if c:
                        pe.wait_ge(sig(f"xg{l}_lo"), past(f"xg{l}_lo") + n)
                    for k in range(KC):
                        mm = pe.transpose(pair_chunks(C_)[:, k, :], xg[c % 2][:, k * P:(k + 1) * P], ident[:, :])
                    mm.then_inc(sig(f"xg{l}_tr"), 1)

                def expert_product(k0, i, bank, hi, lo, k_unit, nbanks):
                    for q in range(2):
                        s = (sb_ + k0 + q) % RING
                        pe.wait_ge(sig("hi_made"), unit_value(sb_, k0 + q, i))
                        pe.wait_ge(sig("lo_made"), unit_value(sb_, k0 + q, i))
                        for kk in range(k_unit):
                            k = q * k_unit + kk
                            for n, (x, w) in enumerate(((hi, whi), (lo, whi), (hi, wlo))):
                                for half in range(nbanks):
                                    at = (kk * nbanks + half) * 512
                                    mm = pe.matmul(ps[:, bank + half, :], x[:, k, :], w[s][:, at:at + 512],
                                                   start=(k == 0 and n == 0), stop=(k == 2 * k_unit - 1 and n == 2))
                        mm.then_inc(sig("split_used"), 1)

                def step(c, i):
                    n, k = c + 2 * i, first_unit(c)
                    if c < EXPERTS:
                        pe.wait_ge(sig(f"xg{l}_hi"), past(f"xg{l}_hi") + n + 1)
                        pe.wait_ge(sig(f"xg{l}_lo"), past(f"xg{l}_lo") + n + 1)
                        if c:
                            pe.wait_ge(sig(f"hid{l}"), past(f"hid{l}") + n)
                        expert_product(k, i, 0, xgT_hi, xgT_lo, 4, 1)
                        expert_product(k + 2, i, 1, xgT_hi, xgT_lo, 4, 1)
                        k += 4
                    if c < EXPERTS - 1:
                        gathered_columns(c + 1, i)
                    if c:
                        pe.wait_ge(sig(f"hid{l}_hi"), past(f"hid{l}_hi") + n)
                        pe.wait_ge(sig(f"hid{l}_lo"), past(f"hid{l}_lo") + n)
                        if c > 1:
                            pe.wait_ge(sig(f"ye{l}"), past(f"ye{l}") + n - 1)
                        expert_product(k, i, 2, hidT_hi, hidT_lo, 2, 2)
                    if c < EXPERTS:
                        pe.wait_ge(sig(f"hid{l}"), past(f"hid{l}") + n + 1)
                        if c:
                            pe.wait_ge(sig(f"hid{l}_lo"), past(f"hid{l}_lo") + n)
                        for k in range(4):
                            mm = pe.transpose(ps[:, 6, k * P:(k + 1) * P], hid[:, k * P:(k + 1) * P], ident[:, :])
                        mm.then_inc(sig(f"hid{l}_tr"), 1)
                    if c < EXPERTS - 2:
                        find_tokens(c + 2, i)

                pe.wait_ge(sig(f"ranked{l}"), past(f"ranked{l}") + 1)
                find_tokens(0, 0)
                find_tokens(1, 0)
                gathered_columns(0, 0)
                step(0, 0)
                for c in range(1, 3):
                    step(c, 0)
                with pe.Fori(0, EXPERTS // 2 - 3) as i:
                    step(3, i)
                    step(4, i)
                for c in range(EXPERTS - 3, EXPERTS):
                    step(c, 0)
                step(EXPERTS, 0)

            def further(l):
                pe.wait_ge(sig(f"ye{l}"), past(f"ye{l}") + EXPERTS)
                pe.wait_ge(sig(f"hid{l}_lo"), past(f"hid{l}_lo") + EXPERTS)
                pe.wait_ge(sig(f"tok{l}"), past(f"tok{l}") + EXPERTS)
                pe.transpose(ps[0:1, 7, 0:1], ident[0:1, 0:1], ident[0:1, 0:1]).then_inc(again(l, "used"), 1)
                n = further_blocks(pe, l)
                with pe.Fori(0, FURTHER) as i:
                    with pe.If(n > i):
                        pe.wait_ge(again(l, "hit"), 1 + i)
                        for t in range(TILES):
                            mm = pe.matmul(ps[:, 7, 0:2], hit_f[:, t, :], tok2_f[:, t, :], start=(t == 0), stop=(t == LASTT))
                        mm.then_inc(again(l, "tok_mm"), 1)
                        for t in range(TILES):
                            mm = pe.transpose(pair_flat(C_)[:, t * P:(t + 1) * P], hit_f[:, t, :], ident[:, :])
                        mm.then_inc(again(l, "tr"), 1)
                        pe.wait_ge(again(l, "copied"), 1 + 4 * i)
                        pe.wait_ge(again(l, "gathered"), 16 + 16 * i)
                        for k in range(KC):
                            mm = pe.transpose(pair_chunks(C_)[:, k, :], xg[0][:, k * P:(k + 1) * P], ident[:, :])
                        mm.then_inc(again(l, "tr"), 1)
                        pe.wait_ge(again(l, "copied"), 2 + 4 * i)
                        pe.wait_ge(again(l, "added"), 1 + TILES * i)
                        for part in range(2):
                            for q in range(2):
                                pe.wait_ge(again(l, f"landed{q}"), 16 * (part + 1) + 48 * i)
                                for kk in range(4):
                                    mm = pe.matmul(ps[:, part, :], rowsT[:, 4 * q + kk, :], w_again[q][:, 512 * kk:512 * kk + 512],
                                                   start=(q == 0 and kk == 0), stop=(q == 1 and kk == 3))
                                mm.then_inc(again(l, "used"), 1)
                        pe.wait_ge(again(l, "hid"), 1 + i)
                        for k in range(4):
                            mm = pe.transpose(ps[:, 6, k * P:(k + 1) * P], hid[:, k * P:(k + 1) * P], ident[:, :])
                        mm.then_inc(again(l, "tr"), 1)
                        pe.wait_ge(again(l, "copied"), 3 + 4 * i)
                        for q in range(2):
                            pe.wait_ge(again(l, f"landed{q}"), 48 + 48 * i)
                            for kk in range(2):
                                for half in range(2):
                                    at = 1024 * kk + 512 * half
                                    mm = pe.matmul(ps[:, 2 + half, :], hidT[:, 2 * q + kk, :], w_again[q][:, at:at + 512],
                                                   start=(q == 0 and kk == 0), stop=(q == 1 and kk == 1))
                            mm.then_inc(again(l, "used"), 1)
                        pe.wait_ge(again(l, "copied"), 4 + 4 * i)
                        for t in range(TILES):
                            if t >= 2:
                                pe.wait_ge(again(l, "added"), t + TILES * i)
                            m = rows(t)
                            for half in range(2):
                                for y in (y_hi, y_lo):
                                    mm = pe.matmul(ps[0:m, 2 * (t % 2) + half, :].rearrange("p (k n) -> p k n", k=2),
                                                   hitT[:, t // 2, P * (t % 2):P * (t % 2) + m], y[:, 2 * half:2 * half + 2, :],
                                                   start=y is y_hi, stop=y is y_lo)
                            mm.then_inc(again(l, "share_mm"), 1)

            def combine_columns(l):
                if l == DEPTH - 1:
                    return
                for t in range(TILES):
                    if t == 0:
                        pe.wait_ge(sig(f"xg{l}_lo"), past(f"xg{l}_lo") + EXPERTS)
                        pe.wait_ge(sig(f"hid{l}_lo"), past(f"hid{l}_lo") + EXPERTS)
                    to_columns(f"moe{l}", t, rows(t), h[:, t, :], lambda: pe.wait_ge(sig(f"moe{l}_row"), past(f"moe{l}_row") + t + 1))

            def conv_layer():
                pe.wait_ge(sig("small_landed1"), 16 * N_SMALL[1])
                pe.wait_ge(sig("moe0_lo"), past("moe0_lo") + TILES)
                for g in range(G4):
                    mm = pe.transpose(ps[:, 4, g * P:g * P + CROWS], tap_rows[:, g * P:(g + 1) * P], ident[0:CROWS, 0:CROWS])
                for g in range(G4):
                    mm = pe.transpose(ps[:, 5, g * P:g * P + NB * HDD], d_rows[:, g * P:(g + 1) * P], ident[0:NB * HDD, 0:NB * HDD])
                for j in range(2):
                    for g in range(G4):
                        mm = pe.transpose(ps[:, 6 + j, g * P:g * P + 4 * HC], c_rows[:, j, g * P:(g + 1) * P], ident[0:4 * HC, 0:4 * HC])
                mm.then_inc(sig("hist1_tr"), 1)
                pe.wait_ge(sig("moe0_hi"), past("moe0_hi") + TILES)
                for g in range(G4):
                    if g:
                        pe.wait_ge(sig("glu"), g)
                    column_product("glu", "wglu", g, 0, A_)
                    column_product("glu", "wglu", g, 1, B_)
                pe.wait_ge(sig("glu"), G4)
                for g in range(G4):
                    if g:
                        pe.wait_ge(sig("cx"), g)
                    column_product("cx", "wcx", g, 0, A_)
                    column_product("cx", "wcx", g, 1, B_)
                pe.wait_ge(sig("cx"), G4)
                for u in range(2):
                    for o in range(2):
                        if u:
                            pe.wait_ge(sig("d_out"), o + 1)
                        column_product("gb", "wgb", u, o, o)
                pe.wait_ge(sig("hist1_copied"), 1)
                for t in range(TILES + 1):
                    if t < TILES:
                        m = rows(t)
                        pe.wait_ge(sig("conv"), G4)
                        if t >= 2:
                            pe.wait_ge(sig("c_norm"), t - 1)
                        for g in range(G4):
                            mm = pe.transpose(ps[0:m, 4 + t % 2, g * P:(g + 1) * P], acc[:, g, cols(t)], ident[:, :])
                        mm.then_inc(sig("c_rows"), 1)
                    if t >= 1:
                        tt, m = t - 1, rows(t - 1)
                        pe.wait_ge(sig("c_norm"), tt + 1)
                        if tt >= 2:
                            pe.wait_ge(sig("c_silu"), tt - 1)
                        for g in range(G4):
                            mm = pe.transpose(ps[:, 6 + tt % 2, g * P:g * P + m], ln_rows[tt % 2][0:m, g * P:(g + 1) * P], ident[0:m, 0:m])
                        mm.then_inc(sig("c_tr"), 1)
                pe.wait_ge(sig("d_out"), 4)
                pe.wait_ge(sig("flat_ready"), 2)
                pe.wait_ge(sig("c_norm"), TILES)
                for n, (m, src) in enumerate(TAIL_SOURCES):
                    for g in range(G4):
                        mm = pe.transpose(ps[0:m, n, g * P:(g + 1) * P], src(g), ident[:, :])
                    mm.then_inc(sig("tails_tr"), 1)

            for l in range(DEPTH):
                if l:
                    conv_layer()
                product_then_columns(f"out{l}", f"wout{l}", out_before(l))
                attention(l)
                product_then_columns(f"o{l}", f"wo{l}", o_before(l))
                router(l)
                experts(l)
                further(l)
                combine_columns(l)

        def ahead(c):
            k, nxt = first_unit(c), first_unit(c + 1)
            own = [k + 3] + ([k + 4, k + 5] if c else [])
            return own, [nxt, nxt + 1] + ([nxt + 2] if c < EXPERTS - 1 else [])

        @block.scalar
        def _(act):
            def make_hi(key):
                i, s = RAW[key], SPL[key]
                act.wait_ge(sig(f"raw_landed{i % RING}"), LANDED[i])
                if s >= RING:
                    act.wait_ge(sig("split_used"), s - RING + 1)
                act.activation(whi[s % RING][:, :], raw[i % RING][:, :], ACT.Copy).then_inc(sig("hi_made"), 1)

            def columns_hi(tag, t, m):
                act.wait_ge(sig(tag + "_tr"), past(tag + "_tr") + t + 1)
                act.activation(xhi[:, :, t * P:t * P + m], pair_chunks(C_ + t % 2)[:, :, 0:m], ACT.Copy).then_inc(sig(tag + "_hi"), 1)

            small = sig("small_landed0")
            act.dma_start(ws_rows, a["w_spatial"][0].rearrange("g t s -> t g s")).then_inc(small, 16)
            act.dma_start(pool_rows, a["state_pool"][0].rearrange("b i n -> (b i) n")).then_inc(small, 16)
            act.dma_start(wp, a["w_pool"][0].rearrange("g c d -> c g d")).then_inc(small, 16)
            with nc.allow_non_contiguous_dma(reason="a few hundred words, once"):
                act.dma_start(b_rows[:, :], a["b_spatial"][0].rearrange("g t -> t g")).then_inc(small, 16)
                act.dma_start(pool_scale[:, :], a["pool_scale"][0].rearrange("(g p) -> p g", p=P)).then_inc(small, 16)
                for b in range(NB):
                    act.dma_start(b_rows_s[b * TS:(b + 1) * TS, :], a["b_spatial"][0][:, 0:TS].rearrange("g t -> t g")).then_inc(small, 16)

            for m in range(MT):
                columns_hi("mem", m, P)
            for q in range(4):
                make_hi(("wk0", q))
            names = ("wk0", "wv0", "wk1", "wv1")
            n = 0
            for w, name in enumerate(names):
                for m in range(MT):
                    if m == 0:
                        act.wait_ge(sig("kv_mm"), w + 1)
                    else:
                        nxt = [(names[w + 1], q) for q in range(4)] if w < 3 else [("wz", 0), ("wz", 1), ("wuv", 0), ("wuv", 1)]
                        for key in nxt:
                            make_hi(key)
                        act.wait_ge(sig("split_used"), SPL[(name, 3)] + 1)
                    if n >= 2:
                        act.wait_ge(sig(f"kv_stored{n % 2}"), 16 * (n // 2))
                    act.activation(kv_rows[n % 2], pair_flat(n % 2), ACT.Copy).then_inc(sig("kv_copied"), 1)
                    n += 1

            for t in range(TILES):
                columns_hi("x", t, rows(t))
            act.wait_ge(sig("hist_zeroed"), 1)
            for u in range(2):
                for o in range(2):
                    j = 2 * u + o
                    wait_column(act, "z", "wz", u, o)
                    act.activation(zT[:, j, HIST:HIST + MOVE], ps[:, 2 * o, 0:MOVE], ACT.Copy)
                    act.activation(zT[:, j, HIST + MOVE:ZW], ps[:, 2 * o + 1, 0:PB], ACT.Copy)
                    act.activation(zT[:, j, ZW:ZL].rearrange("p (b s) -> p b s", b=NB)[:, :, HIST:],
                                   ps[:, 2 * o + 1, PB:MOVE].rearrange("p (b s) -> p b s", b=NB), ACT.Copy).then_inc(sig("z_copied"), 1)
                make_hi(("wuv", 2 + u))
            for t in range(TILES + 2):
                if t < TILES:
                    m = rows(t)
                    if t == LASTT:
                        for q in range(4):
                            make_hi(("wout0", q))
                    wait_product(act, "uv", t, "wuv")
                    if t >= 2:
                        act.wait_ge(sig("a_tr"), t - 1)
                    else:
                        act.wait_ge(sig("ws_copied"), 1)
                    act.activation(uv[t % 2][0:m, :], pair_flat(t % 2)[0:m, :], ACT.Gelu_apprx_tanh).then_inc(sig("uv_gelu"), 1)
                if t >= 2:
                    tt, m = t - 2, rows(t - 2)
                    act.wait_ge(sig("a_tr"), tt + 1)
                    act.activation(xhi[:, 0:G4, cols(tt)], ps[:, 6 + tt % 2, :].rearrange("p (g n) -> p g n", g=G4)[:, :, 0:m],
                                   ACT.Copy).then_inc(sig("a_hi"), 1)
            act.wait_ge(sig("small_landed0"), 16 * N_SMALL[0])
            for g in range(G4):
                act.wait_ge(sig("b_mm"), g + 1)
                act.activation(xhi[:, G4 + g, 0:SEQ], ps[:, 2 * (g % 2), :], ACT.Copy, scale=pool_scale[:, g:g + 1])
                act.activation(xhi[:, G4 + g, SEQ:TOK], ps[:, 2 * (g % 2) + 1, 0:NS], ACT.Copy, scale=pool_scale[:, g:g + 1]).then_inc(sig("b_hi"), 1)
            act.wait_ge(sig("z_back"), 1)
            act.activation(z_tail, ps[0:HIST, 4, :], ACT.Copy).then_inc(sig("z_back_copied"), 1)
            act.wait_ge(sig("z_back"), 2)
            act.activation(z_new, ps[0:NS, 5, :], ACT.Copy).then_inc(sig("z_back_copied"), 1)

            def out_columns(tag, next_units):
                for t in range(TILES):
                    if t == LASTT - 1:
                        for key in next_units:
                            make_hi(key)
                    columns_hi(tag, t, rows(t))

            def key_copy(l, n):
                dst = KT[0] if n == 0 else KT[n % 2]
                if n == 0:
                    act.wait_ge(sig(f"kt{l}_tr"), past(f"kt{l}_tr") + 1)
                else:
                    act.wait_ge(sig(f"kt{l}_tr"), past(f"kt{l}_tr") + n + 1)
                    if n >= 3:
                        act.wait_ge(sig(f"sscore{l}_mm"), past(f"sscore{l}_mm") + n - 2)
                    elif n == 2:
                        act.wait_ge(sig(f"score{l}_mm"), past(f"score{l}_mm") + LASTT)
                act.activation(dst[:, :, 0:P], pair_chunks(C_), ACT.Copy).then_inc(sig(f"kt{l}_a"), 1)

            def attention(l):
                for u in range(4):
                    for o in range(2):
                        j = 2 * u + o
                        wait_column(act, f"q{l}", f"wq{l}", u, o)
                        act.activation(qT[:, j, :].rearrange("p (b n) -> p b n", b=2), PAIR[o][:, :, 0:MOVE], ACT.Copy).then_inc(sig(f"q{l}_copied"), 1)
                key_copy(l, 0)

                def exponents(t, m):
                    act.wait_ge(sig(f"prob{l}_max"), past(f"prob{l}_max") + t + 1)
                    if t:
                        act.wait_ge(sig(f"prob{l}_tr"), past(f"prob{l}_tr") + t)
                    pair = pair_flat(t % 2)
                    for hh in range(HEADS):
                        e = act.activation(prob[0:m, hh * NMEM:(hh + 1) * NMEM], pair[0:m, hh * NMEM:(hh + 1) * NMEM], ACT.Exp,
                                           bias=smax[0:m, t, hh:hh + 1], scale=QSCALE, accum_out=ssum[0:m, t, hh:hh + 1])
                    e.then_inc(sig(f"prob{l}_exp"), 1)

                exponents(0, P)
                for t in range(LASTT):
                    act.wait_ge(sig(f"prob{l}_tr"), past(f"prob{l}_tr") + t + 1)
                    if t:
                        act.wait_ge(sig(f"att{l}_mm"), past(f"att{l}_mm") + t)
                    act.activation(probT, pair_chunks(C_), ACT.Copy).then_inc(sig(f"pt{l}_copied"), 1)
                    if t + 1 < LASTT:
                        exponents(t + 1, P)
                    if t < LASTT - 1:
                        act.wait_ge(sig(f"att{l}_mm"), past(f"att{l}_mm") + t + 1)
                    else:
                        act.wait_ge(sig("plain_used"), PLAIN[("v", l)] + 1)
                    act.activation(xhi[:, :, cols(t)], pair_chunks(D_), ACT.Copy).then_inc(sig(f"att{l}_hi"), 1)
                for b in range(NB):
                    key_copy(l, b + 1)
                exponents(LASTT, NS)
                for q in range(3):
                    make_hi((f"wo{l}", q))
                act.wait_ge(sig(f"os{l}_tr"), past(f"os{l}_tr") + 1)
                act.activation(xhi[:, :, cols(LASTT)], pair_chunks(C_)[:, :, 0:NS], ACT.Copy).then_inc(sig(f"att{l}_hi"), 1)
                make_hi((f"wo{l}", 3))

            def make_hi_moe(l, k, i):
                r, s = MOE_RAW[l] + k, MOE_SPL[l] + k
                act.wait_ge(sig(f"raw_landed{r % RING}"), LANDED[r] + 48 * i)
                act.wait_ge(sig("split_used"), s - RING + 1 + 12 * i)
                act.activation(whi[s % RING][:, :], raw[r % RING][:, :], ACT.Copy).then_inc(sig("hi_made"), 1)

            def router(l):
                act.wait_ge(sig("wr_landed"), 64 * (l + 1))
                act.activation(wrhi[:, :, :], wr_rows, ACT.Copy).then_inc(sig(f"wr{l}_hi"), 1)
                act.wait_ge(sig(f"lg{l}_mm"), past(f"lg{l}_mm") + 1)
                act.wait_ge(sig(f"lg{l}_zeroed"), past(f"lg{l}_zeroed") + 1)
                act.activation(logitT[:, 0:TOK].rearrange("p (b n) -> p b n", b=2), ps[0:ROUTE, 0:2, 0:MOVE], ACT.Identity,
                               bias=rbias[:, :]).then_inc(sig(f"lg{l}_copied"), 1)
                act.wait_ge(sig(f"group{l}_shift"), past(f"group{l}_shift") + 1)
                act.activation(picked[:, :, :], picked[:, :, :], ACT.Exp).then_inc(sig(f"group{l}_exp"), 1)
                act.wait_ge(sig(f"expert{l}_shift"), past(f"expert{l}_shift") + 1)
                act.activation(rt[:, 5, :], rt[:, 4, :], ACT.Exp).then_inc(sig(f"expert{l}_exp"), 1)
                act.wait_ge(sig(f"h_stored"), 32 * (l + 1))
                act.wait_ge(sig(f"o{l}_tr"), past(f"o{l}_tr") + TILES)
                for t in range(TILES):
                    act.activation(h[0:rows(t), t, :], h[0:rows(t), t, :], ACT.Copy, scale=ALPHA).then_inc(sig(f"scaled{l}"), 1)

            def experts(l):
                def gathered_hi(c, i):
                    n = c + 2 * i
                    act.wait_ge(sig(f"xg{l}_tr"), past(f"xg{l}_tr") + n + 1)
                    act.activation(xgT_hi, pair_chunks(C_), ACT.Copy).then_inc(sig(f"xg{l}_hi"), 1)

                def step(c, i):
                    n, k = c + 2 * i, first_unit(c)
                    if c < EXPERTS:
                        own, nxt = ahead(c)
                        for kk in own:
                            make_hi_moe(l, kk, i)
                        act.wait_ge(sig("split_used"), unit_value(MOE_SPL[l], k + 1, i))
                        if c:
                            act.wait_ge(sig(f"hid{l}"), past(f"hid{l}") + n)
                        act.activation(silu, ps[:, 0, :], ACT.Silu).then_inc(sig(f"silu{l}"), 1)
                        for kk in nxt[0:2]:
                            make_hi_moe(l, kk, i)
                        if c < EXPERTS - 1:
                            gathered_hi(c + 1, i)
                        for kk in nxt[2:]:
                            make_hi_moe(l, kk, i)
                    if c:
                        down = k + 5 if c < EXPERTS else k + 1
                        par = (c - 1) % 2
                        act.wait_ge(sig("split_used"), unit_value(MOE_SPL[l], down, i))
                        if c > 2:
                            act.wait_ge(sig(f"y{par}_stored"), 16 * (l * EXPERTS // 2 + (c - 1) // 2) + 16 * i)
                        elif l:
                            act.wait_ge(sig(f"y{par}_stored"), 16 * l * EXPERTS // 2)
                        act.activation(ye[par], pair_flat(B_), ACT.Copy).then_inc(sig(f"ye{l}"), 1)
                    if c < EXPERTS:
                        act.wait_ge(sig(f"hid{l}_tr"), past(f"hid{l}_tr") + n + 1)
                        act.activation(hidT_hi, ps[:, 6, :].rearrange("p (k n) -> p k n", k=4), ACT.Copy).then_inc(sig(f"hid{l}_hi"), 1)
                    if c:
                        act.wait_ge(sig(f"ye{l}"), past(f"ye{l}") + n)
                        e = n - 1
                        dst = y_dram[bass.ds(e * SLOTS, P), :] if not isinstance(e, int) else y_dram[e * SLOTS:e * SLOTS + P, :]
                        act.dma_start(dst, ye[par]).then_inc(sig(f"y{par}_stored"), 16)

                gathered_hi(0, 0)
                step(0, 0)
                for c in range(1, 3):
                    step(c, 0)
                with act.Fori(0, EXPERTS // 2 - 3) as i:
                    step(3, i)
                    step(4, i)
                for c in range(EXPERTS - 3, EXPERTS):
                    step(c, 0)
                step(EXPERTS, 0)

            def further(l):
                act.wait_ge(sig(f"hid{l}"), past(f"hid{l}") + EXPERTS)
                n = further_blocks(act, l)
                with act.Fori(0, FURTHER) as i:
                    with act.If(n > i):
                        act.wait_ge(again(l, "used"), 3 + 6 * i)
                        act.activation(silu, ps[:, 0, :], ACT.Silu).then_inc(again(l, "silu"), 1)
                        act.wait_ge(again(l, "used"), 7 + 6 * i)
                        act.activation(y_hi, pair_flat(B_).rearrange("p (k n) -> p k n", k=4), ACT.Copy).then_inc(again(l, "y_hi"), 1)

            def conv_small():
                for par in range(2):
                    act.wait_ge(sig(f"y{par}_stored"), 16 * EXPERTS // 2)
                act.wait_ge(sig("moe0_combined"), past("moe0_combined") + TILES)
                small = sig("small_landed1")
                act.dma_start(c_rows, a["state_conv_c"][0].rearrange("(j b) i n -> (b i) j n", j=2)).then_inc(small, 16)
                act.dma_start(d_rows, a["state_conv_d"][0].rearrange("b i n -> (b i) n")).then_inc(small, 16)
                at = 0
                for w in (a["conv_c_w"][0], a["conv_d_w"][0], a["conv_c_b"], a["ln_c_g"], a["ln_c_b"]):
                    act.dma_start(tap_rows[at:at + w.shape[0], :], w).then_inc(small, 16)
                    at += w.shape[0]

            def conv_layer():
                for g in range(G4):
                    wait_column(act, "glu", "wglu", g, 1)
                    if g >= 2:
                        act.wait_ge(sig("glu"), g - 1)
                    else:
                        act.wait_ge(sig("moe0_combined"), past("moe0_combined") + TILES)
                    act.activation(gate_tmp[g % 2].rearrange("p (b n) -> p b n", b=2), PAIR[B_][:, :, 0:MOVE], ACT.Sigmoid).then_inc(sig("glu_gate"), 1)
                    make_hi(("wcx", g))
                for g in range(G4):
                    act.wait_ge(sig("cx_mm"), g + 1)
                    if g >= 2:
                        act.wait_ge(sig("cx"), g - 1)
                    else:
                        act.wait_ge(sig("glu"), G4 - 1 + g)
                    act.activation(gate_tmp[g % 2].rearrange("p (b n) -> p b n", b=2), PAIR[A_][:, :, 0:MOVE], ACT.Copy).then_inc(sig("cx_gate"), 1)
                    make_hi(("wgb", g) if g < 2 else ("wout1", g - 2))
                for q in range(2):
                    make_hi(("wout1", 2 + q))
                act.wait_ge(sig("d_out"), 4)
                act.activation(xhi[:, G4:KC, :], cd, ACT.Copy).then_inc(sig("d_hi"), 1)
                for t in range(TILES):
                    m = rows(t)
                    act.wait_ge(sig("c_tr"), t + 1)
                    for g in range(G4):
                        e = act.activation(acc[:, g, cols(t)], ps[:, 6 + t % 2, g * P:g * P + m], ACT.Silu,
                                           scale=ccol[:, g, CROWS - 2:CROWS - 1], bias=ccol[:, g, CROWS - 1:CROWS])
                    e.then_inc(sig("c_silu"), 1)
                    act.wait_ge(sig("c_silu"), t + 1)
                    act.activation(xhi[:, 0:G4, cols(t)], acc[:, :, cols(t)], ACT.Copy).then_inc(sig("c_hi"), 1)
                for n, (m, _) in enumerate(TAIL_SOURCES):
                    act.wait_ge(sig("tails_tr"), n + 1)
                    act.activation(tails[n][0:m, :], ps[0:m, n, :], ACT.Copy).then_inc(sig("tails_copied"), 1)

            for l in range(DEPTH):
                if l:
                    conv_layer()
                out_columns(f"out{l}", [(f"wq{l}", q) for q in range(4)])
                attention(l)
                for t in range(TILES):
                    if t == LASTT - 1:
                        for k in range(3):
                            make_hi_moe(l, k, 0)
                    columns_hi(f"o{l}", t, rows(t))
                router(l)
                experts(l)
                further(l)
                if l == DEPTH - 1:
                    return
                for g in range(G4):
                    make_hi(("wglu", g))
                for t in range(TILES):
                    if t == LASTT:
                        conv_small()
                    columns_hi(f"moe{l}", t, rows(t))

        @block.vector
        def _(dve):
            link = chained(dve, "dve_chain")

            def make_lo(key):
                i, s = RAW[key], SPL[key]
                dve.wait_ge(sig("hi_made"), s + 1)
                dve.tensor_tensor(wlo[s % RING][:, :], raw[i % RING][:, :], whi[s % RING][:, :].bitcast(F32), ALU.subtract).then_inc(sig("lo_made"), 1)

            def lo_of(out, full, hi):
                return dve.tensor_tensor(out, full, hi.bitcast(F32), ALU.subtract)

            def columns_lo(tag, t, m):
                dve.wait_ge(sig(tag + "_hi"), past(tag + "_hi") + t + 1)
                lo_of(xlo[:, :, t * P:t * P + m], pair_chunks(C_ + t % 2)[:, :, 0:m], xhi[:, :, t * P:t * P + m]).then_inc(sig(tag + "_lo"), 1)

            def statistics(tag, t, m, pieces):
                for n, piece in enumerate(pieces):
                    ins = dve.bn_stats(bn[0:m, n, :], piece)
                link(ins)
                dve.bn_aggr(mv[0:m, t, :], bn[0:m, 0:len(pieces), :].rearrange("p a n -> p (a n)")).then_inc(sig(tag + "_mv"), 1)

            def normalise(tag, t, m, out, src, gain, load_key):
                dve.wait_ge(sig(tag + "_rstd"), past(tag + "_rstd") + t + 1)
                link(dve.tensor_scalar(out, src, mv[0:m, t, 0:1], rstd[0:m, t:t + 1], ALU.subtract, ALU.mult))
                if t == 0:
                    dve.wait_ge(sig("gb_landed"), GB_LOADS[load_key])
                dve.tensor_tensor(out, out, gain, ALU.mult).then_inc(sig(tag + "_gain"), 1)

            for m in range(MT):
                columns_lo("mem", m, P)
            for q in range(4):
                make_lo(("wk0", q))
            for name in ("wv0", "wk1", "wv1"):
                for q in range(4):
                    make_lo((name, q))
            for key in (("wz", 0), ("wz", 1), ("wuv", 0), ("wuv", 1)):
                make_lo(key)

            dve.wait_ge(sig("ws_tr"), 1)
            dve.tensor_copy(wsT, ps[:, 4, :].rearrange("p (g n) -> p g n", g=G4)).then_inc(sig("ws_copied"), 1)
            dve.wait_ge(sig("hist_tr"), 1)
            dve.wait_ge(sig("kv_stored0"), 16 * 4)
            dve.wait_ge(sig("kv_stored1"), 16 * 4)
            for g in range(G4):
                ins = dve.tensor_copy(zT[:, g, ZW:ZL].rearrange("p (b s) -> p b s", b=NB)[:, :, 0:HIST],
                                      ps[:, 5, g * P:g * P + NB * HIST].rearrange("p (b s) -> p b s", b=NB))
            ins.then_inc(sig("hist_copied"), 1)
            dve.memset(zT[:, :, 0:HIST], 0.0).then_inc(sig("hist_zeroed"), 1)
            for t in range(TILES):
                columns_lo("x", t, rows(t))
            make_lo(("wuv", 2))
            make_lo(("wuv", 3))

            def pool_group(g):
                cur = zT[:, g, :]
                for lev in range(g + 1):
                    d, new = 2 ** lev, zsum[lev % 2]
                    first = 2 ** (lev + 1) - 1
                    link(dve.tensor_tensor(new[:, first:ZL], cur[:, first:ZL], cur[:, first - d:ZL - d], ALU.add))
                    cur = new
                w = 2 ** (g + 1)
                z_s = zT[:, g, ZW:ZL].rearrange("p (b s) -> p b s", b=NB)[:, :, HIST:]
                s_s = cur[:, ZW:ZL].rearrange("p (b s) -> p b s", b=NB)[:, :, HIST:]
                dve.scalar_tensor_tensor(pz[:, g, w - 1:SEQ], cur[:, HIST + w - 1:ZW], 1.0 / w, zT[:, g, HIST + w - 1:ZW], ALU.mult, ALU.subtract)
                dve.scalar_tensor_tensor(pz[:, g, SEQ:TOK].rearrange("p (b s) -> p b s", b=NB), s_s, 1.0 / w, z_s, ALU.mult, ALU.subtract)
                link(dve.tensor_tensor(pz[:, g, 0:w - 1], cur[:, HIST:HIST + w - 1], inv_count[:, 0:w - 1], ALU.mult))
                dve.tensor_tensor(pz[:, g, 0:w - 1], pz[:, g, 0:w - 1], zT[:, g, HIST:HIST + w - 1], ALU.subtract).then_inc(sig("pooled"), 1)

            dve.wait_ge(sig("consts"), 9)
            link(dve.reciprocal(inv_count[:, :], inv_count[:, :]))
            for t in range(TILES + 1):
                if t < TILES:
                    m = rows(t)
                    v = uv[t % 2][0:m, 512:1024]
                    dve.wait_ge(sig("uv_gelu"), t + 1)
                    statistics("v", t, m, [v])
                    if t < LASTT:
                        if t == 0:
                            dve.wait_ge(sig("z_copied"), 4)
                        pool_group(t)
                    normalise("v", t, m, v, v, gb[0:m, 0, 0:512], "lnv")
                if t >= 1:
                    tt, m = t - 1, rows(t - 1)
                    dve.wait_ge(sig("mixed"), tt + 1)
                    dve.wait_ge(sig("small_landed0"), 16 * N_SMALL[0])
                    bias = b_rows if tt < LASTT else b_rows_s
                    for g in range(G4):
                        u = uv[tt % 2][0:m, g * P:(g + 1) * P]
                        ins = dve.scalar_tensor_tensor(u, ps[0:m, 4 + tt % 2, g * P:(g + 1) * P], bias[0:m, g:g + 1], u, ALU.add, ALU.mult)
                    ins.then_inc(sig("gated"), 1)
                    dve.wait_ge(sig("a_hi"), tt + 1)
                    lo_of(xlo[:, 0:G4, cols(tt)], ps[:, 6 + tt % 2, :].rearrange("p (g n) -> p g n", g=G4)[:, :, 0:m],
                          xhi[:, 0:G4, cols(tt)]).then_inc(sig("a_lo"), 1)
            for g in range(G4):
                dve.wait_ge(sig("b_hi"), g + 1)
                dve.scalar_tensor_tensor(xlo[:, G4 + g, 0:SEQ], ps[:, 2 * (g % 2), :], pool_scale[:, g:g + 1],
                                         xhi[:, G4 + g, 0:SEQ].bitcast(F32), ALU.mult, ALU.subtract)
                dve.scalar_tensor_tensor(xlo[:, G4 + g, SEQ:TOK], ps[:, 2 * (g % 2) + 1, 0:NS], pool_scale[:, g:g + 1],
                                         xhi[:, G4 + g, SEQ:TOK].bitcast(F32), ALU.mult, ALU.subtract).then_inc(sig("b_lo"), 1)
            for q in range(4):
                make_lo(("wout0", q))

            def residual_norm(tag, t, psum_ready):
                m = rows(t)
                psum_ready()
                hv = h[0:m, t, :]
                ins = dve.scalar_tensor_tensor(hv, hv, ALPHA, pair_flat(t % 2)[0:m, :], ALU.mult, ALU.add)
                ins.then_inc(sig(tag + "_res"), 1)
                dve.wait_ge(sig(tag + "_res"), past(tag + "_res") + t + 1)
                statistics(tag, t, m, [h[0:m, t, 0:512], h[0:m, t, 512:1024]])
                normalise(tag, t, m, hv, hv, gb[0:m, 0, :], tag)

            def out_norm(tag, name, next_lo):
                for t in range(TILES):
                    residual_norm(tag, t, lambda: wait_product(dve, tag, t, name))
                    if t >= 1:
                        if t == LASTT:
                            next_lo()
                        columns_lo(tag, t - 1, rows(t - 1))
                columns_lo(tag, LASTT, NS)

            def key_copy(l, n):
                key = ("k", l) if n == 0 else ("ks", l, n - 1)
                dst = KT[n % 2]
                dve.wait_ge(sig("plain_used"), PLAIN[key] + 1)
                if n >= 3:
                    dve.wait_ge(sig(f"sscore{l}_mm"), past(f"sscore{l}_mm") + n - 2)
                elif n == 2:
                    dve.wait_ge(sig(f"score{l}_mm"), past(f"score{l}_mm") + LASTT)
                dve.tensor_copy(dst[:, :, P:2 * P], pair_chunks(D_)).then_inc(sig(f"kt{l}_b"), 1)

            def attention(l):
                dve.wait_ge(sig(f"out{l}_row"), past(f"out{l}_row") + TILES)
                link(dve.memset(gb[:, :, :], 0.0))
                dve.wait_ge(sig(f"q{l}_copied"), past(f"q{l}_copied") + KC)
                for b in range(NB):
                    ins = dve.tensor_copy(q_only[:, :, b, b * TS:(b + 1) * TS], qT[:, :, SEQ + b * TS:SEQ + (b + 1) * TS])
                ins.then_inc(sig(f"q{l}_only"), 1)
                key_copy(l, 0)

                def maxima(t, m):
                    if t < LASTT:
                        dve.wait_ge(sig(f"score{l}_mm"), past(f"score{l}_mm") + t + 1)
                    else:
                        dve.wait_ge(sig(f"sscore{l}_mm"), past(f"sscore{l}_mm") + NB)
                    link(dve.tensor_reduce(smax[0:m, t, :], pair_flat(t % 2)[0:m, :].rearrange("p (h n) -> p h n", h=HEADS), AX, ALU.max))
                    dve.tensor_scalar(smax[0:m, t, :], smax[0:m, t, :], -QSCALE, None, ALU.mult).then_inc(sig(f"prob{l}_max"), 1)

                def normal(t, m):
                    dve.wait_ge(sig(f"prob{l}_exp"), past(f"prob{l}_exp") + t + 1)
                    link(dve.reciprocal(ssum[0:m, t, :], ssum[0:m, t, :]))
                    for hh in range(HEADS):
                        v = prob[0:m, hh * NMEM:(hh + 1) * NMEM]
                        ins = dve.tensor_scalar(v, v, ssum[0:m, t, hh:hh + 1], None, ALU.mult)
                    ins.then_inc(sig(f"prob{l}_norm"), 1)

                maxima(0, P)
                for t in range(LASTT):
                    normal(t, P)
                    if t + 1 < LASTT:
                        maxima(t + 1, P)
                    dve.wait_ge(sig(f"att{l}_hi"), past(f"att{l}_hi") + t + 1)
                    lo_of(xlo[:, :, cols(t)], pair_chunks(D_), xhi[:, :, cols(t)]).then_inc(sig(f"att{l}_lo"), 1)
                dve.wait_ge(sig(f"score{l}_mm"), past(f"score{l}_mm") + LASTT)
                dve.wait_ge(sig(f"q{l}_only"), past(f"q{l}_only") + 1)
                link(dve.memset(p_only, 0.0))
                for b in range(NB):
                    key_copy(l, b + 1)
                maxima(LASTT, NS)
                normal(LASTT, NS)
                dve.wait_ge(sig(f"prob{l}_tr"), past(f"prob{l}_tr") + LASTT + 1)
                for b in range(NB):
                    ins = dve.tensor_copy(p_only[:, :, b, b * TS:(b + 1) * TS], pair_chunks(C_)[:, :, b * TS:(b + 1) * TS])
                ins.then_inc(sig(f"prob{l}_only"), 1)
                make_lo((f"wo{l}", 0))
                dve.wait_ge(sig("plain_used"), PLAIN[("vs", l, NB - 1)] + 1)
                dve.tensor_copy(prob[0:NS, :], pair_flat(B_)[0:NS, :]).then_inc(sig(f"os{l}_copied"), 1)
                make_lo((f"wo{l}", 1))
                make_lo((f"wo{l}", 2))
                dve.wait_ge(sig(f"att{l}_hi"), past(f"att{l}_hi") + TILES)
                lo_of(xlo[:, :, cols(LASTT)], pair_chunks(C_)[:, :, 0:NS], xhi[:, :, cols(LASTT)]).then_inc(sig(f"att{l}_lo"), 1)
                make_lo((f"wo{l}", 3))

            def make_lo_moe(l, k, i):
                r, s = MOE_RAW[l] + k, MOE_SPL[l] + k
                dve.wait_ge(sig("hi_made"), s + 1 + 12 * i)
                dve.tensor_tensor(wlo[s % RING][:, :], raw[r % RING][:, :], whi[s % RING][:, :].bitcast(F32), ALU.subtract).then_inc(sig("lo_made"), 1)

            def first_of_ties(one_hot, done):
                link(dve.tensor_scalar(done, one_hot[:, :, 0:1], -1.0, 1.0, ALU.mult, ALU.add))
                for j in range(1, 4):
                    link(dve.tensor_tensor(one_hot[:, :, j:j + 1], one_hot[:, :, j:j + 1], done, ALU.mult))
                    if j < 3:
                        link(dve.tensor_tensor(done, done, one_hot[:, :, j:j + 1], ALU.subtract))

            def router(l):
                dve.wait_ge(sig(f"wr{l}_hi"), past(f"wr{l}_hi") + 1)
                lo_of(wrlo[:, :, :], wr_rows, wrhi[:, :, :]).then_inc(sig(f"wr{l}_lo"), 1)
                dve.wait_ge(sig(f"lg{l}_tr"), past(f"lg{l}_tr") + 1)
                link(dve.tensor_copy(lgt[:, :, :], ps[:, 2, 0:32 * TILES].rearrange("p (t n) -> p t n", t=TILES)[:, :, 0:ROUTE]))
                full = [P, TILES, 4]

                def per_token(n):
                    return rt[:, n, :].unsqueeze(2)

                G = lgt[:, :, 0:GROUPS]
                link(dve.tensor_reduce(rt[:, 0, :], G, AX, ALU.max))
                link(dve.tensor_tensor(picked[:, :, :], G, per_token(0).to_broadcast(full), ALU.subtract))
                link(dve.tensor_scalar(chosen[:, :, 0, :], picked[:, :, :], 0.0, None, ALU.is_equal))
                dve.tensor_copy(rt[:, 7, :], rt[:, 0, :]).then_inc(sig(f"group{l}_shift"), 1)
                dve.wait_ge(sig(f"group{l}_exp"), past(f"group{l}_exp") + 1)
                link(dve.tensor_reduce(rt[:, 1, :], picked[:, :, :], AX, ALU.add))
                link(dve.reciprocal(rt[:, 1, :], rt[:, 1, :]))
                og = chosen[:, :, 0, :]
                first_of_ties(og, per_token(6))
                by_group = both[:, 0, :, :].rearrange("p t (g k) -> p t g k", g=GROUPS)
                for g in range(GROUPS):
                    ins = dve.tensor_tensor(by_group[:, :, g, :], lgt[:, :, GROUPS + PER * g:GROUPS + PER * (g + 1)],
                                            og[:, :, g:g + 1].to_broadcast(full), ALU.mult)
                link(ins)
                link(dve.tensor_tensor(picked[:, :, :], by_group[:, :, 0, :], by_group[:, :, 1, :], ALU.add))
                link(dve.tensor_tensor(picked[:, :, :], picked[:, :, :], by_group[:, :, 2, :], ALU.add))
                link(dve.tensor_tensor(picked[:, :, :], picked[:, :, :], by_group[:, :, 3, :], ALU.add))
                link(dve.tensor_reduce(rt[:, 2, :], picked[:, :, :], AX, ALU.max))
                link(dve.tensor_tensor(chosen[:, :, 1, :], picked[:, :, :], per_token(2).to_broadcast(full), ALU.is_equal))
                first_of_ties(chosen[:, :, 1, :], per_token(6))
                link(dve.scalar_tensor_tensor(picked[:, :, :], chosen[:, :, 1, :], -3.0e38, picked[:, :, :], ALU.mult, ALU.add))
                link(dve.tensor_reduce(rt[:, 3, :], picked[:, :, :], AX, ALU.max))
                link(dve.tensor_tensor(chosen[:, :, 2, :], picked[:, :, :], per_token(3).to_broadcast(full), ALU.is_equal))
                first_of_ties(chosen[:, :, 2, :], per_token(6))
                dve.tensor_tensor(rt[:, 4, :], rt[:, 3, :], rt[:, 2, :], ALU.subtract).then_inc(sig(f"expert{l}_shift"), 1)
                link(dve.tensor_tensor(og, og, valid[:, :].unsqueeze(2).to_broadcast(full), ALU.mult))
                for j in range(2):
                    dst = both[:, j, :, :].rearrange("p t (g k) -> p t g k", g=GROUPS)
                    for g in range(GROUPS):
                        ins = dve.tensor_tensor(dst[:, :, g, :], chosen[:, :, 1 + j, :], og[:, :, g:g + 1].to_broadcast(full), ALU.mult)
                link(ins)
                dve.tensor_tensor(member[:, :, :], both[:, 0, :, :], both[:, 1, :, :], ALU.add).then_inc(sig(f"member{l}"), 1)
                dve.wait_ge(sig(f"expert{l}_exp"), past(f"expert{l}_exp") + 1)
                link(dve.tensor_scalar(rt[:, 6, :], rt[:, 5, :], 1.0, None, ALU.add))
                link(dve.reciprocal(rt[:, 6, :], rt[:, 6, :]))
                link(dve.tensor_tensor(rw[:, :, 0], rt[:, 6, :], rt[:, 1, :], ALU.mult))
                link(dve.tensor_tensor(rw[:, :, 1], rt[:, 5, :], rw[:, :, 0], ALU.mult))
                dve.wait_ge(sig(f"rank{l}_mm"), past(f"rank{l}_mm") + 1)
                dve.wait_ge(sig(f"member{l}"), past(f"member{l}") + 1)
                link(dve.tensor_copy(rank[:, :, :], ps[:, 3, 0:TILES * EXPERTS].rearrange("p (t e) -> p t e", t=TILES)))
                by_expert = [P, TILES, EXPERTS]
                link(dve.tensor_tensor(gates, both[:, 0, :, :], rw[:, :, 0:1].to_broadcast(by_expert), ALU.mult))
                link(dve.tensor_tensor(kept, both[:, 1, :, :], rw[:, :, 1:2].to_broadcast(by_expert), ALU.mult))
                link(dve.tensor_tensor(gates, gates, kept, ALU.add))
                link(dve.tensor_scalar(kept, rank[:, :, :], SLOTS - 0.5, None, ALU.is_lt))
                link(dve.tensor_tensor(slot_value, rank[:, :, :], slot0[:, :].unsqueeze(1).to_broadcast(by_expert), ALU.add))
                for j in range(2):
                    link(dve.tensor_tensor(both[:, j, :, :], both[:, j, :, :], kept, ALU.mult))
                    link(dve.tensor_reduce(rt[:, 6, :], both[:, j, :, :], AX, ALU.add))
                    link(dve.tensor_tensor(rw[:, :, j], rw[:, :, j], rt[:, 6, :], ALU.mult))
                    link(dve.tensor_tensor(both[:, j, :, :], both[:, j, :, :], slot_value, ALU.mult))
                    link(dve.tensor_reduce(slot_f[:, :, j], both[:, j, :, :], AX, ALU.add))
                dve.tensor_copy(slot_of[:, :, :], slot_f[:, :, :]).then_inc(sig(f"slots{l}"), 1)
                link(dve.scalar_tensor_tensor(rank[:, :, :], rank[:, :, :], 1.0, member[:, :, :], ALU.add, ALU.mult))
                link(dve.tensor_scalar(rank[:, :, :], rank[:, :, :], -1.0, None, ALU.add))
                dve.tensor_copy(rt[:, 7, :], rt[:, 0, :]).then_inc(sig(f"ranked{l}"), 1)

            def experts(l):
                def hits(c, i):
                    n = c + 2 * i
                    if c >= 2:
                        dve.wait_ge(sig(f"tok{l}_mm"), past(f"tok{l}_mm") + n - 1)
                    r = rank[:, :, n:n + 1] if isinstance(n, int) else rank[:, :, bass.ds(n, 1)]
                    dve.tensor_tensor(hit[c % 2], iota[:, :].unsqueeze(1).to_broadcast([P, TILES, P]), r.to_broadcast([P, TILES, P]),
                                      ALU.is_equal).then_inc(sig(f"hit{l}"), 1)

                def tokens(c, i):
                    n = c + 2 * i
                    dve.wait_ge(sig(f"tok{l}_mm"), past(f"tok{l}_mm") + n + 1)
                    if c >= 2:
                        dve.wait_ge(sig(f"gathered{c % 2}"), 16 * (l * EXPERTS // 2 + c // 2) + 16 * i)
                    with nc.allow_low_precision(reason="whole numbers below 1024"):
                        dve.tensor_reduce(tok_of[c % 2][:, :], ps[:, 7, 0:2], AX, ALU.add).then_inc(sig(f"tok{l}"), 1)

                def gathered_lo(c, i):
                    n = c + 2 * i
                    dve.wait_ge(sig(f"xg{l}_hi"), past(f"xg{l}_hi") + n + 1)
                    lo_of(xgT_lo, pair_chunks(C_), xgT_hi).then_inc(sig(f"xg{l}_lo"), 1)

                def step(c, i):
                    n, k = c + 2 * i, first_unit(c)
                    own, nxt = ahead(c)
                    if c and c < EXPERTS - 1:
                        tokens(c + 1, i)
                    make_lo_moe(l, own[0], i)
                    if c < EXPERTS - 2:
                        hits(c + 2, i)
                    for kk in own[1:] + nxt[0:2]:
                        make_lo_moe(l, kk, i)
                    dve.wait_ge(sig("split_used"), unit_value(MOE_SPL[l], k + 3, i))
                    dve.wait_ge(sig(f"silu{l}"), past(f"silu{l}") + n + 1)
                    if c:
                        dve.wait_ge(sig(f"hid{l}_tr"), past(f"hid{l}_tr") + n)
                    dve.tensor_tensor(hid, silu, ps[:, 1, :], ALU.mult).then_inc(sig(f"hid{l}"), 1)
                    if c < EXPERTS - 1:
                        gathered_lo(c + 1, i)
                    for kk in nxt[2:]:
                        make_lo_moe(l, kk, i)
                    dve.wait_ge(sig(f"hid{l}_hi"), past(f"hid{l}_hi") + n + 1)
                    lo_of(hidT_lo, ps[:, 6, :].rearrange("p (k n) -> p k n", k=4), hidT_hi).then_inc(sig(f"hid{l}_lo"), 1)

                dve.wait_ge(sig(f"ranked{l}"), past(f"ranked{l}") + 1)
                hits(0, 0)
                hits(1, 0)
                tokens(0, 0)
                tokens(1, 0)
                list_blocks(l)
                gathered_lo(0, 0)
                step(0, 0)
                for c in range(1, 3):
                    step(c, 0)
                with dve.Fori(0, EXPERTS // 2 - 3) as i:
                    step(3, i)
                    step(4, i)
                for c in range(EXPERTS - 3, EXPERTS):
                    step(c, 0)

            def list_blocks(l):
                count = ps[:, 3, TILES * EXPERTS:(TILES + 1) * EXPERTS]
                pad = EXPERTS // 2
                for r in range(LEVELS):
                    dve.tensor_scalar(level[:, r, :], count, SLOTS * (r + 1) + 0.5, None, ALU.is_gt)
                dve.memset(total[0][:, 0:pad], 0.0)
                link(dve.memset(total[1][:, 0:pad], 0.0))
                link(dve.tensor_reduce(total[0][:, pad:], level.rearrange("p r e -> p e r"), AX, ALU.add))
                link(dve.tensor_copy(level[:, 0, :], total[0][:, pad:]))
                for n in range(4):
                    src, dst, d = total[n % 2], total[(n + 1) % 2], 2 ** n
                    link(dve.tensor_tensor(dst[:, pad:], src[:, pad:], src[:, pad - d:pad + EXPERTS - d], ALU.add))
                upto = total[0][:, pad:]
                link(dve.tensor_tensor(level[:, 0, :], upto, level[:, 0, :], ALU.subtract))
                table = [P, FURTHER, EXPERTS]
                number = iota[:, 0:FURTHER].unsqueeze(2).to_broadcast(table)
                start = level[:, 0:1, :].to_broadcast(table)
                link(dve.tensor_tensor(nth, number, start, ALU.is_ge))
                link(dve.tensor_tensor(is_of, number, upto.unsqueeze(1).to_broadcast(table), ALU.is_lt))
                link(dve.tensor_tensor(is_of, is_of, nth, ALU.mult))
                link(dve.tensor_tensor(nth, number, start, ALU.subtract))
                link(dve.tensor_tensor(nth, nth, is_of, ALU.mult))
                link(dve.tensor_reduce(first_rank, nth, AX, ALU.add))
                link(dve.tensor_scalar(first_rank, first_rank, 1.0, float(SLOTS), ALU.add, ALU.mult))
                link(dve.tensor_tensor(nth, is_of, iota[:, 0:EXPERTS].unsqueeze(1).to_broadcast(table), ALU.mult))
                with nc.allow_low_precision(reason="whole numbers below 16"):
                    link(dve.tensor_reduce(block_expert[:, :], nth[0:1, :, :], AX, ALU.add))
                dve.tensor_copy(blocks[:, :], upto[0:1, EXPERTS - 1:EXPERTS]).then_inc(sig(f"listed{l}"), 1)

            def further(l):
                dve.wait_ge(sig("y0_stored"), 16 * (l + 1) * EXPERTS // 2)
                dve.wait_ge(sig("y1_stored"), 16 * (l + 1) * EXPERTS // 2)
                dve.wait_ge(sig(f"scaled{l}"), past(f"scaled{l}") + TILES)
                dve.tensor_copy(tok2_f, tok2[:, :, :]).then_inc(again(l, "added"), 1)
                n = further_blocks(dve, l)
                with dve.Fori(0, FURTHER) as i:
                    with dve.If(n > i):
                        done = [0]

                        def step(ins):
                            done[0] += 1
                            ins.then_inc(again(l, "own"), 1)
                            dve.wait_ge(again(l, "own"), done[0] + 6 * i)
                        expert = is_of[:, bass.ds(i, 1), :].to_broadcast([P, TILES, EXPERTS])
                        step(dve.tensor_tensor(own, rank[:, :, :], expert, ALU.mult))
                        step(dve.tensor_reduce(own_rank, own, AX, ALU.add))
                        step(dve.tensor_scalar(own_rank, own_rank, first_rank[:, bass.ds(i, 1)], None, ALU.subtract))
                        step(dve.tensor_tensor(own, gates, expert, ALU.mult))
                        step(dve.tensor_reduce(own_gate, own, AX, ALU.add))
                        marks = [P, TILES, P]
                        dve.tensor_tensor(hit_f, iota[:, :].unsqueeze(1).to_broadcast(marks), own_rank.unsqueeze(2).to_broadcast(marks),
                                          ALU.is_equal).then_inc(again(l, "hit"), 1)
                        dve.wait_ge(again(l, "tok_mm"), 1 + i)
                        with nc.allow_low_precision(reason="whole numbers below 1024"):
                            dve.tensor_reduce(tok_of[0][:, :], ps[:, 7, 0:2], AX, ALU.add).then_inc(again(l, "tok"), 1)
                        dve.wait_ge(again(l, "tr"), 1 + 3 * i)
                        dve.tensor_copy(hitT[:, 0:2, :], ps[:, 4, :].rearrange("p (k n) -> p k n", k=2))
                        dve.tensor_copy(hitT[:, 2, 0:P], ps[:, 5, 0:P]).then_inc(again(l, "copied"), 1)
                        dve.wait_ge(again(l, "tr"), 2 + 3 * i)
                        dve.tensor_copy(rowsT, pair_chunks(C_)).then_inc(again(l, "copied"), 1)
                        dve.wait_ge(again(l, "used"), 5 + 6 * i)
                        dve.wait_ge(again(l, "silu"), 1 + i)
                        dve.tensor_tensor(hid, silu, ps[:, 1, :], ALU.mult).then_inc(again(l, "hid"), 1)
                        dve.wait_ge(again(l, "tr"), 3 + 3 * i)
                        dve.tensor_copy(hidT, ps[:, 6, :].rearrange("p (k n) -> p k n", k=4)).then_inc(again(l, "copied"), 1)
                        dve.wait_ge(again(l, "y_hi"), 1 + i)
                        lo_of(y_lo, pair_flat(B_).rearrange("p (k n) -> p k n", k=4), y_hi).then_inc(again(l, "copied"), 1)
                        for t in range(TILES):
                            hv, m = h[0:rows(t), t, :], rows(t)
                            dve.wait_ge(again(l, "share_mm"), t + 1 + TILES * i)
                            dve.scalar_tensor_tensor(hv, pair_flat(t % 2)[0:m, :], own_gate[0:m, t:t + 1], hv, ALU.mult, ALU.add).then_inc(again(l, "added"), 1)
                        dve.wait_ge(again(l, "added"), 1 + TILES + TILES * i)
                        dve.tensor_copy(spare, own_rank[:, 0:1]).then_inc(again(l, "own"), 1)

            def combine(l, lo_keys):
                tag = f"moe{l}"
                for t in range(TILES):
                    m = rows(t)
                    hv = h[0:m, t, :]
                    dve.wait_ge(sig(f"scaled{l}"), past(f"scaled{l}") + t + 1)
                    dve.wait_ge(sig(f"back_landed{t % 2}"), 32 * (l * len(range(t % 2, TILES, 2)) + t // 2 + 1))
                    link(dve.scalar_tensor_tensor(hv, back[t % 2][0][0:m, :], rw[0:m, t, 0:1], hv, ALU.mult, ALU.add))
                    dve.scalar_tensor_tensor(hv, back[t % 2][1][0:m, :], rw[0:m, t, 1:2], hv, ALU.mult, ALU.add).then_inc(sig(tag + "_combined"), 1)
                    dve.wait_ge(sig(tag + "_combined"), past(tag + "_combined") + t + 1)
                    statistics(tag, t, m, [h[0:m, t, 0:512], h[0:m, t, 512:1024]])
                    if t < len(lo_keys):
                        make_lo(lo_keys[t])
                    normalise(tag, t, m, hv, hv, gb[0:m, 0, :], tag)
                    if l < DEPTH - 1 and t:
                        columns_lo(tag, t - 1, rows(t - 1))
                if l < DEPTH - 1:
                    columns_lo(tag, LASTT, NS)

            def conv_layer():
                dve.wait_ge(sig("hist1_tr"), 1)
                link(dve.tensor_copy(ccol[:, :, :], ps[:, 4, :].rearrange("p (g n) -> p g n", g=G4)[:, :, 0:CROWS]))
                for g in range(G4):
                    dve.tensor_copy(cxT[:, g, DW:DL].rearrange("p (b s) -> p b s", b=NB)[:, :, 0:HDD],
                                    ps[:, 5, g * P:g * P + NB * HDD].rearrange("p (b s) -> p b s", b=NB))
                    for j in range(2):
                        dve.tensor_copy(gluT[:, g, CW:CL].rearrange("p (b s) -> p b s", b=NB)[:, 4 * j:4 * j + 4, 0:HC],
                                        ps[:, 6 + j, g * P:g * P + 4 * HC].rearrange("p (b s) -> p b s", b=4))
                dve.memset(gluT[:, :, 0:HC], 0.0)
                link(dve.memset(cxT[:, :, 0:HDD], 0.0))
                dve.tensor_copy(rt[:, 7, :], rt[:, 0, :]).then_inc(sig("hist1_copied"), 1)

                def sequences(x, width, hist, start):
                    return x[:, width:].rearrange("p (b s) -> p b s", b=NB)[:, :, start:start + TS]

                def taps(first, last):
                    for j in range(first, last):
                        g, k = divmod(j, TAPS_C)
                        src = gluT[:, g, :]
                        p_in, p_out = src[:, k:k + SEQ], acc[:, g, 0:SEQ]
                        s_in, s_out = sequences(src, CW, HC, k), acc[:, g, SEQ:TOK].rearrange("p (b s) -> p b s", b=NB)
                        w = ccol[:, g, k:k + 1]
                        if k == 0:
                            bias = ccol[:, g, TAPS_C + TAPS_D:TAPS_C + TAPS_D + 1]
                            dve.tensor_scalar(p_out, p_in, w, bias, ALU.mult, ALU.add)
                            ins = dve.tensor_scalar(s_out, s_in, w, bias, ALU.mult, ALU.add)
                        else:
                            dve.scalar_tensor_tensor(p_out, p_in, w, p_out, ALU.mult, ALU.add)
                            ins = dve.scalar_tensor_tensor(s_out, s_in, w, s_out, ALU.mult, ALU.add)
                        if k == TAPS_C - 1:
                            ins.then_inc(sig("conv"), 1)
                        else:
                            link(ins)

                def to_sequences(dst, width, hist, pair, gate, name):
                    dve.tensor_tensor(dst[:, hist:hist + MOVE], ps[:, 2 * pair, 0:MOVE], gate[:, 0:MOVE], ALU.mult)
                    dve.tensor_tensor(dst[:, hist + MOVE:width], ps[:, 2 * pair + 1, 0:PB], gate[:, MOVE:MOVE + PB], ALU.mult)
                    link(dve.tensor_tensor(sequences(dst, width, hist, hist), ps[:, 2 * pair + 1, PB:MOVE].rearrange("p (b s) -> p b s", b=NB),
                                           gate[:, MOVE + PB:].rearrange("p (b s) -> p b s", b=NB), ALU.mult))
                    dve.tensor_copy(rt[:, 7, :], rt[:, 0, :]).then_inc(sig(name), 1)

                def short_conv(g):
                    for k in range(TAPS_D):
                        src = cxT[:, g, :]
                        p_in, p_out = src[:, k:k + SEQ], cd[:, g, 0:SEQ]
                        s_in, s_out = sequences(src, DW, HDD, k), cd[:, g, SEQ:TOK].rearrange("p (b s) -> p b s", b=NB)
                        w = ccol[:, g, TAPS_C + k:TAPS_C + k + 1]
                        if k == 0:
                            dve.tensor_scalar(p_out, p_in, w, None, ALU.mult)
                            link(dve.tensor_scalar(s_out, s_in, w, None, ALU.mult))
                        else:
                            dve.scalar_tensor_tensor(p_out, p_in, w, p_out, ALU.mult, ALU.add)
                            link(dve.scalar_tensor_tensor(s_out, s_in, w, s_out, ALU.mult, ALU.add))

                done, per_step = 0, 12
                for g in range(G4):
                    dve.wait_ge(sig("glu_gate"), g + 1)
                    dve.wait_ge(sig("glu_mm"), g + 1)
                    to_sequences(gluT[:, g, :], CW, HC, A_, gate_tmp[g % 2], "glu")
                    make_lo(("wcx", g))
                    taps(done, done + per_step)
                    done += per_step
                for g in range(G4):
                    dve.wait_ge(sig("cx_gate"), g + 1)
                    wait_column(dve, "cx", "wcx", g, 1)
                    to_sequences(cxT[:, g, :], DW, HDD, B_, gate_tmp[g % 2], "cx")
                    make_lo(("wgb", g) if g < 2 else ("wout1", g - 2))
                    short_conv(g)
                    taps(done, done + per_step - 2)
                    done += per_step - 2
                for u in range(2):
                    for o in range(2):
                        j = 2 * u + o
                        wait_column(dve, "gb", "wgb", u, o)
                        v = cd[:, j, :].rearrange("p (b n) -> p b n", b=2)
                        dve.tensor_tensor(v, v, PAIR[o][:, :, 0:MOVE], ALU.mult).then_inc(sig("d_out"), 1)
                    make_lo(("wout1", 2 + u))
                    if u == 0:
                        taps(done, done + 16)
                        done += 16
                taps(done, G4 * TAPS_C)
                dve.wait_ge(sig("d_hi"), 1)
                lo_of(xlo[:, G4:KC, :], cd, xhi[:, G4:KC, :]).then_inc(sig("d_lo"), 1)
                for t in range(TILES + 1):
                    if t < TILES:
                        m = rows(t)
                        dve.wait_ge(sig("c_rows"), t + 1)
                        statistics("c", t, m, [ps[0:m, 4 + t % 2, :]])
                    if t >= 1:
                        tt, m = t - 1, rows(t - 1)
                        dve.wait_ge(sig("c_hi"), tt + 1)
                        lo_of(xlo[:, 0:G4, cols(tt)], acc[:, :, cols(tt)], xhi[:, 0:G4, cols(tt)]).then_inc(sig("c_lo"), 1)
                    if t < TILES:
                        m = rows(t)
                        if t >= 2:
                            dve.wait_ge(sig("c_tr"), t - 1)
                        dve.wait_ge(sig("c_rstd"), past("c_rstd") + t + 1)
                        dve.tensor_scalar(ln_rows[t % 2][0:m, :], ps[0:m, 4 + t % 2, :], mv[0:m, t, 0:1], rstd[0:m, t:t + 1],
                                          ALU.subtract, ALU.mult).then_inc(sig("c_norm"), 1)

            for l in range(DEPTH):
                if l:
                    conv_layer()
                out_norm(f"out{l}", f"wout{l}", lambda: [make_lo((f"wq{l}", q)) for q in range(4)])
                attention(l)
                out_norm(f"o{l}", f"wo{l}", lambda: [make_lo_moe(l, k, 0) for k in range(3)])
                router(l)
                experts(l)
                further(l)
                combine(l, [("wglu", g) for g in range(G4)] if l < DEPTH - 1 else [])

        @block.gpsimd
        def _(pool):
            link = chained(pool, "pool_chain")
            consts = sig("consts")
            link(pool.memset(ident[:, :], 0.0))
            pool.affine_select(out=ident[:, :], in_=ident[:, :], compare_op=ALU.not_equal, fill=1.0, base=0,
                               pattern=[[-1, P]], channel_multiplier=1).then_inc(consts, 1)
            link(pool.memset(before[:, :], 1.0))
            pool.affine_select(out=before[:, :], in_=before[:, :], compare_op=ALU.is_gt, fill=0.0, base=0,
                               pattern=[[1, P]], channel_multiplier=-1).then_inc(consts, 1)
            pool.memset(ones[:, :], 1.0).then_inc(consts, 1)
            pool.iota(iota[:, :], pattern=[[1, P]], base=0, channel_multiplier=0, allow_small_or_imprecise_dtypes=True).then_inc(consts, 1)
            pool.iota(tok2[:, :, 0], pattern=[[P, TILES]], base=0, channel_multiplier=0, allow_small_or_imprecise_dtypes=True)
            pool.iota(tok2[:, :, 1], pattern=[[0, TILES]], base=0, channel_multiplier=1, allow_small_or_imprecise_dtypes=True).then_inc(consts, 1)
            pool.iota(slot0[:, :], pattern=[[SLOTS, EXPERTS]], base=0, channel_multiplier=0, allow_small_or_imprecise_dtypes=True).then_inc(consts, 1)
            pool.iota(inv_count[:, :], pattern=[[1, HIST + 1]], base=1, channel_multiplier=0, allow_small_or_imprecise_dtypes=True).then_inc(consts, 1)
            pool.memset(minus_half[:, :], -0.5).then_inc(consts, 1)
            link(pool.memset(valid[:, :], 1.0))
            pool.affine_select(out=valid[:, LASTT:TILES], in_=valid[:, LASTT:TILES], compare_op=ALU.is_ge, fill=0.0, base=NS - 1,
                               pattern=[[0, 1]], channel_multiplier=-1).then_inc(consts, 1)

            def load_gb(g, b):
                n = g.shape[0]
                pool.dma_start(gb[:, 0, 0:n], g.partition_broadcast(P)).then_inc(sig("gb_landed"), 16)
                pool.dma_start(gb[:, 1, 0:n], b.partition_broadcast(P)).then_inc(sig("gb_landed"), 16)

            def reciprocal_deviation(tag, t, m):
                pool.wait_ge(sig(tag + "_mv"), past(tag + "_mv") + t + 1)
                link(pool.tensor_scalar(ve[0:m, t:t + 1], mv[0:m, t, 1:2], EPS, None, ALU.add))
                pool.tensor_tensor(rstd[0:m, t:t + 1], ve[0:m, t:t + 1], minus_half[0:m, :], ALU.pow).then_inc(sig(tag + "_rstd"), 1)

            def add_bias(tag, t, m, out, bias):
                pool.wait_ge(sig(tag + "_gain"), past(tag + "_gain") + t + 1)
                pool.tensor_tensor(out, out, bias, ALU.add).then_inc(sig(tag + "_row"), 1)

            load_gb(a["ln_v_g"][0], a["ln_v_b"][0])
            n = 0
            for l in range(DEPTH):
                for out in (o_memk, o_memv):
                    for m in range(MT):
                        pool.wait_ge(sig("kv_copied"), n + 1)
                        pool.dma_start(out[l, 0, m * P:(m + 1) * P].rearrange("m h c -> m (h c)"), kv_rows[n % 2]).then_inc(sig(f"kv_stored{n % 2}"), 16)
                        n += 1

            pool.wait_ge(sig("ws_copied"), 1)
            pool.affine_select(out=wsT, in_=wsT, compare_op=ALU.is_ge, fill=0.0, base=0,
                               pattern=[[0, G4], [1, P]], channel_multiplier=-1).then_inc(sig("ws_masked"), 1)
            link(pool.memset(wsS, 0.0))
            pool.wait_ge(sig("ws_masked"), 1)
            for b in range(NB):
                pool.dma_start(wsS[b * TS:(b + 1) * TS, :, b * TS:(b + 1) * TS], wsT[0:TS, :, 0:TS]).then_inc(sig("wss_landed"), 16)
            for t in range(TILES):
                m = rows(t)
                v = uv[t % 2][0:m, 512:1024]
                reciprocal_deviation("v", t, m)
                if t == 0:
                    pool.wait_ge(sig("gb_landed"), GB_LOADS["lnv"])
                add_bias("v", t, m, v, gb[0:m, 1, 0:512])
            pool.wait_ge(sig("v_row"), past("v_row") + TILES)
            pool.dma_start(o_chunk[0].rearrange("b t n -> (b t) n"), uv[LASTT % 2][0:NS, 512:1024]).then_inc(sig("stored"), 16)
            load_gb(a["ln_g"][0, 0], a["ln_b"][0, 0])
            for g in range(G4):
                ins = pool.tensor_copy(flat[:, 0, g, :].rearrange("p (b s) -> p b s", b=NB), zT[:, g, ZW:ZL].rearrange("p (b s) -> p b s", b=NB)[:, :, HIST:])
            ins.then_inc(sig("z_flat"), 1)
            pool.dma_start(o_pool_s[0][:, 0:HIST - TS, :], a["state_pool"][0][:, TS:HIST, :]).then_inc(sig("stored"), 16)
            pool.wait_ge(sig("z_back_copied"), 2)
            pool.dma_start(o_pool_p[0, 0], z_tail).then_inc(sig("stored"), 16)
            for b in range(NB):
                pool.dma_start(o_pool_s[0, b, HIST - TS:HIST, :], z_new[b * TS:(b + 1) * TS, :]).then_inc(sig("stored"), 16)
            pool.wait_ge(sig("stored"), 16 * (3 + NB))

            def norm_tiles(tag):
                for t in range(TILES):
                    m = rows(t)
                    reciprocal_deviation(tag, t, m)
                    if t == 0:
                        pool.wait_ge(sig("gb_landed"), GB_LOADS[tag])
                    add_bias(tag, t, m, h[0:m, t, :], gb[0:m, 1, :])

            def next_gb(tag, l, which, after):
                for name, value in after:
                    pool.wait_ge(sig(name), past(name) + value)
                load_gb(a["ln_g"][l, which], a["ln_b"][l, which])

            def experts(l):
                def gather(c, i):
                    n = c + 2 * i
                    pool.wait_ge(sig(f"tok{l}"), past(f"tok{l}") + n + 1)
                    if c >= 2:
                        pool.wait_ge(sig(f"xg{l}_tr"), past(f"xg{l}_tr") + n - 1)
                    if l or c:
                        pool.wait_ge(sig("marked"), l * EXPERTS + n)
                    pool.tensor_tensor(wait_mark[:, 0:1], minus_half[0:1, :], minus_half[0:1, :], ALU.add).then_inc(sig("marked"), 1)
                    pool.indirect_dma_start(xg[c % 2], None, h_dram, bass.IndirectOffsetOnAxis(tok_of[c % 2][:, 0:1], 0)).then_inc(sig(f"gathered{c % 2}"), 16)

                def step(c, i):
                    if c < EXPERTS - 1:
                        gather(c + 1, i)

                pool.wait_ge(sig("h_stored"), 32 * (l + 1))
                gather(0, 0)
                gather(1, 0)
                for c in range(1, 3):
                    step(c, 0)
                with pool.Fori(0, EXPERTS // 2 - 3) as i:
                    step(3, i)
                    step(4, i)
                for c in range(EXPERTS - 3, EXPERTS - 1):
                    step(c, 0)

            def further(l):
                pool.wait_ge(sig(f"xg{l}_tr"), past(f"xg{l}_tr") + EXPERTS)
                pool.tensor_tensor(wait_mark[:, 1 + l:2 + l], minus_half[0:1, :], minus_half[0:1, :], ALU.add).then_inc(again(l, "marked"), 1)
                n = further_blocks(pool, l)
                with pool.Fori(0, FURTHER) as i:
                    with pool.If(n > i):
                        pool.wait_ge(again(l, "tok"), 1 + i)
                        pool.wait_ge(again(l, "marked"), 1 + i)
                        pool.tensor_tensor(wait_mark[:, 1 + l:2 + l], minus_half[0:1, :], minus_half[0:1, :], ALU.add).then_inc(again(l, "marked"), 1)
                        pool.indirect_dma_start(xg[0], None, h_dram, bass.IndirectOffsetOnAxis(tok_of[0][:, 0:1], 0)).then_inc(again(l, "gathered"), 16)
                        pool.wait_ge(again(l, "used"), 7 + 6 * i)

            def combine(l):
                tag = f"moe{l}"
                pool.wait_ge(sig(f"slots{l}"), past(f"slots{l}") + 1)
                for par in range(2):
                    pool.wait_ge(sig(f"y{par}_stored"), 16 * (l + 1) * EXPERTS // 2)

                def fetch(t):
                    m = rows(t)
                    if t >= 2:
                        pool.wait_ge(sig(tag + "_combined"), past(tag + "_combined") + t - 1)
                    for j in range(2):
                        pool.indirect_dma_start(back[t % 2][j][0:m, :], None, y_dram, bass.IndirectOffsetOnAxis(slot_of[0:m, t, j:j + 1], 0)).then_inc(sig(f"back_landed{t % 2}"), 16)
                fetch(0)
                fetch(1)
                for t in range(TILES):
                    m = rows(t)
                    reciprocal_deviation(tag, t, m)
                    if t == 0:
                        pool.wait_ge(sig("gb_landed"), GB_LOADS[tag])
                    if t + 2 < TILES:
                        fetch(t + 2)
                    add_bias(tag, t, m, h[0:m, t, :], gb[0:m, 1, :])

            def conv_layer():
                for t in range(TILES):
                    if t == 0:
                        pool.wait_ge(sig("cx"), G4)
                        for g in range(G4):
                            ins = pool.tensor_copy(flat[:, 0, g, :].rearrange("p (b s) -> p b s", b=NB), gluT[:, g, CW:CL].rearrange("p (b s) -> p b s", b=NB)[:, :, HC:])
                        ins.then_inc(sig("flat_ready"), 1)
                        for g in range(G4):
                            ins = pool.tensor_copy(flat[:, 1, g, 0:NB * HDD].rearrange("p (b s) -> p b s", b=NB), cxT[:, g, DW:DL].rearrange("p (b s) -> p b s", b=NB)[:, :, DSW - HDD:])
                        ins.then_inc(sig("flat_ready"), 1)
                    reciprocal_deviation("c", t, rows(t))
                pool.dma_start(o_cc_s[0][:, 0:HC - TS, :], a["state_conv_c"][0][:, TS:HC, :]).then_inc(sig("stored"), 16)
                pool.wait_ge(sig("tails_copied"), 4)
                pool.dma_start(o_cc_p[0, 0], tails[0][0:HC, :]).then_inc(sig("stored"), 16)
                pool.dma_start(o_cd_p[0, 0], tails[2][0:HDD, :]).then_inc(sig("stored"), 16)
                pool.dma_start(o_cd_s[0].rearrange("b i n -> (b i) n"), tails[3][0:NB * HDD, :]).then_inc(sig("stored"), 16)
                for b in range(NB):
                    pool.dma_start(o_cc_s[0, b, HC - TS:HC, :], tails[1][b * TS:(b + 1) * TS, :]).then_inc(sig("stored"), 16)

            stores = 3 + NB
            for l in range(DEPTH):
                if l:
                    conv_layer()
                    stores += 4 + NB
                    next_gb("out1", 1, 0, [("stored", 16 * stores)])
                norm_tiles(f"out{l}")
                if l:
                    pool.wait_ge(sig("lg0_copied"), past("lg0_copied") + 1)
                pool.dma_start(wr_rows[:, :, 0:GROUPS], a["w_group"][l].rearrange("(k p) n -> p k n", p=P)).then_inc(sig("wr_landed"), 16)
                pool.dma_start(wr_rows[:, :, GROUPS:ROUTE], a["w_router"][l].rearrange("(k p) n -> p k n", p=P)).then_inc(sig("wr_landed"), 16)
                with nc.allow_non_contiguous_dma(reason="20 words"):
                    pool.dma_start(rbias[0:GROUPS, :], a["b_group"][l].rearrange("(g o) -> g o", o=1)).then_inc(sig("wr_landed"), 16)
                    pool.dma_start(rbias[GROUPS:ROUTE, :], a["b_router"][l].rearrange("(g o) -> g o", o=1)).then_inc(sig("wr_landed"), 16)
                next_gb(f"o{l}", l, 1, [(f"sscore{l}_mm", NB)])
                norm_tiles(f"o{l}")
                pool.wait_ge(sig(f"o{l}_row"), past(f"o{l}_row") + TILES)
                pool.dma_start(h_dram[0:SEQ, :].rearrange("(t p) n -> p t n", p=P), h[:, 0:LASTT, :]).then_inc(sig("h_stored"), 16)
                pool.dma_start(h_dram[SEQ:TOK, :], h[0:NS, LASTT, :]).then_inc(sig("h_stored"), 16)
                next_gb(f"moe{l}", l, 2, [])
                pool.wait_ge(sig(f"o{l}_lo"), past(f"o{l}_lo") + TILES)
                pool.memset(logitT[:, TOK:TILES * P], 0.0).then_inc(sig(f"lg{l}_zeroed"), 1)
                experts(l)
                further(l)
                combine(l)
            pool.wait_ge(sig("moe1_row"), past("moe1_row") + TILES)
            pool.dma_start(y_prompt[0].rearrange("(t p) n -> p t n", p=P), h[:, 0:LASTT, :]).then_inc(sig("stored"), 16)
            pool.dma_start(y_sample.rearrange("b t n -> (b t) n"), h[0:NS, LASTT, :]).then_inc(sig("stored"), 16)
            pool.wait_ge(sig("stored"), 16 * (stores + 2))
            for par in range(2):
                pool.wait_ge(sig(f"kv_stored{par}"), 16 * 4)


_INS = ["x_prompt", "x_sample", "cache_mem_k", "cache_mem_v", "state_pool", "state_conv_c", "state_conv_d", "mem_prompt",
        "w_in_ab", "ln_v_g", "ln_v_b", "w_spatial", "b_spatial", "w_pool", "pool_scale", "w_out_ab", "w_in_cd", "conv_c_w",
        "conv_c_b", "ln_c_g", "ln_c_b", "conv_d_w", "w_out_cd", "w_q", "w_k", "w_v", "w_o", "w_group", "b_group",
        "w_router", "b_router", "w_gate", "w_up", "w_down", "ln_g", "ln_b"]


def _out_shapes(x):
    depth, batch, n_mem = x["w_q"].shape[0], x["x_prompt"].shape[0], x["mem_prompt"].shape[1]
    heads, head_dim = x["cache_mem_k"].shape[3:]
    db, ts = x["x_sample"].shape[:2]
    ne, no = x["state_pool"].shape[0], x["state_conv_c"].shape[0]
    half = x["state_pool"].shape[3]
    return [x["x_prompt"].shape, x["x_sample"].shape, (depth, batch, n_mem, heads, head_dim), (depth, batch, n_mem, heads, head_dim),
            (ne, batch) + x["state_pool"].shape[2:], (no, batch) + x["state_conv_c"].shape[2:], (no, batch) + x["state_conv_d"].shape[2:],
            (ne, db, ts, half), x["state_pool"].shape, x["state_conv_c"].shape, x["state_conv_d"].shape]


def kernel(**inputs):
    import numpy as _np
    import concourse.bacc as _bacc
    from concourse import mybir as _mybir
    from concourse.bass_utils import run_bass_kernel_spmd as _run

    nc = _bacc.Bacc("TRN2", target_bir_lowering=False, num_devices=1)
    arrays, ins, outs = {}, {}, []
    for name in _INS:
        x = _np.ascontiguousarray(inputs[name])
        arrays[f"in_{name}_dram"] = x
        ins[name] = nc.dram_tensor(f"in_{name}_dram", x.shape, _mybir.dt.from_np(x.dtype), kind="ExternalInput").ap()
    shapes = _out_shapes(arrays and {n: arrays[f"in_{n}_dram"] for n in _INS})
    for i, shape in enumerate(shapes):
        outs.append(nc.dram_tensor(f"out_{i}_dram", tuple(shape), _mybir.dt.float32, kind="ExternalOutput").ap())
    trunk_kernel(nc, ins, outs)
    r = _run(nc, [arrays], core_ids=[0])
    return tuple(r.results[0][f"out_{i}_dram"] for i in range(len(shapes)))
```

```python
from contextlib import ExitStack

import concourse.bass as bass
from concourse import mybir

ALU = mybir.AluOpType
ACT = mybir.ActivationFunctionType
AX = mybir.AxisListType.X
F32 = mybir.dt.float32
F32R = mybir.dt.float32r
BF16 = mybir.dt.bfloat16
U32 = mybir.dt.uint32
I32 = mybir.dt.int32

P = 128


def trunk_kernel(nc, a, outs):
    D = a["x_prompt"].shape[2]
    SEQ = a["x_prompt"].shape[1]
    NB, TS = a["x_sample"].shape[0], a["x_sample"].shape[1]
    DEPTH = a["w_q"].shape[0]
    NMEM = a["mem_prompt"].shape[1]
    HEADS, HD = a["cache_mem_k"].shape[3], a["cache_mem_k"].shape[4]
    EXPERTS, FF = a["w_gate"].shape[1], a["w_gate"].shape[3]
    GROUPS = a["w_group"].shape[2]
    PER = EXPERTS // GROUPS
    HIST = a["state_pool"].shape[2]
    HALF = D // 2
    TAPS_C, TAPS_D = a["conv_c_w"].shape[1], a["conv_d_w"].shape[1]
    HC, HDD = TAPS_C - 1, TAPS_D - 1
    KC = D // P
    G4 = HALF // P
    NS = NB * TS
    TOK = SEQ + NS
    TILES = SEQ // P + 1
    LASTT = TILES - 1
    MT = NMEM // P
    MOVE = TOK // 2
    PB = MOVE - NS
    ALPHA = (2 * DEPTH) ** 0.25
    EPS = 1e-5
    QSCALE = HD ** -0.5
    SLOTS = P
    LEVELS = -(-TOK // SLOTS) - 1
    FURTHER = 2 * TOK // SLOTS
    POOL_TAPS = 9
    RING = 4
    UW = 2048
    ROUTE = GROUPS + EXPERTS
    assert (D, SEQ, NS, NMEM, FF, DEPTH, EXPERTS, HIST) == (1024, 512, 32, 256, 512, 2, 16, 15)

    (y_prompt, y_sample, o_memk, o_memv, o_pool_p, o_cc_p, o_cd_p, o_chunk, o_pool_s, o_cc_s, o_cd_s) = outs

    def rows(t):
        return P if t < LASTT else NS

    def cols(t):
        return slice(t * P, t * P + rows(t))

    UNITS, RAW, SPL, PLAIN = [], {}, {}, {}
    MOE_RAW, MOE_SPL = {}, {}
    count = {"raw": 0, "spl": 0, "plain": 0}

    LANDED = []
    landed_now = [0] * RING

    def lands(pieces):
        slot = len(LANDED) % RING
        landed_now[slot] += 16 * pieces
        LANDED.append(landed_now[slot])

    def plan(key, dst_split, src, wait_kv=False, pieces=1):
        RAW[key] = count["raw"]
        count["raw"] += 1
        lands(pieces)
        kind = "spl" if dst_split else "plain"
        (SPL if dst_split else PLAIN)[key] = count[kind]
        count[kind] += 1
        UNITS.append(("unit", key, src, wait_kv))

    def plan_rows(name, w, quarters=range(4)):
        for q in quarters:
            plan((name, q), True, (lambda q: lambda s: [(s.rearrange("p (k n) -> p k n", k=2),
                 w[256 * q:256 * q + 256, :].rearrange("(k p) n -> p k n", p=P))])(q))

    def plan_cols(name, u, w, c0, c1):
        def src(s):
            v = s.rearrange("p (k n) -> p k n", k=KC)
            wv = w.rearrange("(k p) n -> p k n", p=P)
            if c1 == c0 + P:
                return [(v, wv[:, :, c0:c0 + 2 * P])]
            return [(v[:, :, 0:P], wv[:, :, c0:c0 + P]), (v[:, :, P:2 * P], wv[:, :, c1:c1 + P])]
        plan((name, u), True, src, pieces=1 if c1 == c0 + P else 2)

    def plan_memory(name, src_ap, wait_kv=False):
        plan(name, False, lambda s: [(s.rearrange("p (m n) -> p m n", m=MT),
             src_ap.rearrange("(m p) n -> p m n", p=P))], wait_kv)

    for l in range(DEPTH):
        plan_rows(f"wk{l}", a["w_k"][l])
        plan_rows(f"wv{l}", a["w_v"][l])
    for l in range(DEPTH):
        if l == 0:
            w = a["w_in_ab"][0]
            for u in range(2):
                plan_cols("wz", u, w, D + 256 * u, D + 256 * u + P)
            plan_rows("wuv", w[:, 0:D])
            plan_rows("wout0", a["w_out_ab"][0])
        else:
            w = a["w_in_cd"][0]
            for g in range(G4):
                plan_cols("wglu", g, w, g * P, HALF + g * P)
            for g in range(G4):
                plan_cols("wcx", g, w, 3 * HALF + g * P, 4 * HALF + g * P)
            for u in range(2):
                plan_cols("wgb", u, w, 2 * HALF + 256 * u, 2 * HALF + 256 * u + P)
            plan_rows("wout1", a["w_out_cd"][0])
        for u in range(4):
            plan_cols(f"wq{l}", u, a["w_q"][l], 256 * u, 256 * u + P)
        plan_memory(("k", l), o_memk[l, 0].rearrange("m h c -> m (h c)"), True)
        plan_memory(("v", l), o_memv[l, 0].rearrange("m h c -> m (h c)"), True)
        for b in range(NB):
            plan_memory(("ks", l, b), a["cache_mem_k"][l, b].rearrange("m h c -> m (h c)"))
            if b >= 4:
                plan_rows(f"wo{l}", a["w_o"][l], [b - 4])
        for b in range(NB):
            plan_memory(("vs", l, b), a["cache_mem_v"][l, b].rearrange("m h c -> m (h c)"))
        MOE_RAW[l], MOE_SPL[l] = count["raw"], count["spl"]
        UNITS.append(("moe", l))
        count["raw"] += 6 * EXPERTS
        count["spl"] += 6 * EXPERTS
        for _ in range(6 * EXPERTS):
            lands(1)
    ring_release = []
    for u in UNITS:
        if u[0] == "unit":
            key = u[1]
            ring_release.append(("spl", SPL[key] + 1) if key in SPL else ("plain", PLAIN[key] + 1))
        else:
            ring_release += [("spl", MOE_SPL[u[1]] + j + 1) for j in range(6 * EXPERTS)]

    SHARED = {}

    def share(semaphore, stages):
        at = 0
        for name, n in stages:
            SHARED[name] = (semaphore, at)
            at += n

    LAYERED = dict(q_mm=KC // 2, q_copied=KC, kt_tr=NB + 1, kt_a=NB + 1, kt_b=NB + 1, score_mm=LASTT, prob_max=TILES,
                   prob_exp=TILES, prob_norm=TILES, prob_tr=TILES, pt_copied=LASTT, att_mm=LASTT - 1, att_hi=TILES,
                   att_lo=TILES, sscore_mm=NB, os_copied=1, os_tr=1, wr_hi=1, wr_lo=1, 
                   lg_copied=1, lg_zeroed=1, 
                   scaled=TILES, moe_combined=TILES, out_mm=LASTT, o_mm=LASTT)
    LAYERED.update({name: EXPERTS for name in ("hit", "tok_mm", "tok", "xg_tr", "xg_hi", "xg_lo", "hid", "hid_tr", "hid_hi",
                                               "hid_lo", "ye", "silu")})
    for name, n in LAYERED.items():
        stem, _, rest = name.partition("_")
        share(name, [(f"{stem}{l}_{rest}" if rest else f"{stem}{l}", n) for l in range(DEPTH)])
    for name, parts in (("routing_mm", ("lg{}_mm", "lg{}_tr", "rank{}_mm")), ("routed", ("member{}", "ranked{}", "slots{}", "listed{}")),
                        ("shifted", ("group{}_shift", "expert{}_shift")), ("exponential", ("group{}_exp", "expert{}_exp")),
                        ("only", ("q{}_only", "prob{}_only"))):
        share(name, [(part.format(l), 1) for l in range(DEPTH) for part in parts])
    for event in ("tr", "hi", "lo"):
        share("columns_" + event, [(f"mem_{event}", MT)] + [(f"{stage}_{event}", TILES)
                                                             for stage in ("x", "out0", "o0", "moe0", "out1", "o1")])
    for event in ("mv", "rstd"):
        share("norm_" + event, [(f"{stage}_{event}", TILES) for stage in ("v", "out0", "o0", "moe0", "c", "out1", "o1", "moe1")])
    for event in ("gain", "row"):
        share("norm_" + event, [(f"{stage}_{event}", TILES) for stage in ("v", "out0", "o0", "moe0", "out1", "o1", "moe1")])
    share("history", [(name, 1) for name in ("ws_copied", "hist_copied", "hist_zeroed", "hist1_copied")])
    share("norm_res", [(f"{stage}_res", TILES) for stage in ("out0", "o0", "out1", "o1")])

    with ExitStack() as ctx:
        def sb(name, shape, dt=F32):
            return ctx.enter_context(nc.sbuf_tensor(name, shape, dt))

        SIGS = {}

        def sig(name):
            name = SHARED.get(name, (name, 0))[0]
            if name not in SIGS:
                SIGS[name] = ctx.enter_context(nc.semaphore("s_" + name))
            return SIGS[name]

        def past(name):
            return SHARED.get(name, (name, 0))[1]

        raw = [sb(f"raw{i}", [P, UW]) for i in range(RING)]
        whi = [sb(f"whi{i}", [P, UW], F32R) for i in range(RING)]
        wlo = [sb(f"wlo{i}", [P, UW], F32R) for i in range(RING)]
        h = sb("h", [P, TILES, D])
        xhi = sb("xhi", [P, KC, TOK], F32R)
        xlo = sb("xlo", [P, KC, TOK], F32R)
        gb = sb("gb", [P, 2, D])
        ARENA = 11008
        arena = sb("arena", [P, ARENA])
        ident = sb("ident", [P, P])
        iota = sb("iota", [P, P])
        before = sb("before", [P, P], BF16)
        ones = sb("ones", [P, P], BF16)
        tok2 = sb("tok2", [P, TILES, 2], BF16)
        valid = sb("valid", [P, TILES])
        minus_half = sb("minus_half", [P, 1])
        falling = sb("falling", [P, 4])
        slot0 = sb("slot0", [P, EXPERTS])
        inv_count = sb("inv_count", [P, HIST + 1])
        b_rows = sb("b_rows", [P, G4])
        b_rows_s = sb("b_rows_s", [NS, G4])
        pool_scale = sb("pool_scale", [P, G4])
        CROWS = TAPS_C + TAPS_D + 3
        ccol = sb("ccol", [P, G4, CROWS])
        bn = sb("bn", [P, 2, 6])
        mv = sb("mv", [P, TILES, 2])
        ve = sb("ve", [P, TILES])
        rstd = sb("rstd", [P, TILES])
        flat = sb("flat", [P, 2, G4, NS])
        smax = sb("smax", [P, TILES, HEADS])
        ssum = sb("ssum", [P, TILES, HEADS])
        wrhi = sb("wrhi", [P, KC, ROUTE], F32R)
        wrlo = sb("wrlo", [P, KC, ROUTE], F32R)
        rbias = sb("rbias", [ROUTE, 1])
        lgt = sb("lgt", [P, TILES, ROUTE])
        chosen = sb("chosen", [P, TILES, 3, 4])
        picked = sb("picked", [P, TILES, 4])
        rt = sb("rt", [P, 8, TILES])
        rw = sb("rw", [P, TILES, 2])
        member = sb("member", [P, TILES, EXPERTS], BF16)
        rank = sb("rank", [P, TILES, EXPERTS])
        wait_mark = sb("wait_mark", [1, 3])
        blocks = sb("blocks", [1, 1], I32)
        block_expert = sb("block_expert", [1, FURTHER], I32)
        slot_f = sb("slot_f", [P, TILES, 2])
        slot_of = sb("slot_of", [P, TILES, 2], U32)
        tok_of = [sb(f"tok_of{i}", [P, 1], U32) for i in range(2)]
        ps = ctx.enter_context(nc.psum_tensor("ps", [P, 8, 512], F32))

        h_dram = nc.dram_tensor("h_rows", [TOK, D], F32, kind="Internal").ap()
        y_dram = nc.dram_tensor("expert_rows", [EXPERTS * SLOTS, D], F32, kind="Internal").ap()

        def area(at, n, pattern=None, p=P, **kw):
            v = arena[0:p, at:at + n]
            return v.rearrange(pattern, **kw) if pattern else v

        mem_rows = area(0, 2048, "p (m n) -> p m n", m=MT)
        kv_rows = [area(4074 + 1024 * i, 1024) for i in range(2)]
        ZW, SW = HIST + SEQ, HIST + TS
        ZL = ZW + NB * SW
        zT = area(0, G4 * ZL, "p (g n) -> p g n", g=G4)
        zsum = [area(2716 + ZL * i, ZL) for i in range(2)]
        pz = area(4074, G4 * TOK, "p (g n) -> p g n", g=G4)
        wp = area(6250, 512, "p (g n) -> p g n", g=G4)
        wsT = area(6762, 512, "p (g n) -> p g n", g=G4)
        wsS = area(7274, 128, "p (g n) -> p g n", NS, g=G4)
        pool_rows = area(7402, 512, p=NB * HIST)
        z_tail = area(7914, 512, p=HIST)
        z_new = area(8426, 512, p=NS)
        uv = [area(8938 + 1024 * i, 1024) for i in range(2)]
        ws_rows = area(8938, 512, "p (g n) -> p g n", g=G4)
        CW, CSW = HC + SEQ, HC + TS
        CL = CW + NB * CSW
        gluT = area(0, G4 * CL, "p (g n) -> p g n", g=G4)
        acc = area(3256, G4 * TOK, "p (g n) -> p g n", g=G4)
        c_rows = area(3256, 1024, "p (j n) -> p j n", 4 * HC, j=2)
        d_rows = area(4280, 512, p=NB * HDD)
        tap_rows = area(4792, 512, p=CROWS)
        DW, DSW = HDD + SEQ, HDD + TS
        DL = DW + NB * DSW
        cxT = area(5432, G4 * DL, "p (g n) -> p g n", g=G4)
        cd = area(7680, G4 * TOK, "p (g n) -> p g n", g=G4)
        gate_tmp = [area(9856 + TOK * i, TOK) for i in range(2)]
        ln_rows = [area(9856 + 512 * i, 512) for i in range(2)]
        gb_flat = gb[:, :, :].rearrange("p a n -> p (a n)")
        conv_part = [gb_flat[:, TOK * i:TOK * (i + 1)] for i in range(2)]
        conv_rest = gb_flat[:, 2 * TOK:3 * TOK]
        tails = [gb[:, 0, 0:512], gb[:, 0, 512:1024], gb[:, 1, 0:512], gb[:, 1, 512:1024]]
        qT = area(0, KC * TOK, "p (k n) -> p k n", k=KC)
        KT = [area(4352 + 2048 * i, 2048, "p (k m) -> p k m", k=KC) for i in range(2)]
        prob = area(8448, 1024)
        probT = area(9472, 1024, "p (k n) -> p k n", k=KC)
        q_only = gb[:, :, :].rearrange("p a n -> p (a n)").rearrange("p (k b n) -> p k b n", k=KC, b=NB)
        p_only = area(0, 2048, "p (k b n) -> p k b n", k=KC, b=NB)
        xg = [area(1024 * i, 1024) for i in range(2)]
        silu = area(2048, 512)
        hid = area(2560, 512)
        both = area(5760, 2 * TILES * EXPERTS, "p (j t e) -> p j t e", j=2, t=TILES)
        ye = [area(3072 + 1024 * i, 1024) for i in range(2)]
        hit = [area(5120 + 320 * i, 320).bitcast(BF16).rearrange("p (t n) -> p t n", t=TILES) for i in range(2)]
        logitT = area(6400, 640, p=ROUTE)
        back = [[area(6400 + 2048 * i + 1024 * j, 1024) for j in range(2)] for i in range(2)]
        wr_rows = area(10496, KC * ROUTE, "p (k n) -> p k n", k=KC)
        xgT_hi = xhi[:, :, 0:P]
        xgT_lo = xlo[:, :, 0:P]
        hidT_hi = xhi[:, 0:4, P:2 * P]
        hidT_lo = xlo[:, 0:4, P:2 * P]
        kept = area(5920, TILES * EXPERTS, "p (t e) -> p t e", t=TILES)
        slot_value = area(6000, TILES * EXPERTS, "p (t e) -> p t e", t=TILES)
        gates = lgt[:, :, 0:EXPERTS]
        tok2_f = lgt[:, :, EXPERTS:EXPERTS + 2]
        is_of = area(10656, FURTHER * EXPERTS, "p (j e) -> p j e", j=FURTHER)
        first_rank = area(10784, FURTHER)
        nth = area(6080, FURTHER * EXPERTS, "p (j e) -> p j e", j=FURTHER)
        level = area(10800, LEVELS * EXPERTS, "p (r e) -> p r e", r=LEVELS)
        total = [area(10864 + 24 * i, EXPERTS // 2 + EXPERTS) for i in range(2)]
        own = area(10800, TILES * EXPERTS, "p (t e) -> p t e", t=TILES)
        own_rank = area(10912, TILES)
        own_gate = area(10920, TILES)
        spare = area(10928, 1)
        group_exp = area(10936, TILES * GROUPS, "p (t g) -> p t g", t=TILES)
        hit_f = area(5120, TILES * P, "p (t n) -> p t n", t=TILES)
        rowsT = area(4096, 1024, "p (k n) -> p k n", k=KC)
        hidT = area(1024, 512, "p (k n) -> p k n", k=4)
        y_hi = xhi[:, 0:4, 2 * P:4 * P]
        y_lo = xlo[:, 0:4, 2 * P:4 * P]
        hitT = xhi[:, 4:4 + (TILES + 1) // 2, 2 * P:4 * P]

        PAIR = [ps[:, 2 * i:2 * i + 2, :] for i in range(4)]
        A_, B_, C_, D_ = range(4)

        def pair_flat(i):
            return PAIR[i].rearrange("p b n -> p (b n)")

        def pair_chunks(i):
            return pair_flat(i).rearrange("p (k n) -> p k n", k=KC)

        block = ctx.enter_context(nc.Block())

        def wait_release(eng, i, shift=0):
            if i >= RING:
                kind, value = ring_release[i - RING]
                eng.wait_ge(sig("lo_made" if kind == "spl" else "plain_used"), value + shift)

        def chained(eng, name):
            n = [0]

            def link(ins):
                n[0] += 1
                ins.then_inc(sig(name), 1)
                eng.wait_ge(sig(name), n[0])

            def mark(ins):
                n[0] += 1
                ins.then_inc(sig(name), 1)
                return n[0]

            link.mark = mark
            return link

        def wait_product(eng, tag, t, name):
            if t == LASTT:
                eng.wait_ge(sig("split_used"), SPL[(name, 3)] + 1)
            else:
                eng.wait_ge(sig(tag + "_mm"), past(tag + "_mm") + t + 1)

        def wait_column(eng, tag, name, u, o):
            if o == 1:
                eng.wait_ge(sig("split_used"), SPL[(name, u)] + 1)
            else:
                eng.wait_ge(sig(tag + "_mm"), past(tag + "_mm") + u + 1)

        def first_unit(c):
            return 4 + 6 * (c - 1) if c else 0

        def unit_value(base, k, i):
            return base + k + 1 + 12 * i

        N_SMALL = {0: 5 + NB, 1: 7}
        GB_LOADS = {}
        for n_, key_ in enumerate(("lnv", "out0", "o0", "moe0", "out1", "o1", "moe1")):
            GB_LOADS[key_] = 32 * (n_ + 1)
        def odd(tag):
            return int(tag[:-1] == "o")

        C_ROWS_BANK = (4, 5, 2, 3, 4)
        TAIL_SOURCES = ((HC, lambda g: gluT[:, g, CW - HC:CW]), (NS, lambda g: flat[:, 0, g, :]),
                        (HDD, lambda g: cxT[:, g, DW - HDD:DW]), (NB * HDD, lambda g: flat[:, 1, g, 0:NB * HDD]))

        def further_blocks(eng, l):
            eng.wait_ge(sig(f"listed{l}"), past(f"listed{l}") + 1)
            return eng.value_load(blocks[0:1, 0:1], min_val=0, max_val=FURTHER)

        def again(l, name):
            return sig(f"again{l}_{name}")

        def again_slot(l, unit):
            return raw[(MOE_RAW[l] + 6 * EXPERTS + unit % 4) % RING]

        @block.sync
        def _(sp):
            sp.dma_start(mem_rows, a["mem_prompt"][0].rearrange("(m p) n -> p m n", p=P)).then_inc(sig("mem_landed"), 16)
            i_raw = 0
            for u in UNITS:
                if u[0] == "unit":
                    _, key, src, wait_kv = u
                    if wait_kv:
                        for par in range(2):
                            sp.wait_ge(sig(f"kv_stored{par}"), 16 * 2 * DEPTH)
                    wait_release(sp, i_raw)
                    for dst, part in src(raw[i_raw % RING][:, :]):
                        sp.dma_start(dst, part).then_inc(sig(f"raw_landed{i_raw % RING}"), 16)
                    i_raw += 1
                    if key == ("wk0", 3):
                        sp.dma_start(h[:, 0:LASTT, :], a["x_prompt"][0].rearrange("(t p) n -> p t n", p=P)).then_inc(sig("x_landed"), 16)
                        sp.dma_start(h[0:NS, LASTT, :], a["x_sample"].rearrange("b t n -> (b t) n")).then_inc(sig("x_landed"), 16)
                    continue
                l, rb = u[1], i_raw
                w_gate = a["w_gate"][l].rearrange("e (u k p) n -> u e p k n", u=2, p=P)
                w_up = a["w_up"][l].rearrange("e (u k p) n -> u e p k n", u=2, p=P)
                w_down = a["w_down"][l].rearrange("e (u k p) n -> u e p k n", u=2, p=P)

                def expert_load(k, i, w, e):
                    wait_release(sp, rb + k, 12 * i)
                    slot = (rb + k) % RING
                    if isinstance(e, int):
                        src = w[e]
                    else:
                        src = w[bass.ds(e, 1)].rearrange("a p k n -> (a p) k n")
                    sp.dma_start(raw[slot][:, :].rearrange("p (k n) -> p k n", k=src.shape[1]), src).then_inc(sig(f"raw_landed{slot}"), 16)

                def load_step(c, i):
                    k, n = first_unit(c), c + 2 * i
                    if c < EXPERTS:
                        expert_load(k, i, w_gate[0], n)
                        expert_load(k + 1, i, w_gate[1], n)
                        expert_load(k + 2, i, w_up[0], n)
                        expert_load(k + 3, i, w_up[1], n)
                        k += 4
                    if c:
                        expert_load(k, i, w_down[0], n - 1)
                        expert_load(k + 1, i, w_down[1], n - 1)

                load_step(0, 0)
                for c in range(1, 3):
                    load_step(c, 0)
                with sp.Fori(0, EXPERTS // 2 - 3) as i:
                    load_step(3, i)
                    load_step(4, i)
                for c in range(EXPERTS - 3, EXPERTS + 1):
                    load_step(c, 0)
                i_raw += 6 * EXPERTS
                n = further_blocks(sp, l)
                def one_block(i):
                    e = sp.value_load(block_expert[0:1, i:i + 1] if isinstance(i, int) else block_expert[0:1, bass.ds(i, 1)], min_val=0, max_val=EXPERTS - 1)
                    for k, w in enumerate((w_gate, w_up, w_down)):
                        for q in range(2):
                            if k == 2:
                                sp.wait_ge(again(l, "used"), 2 + q + 6 * i)
                            elif isinstance(i, int):
                                wait_release(sp, i_raw + 2 * k + q)
                            elif k == q == 0:
                                sp.wait_ge(again(l, "used"), 1 + 6 * i)
                            src = w[q][bass.ds(e, 1)].rearrange("a p k n -> (a p) k n")
                            sp.dma_start(again_slot(l, 2 * k + q)[:, :].rearrange("p (k n) -> p k n", k=src.shape[1]), src).then_inc(again(l, f"landed{q}"), 16)

                with sp.If(n > 0):
                    one_block(0)
                with sp.If(n > 1):
                    with sp.Fori(1, FURTHER) as i:
                        with sp.If(n > i):
                            one_block(i)
                if l < DEPTH - 1:
                    sp.wait_ge(again(l, "used"), 1 + 6 * n)

        @block.tensor
        def _(pe):
            def to_columns(tag, t, m, source, ready):
                ready()
                if t >= 2:
                    pe.wait_ge(sig(tag + "_lo"), past(tag + "_lo") + t - 1)
                pair = pair_chunks(C_ + t % 2)
                for k in range(KC):
                    mm = pe.transpose(pair[:, k, 0:m], source[0:m, k * P:(k + 1) * P], ident[0:m, 0:m])
                mm.then_inc(sig(tag + "_tr"), 1)

            def row_product(tag, t, m, lhs_cols, pair, name, first, last):
                for q in range(4):
                    s = SPL[(name, q)]
                    if first:
                        pe.wait_ge(sig("hi_made"), s + 1)
                        pe.wait_ge(sig("lo_made"), s + 1)
                    for kk in range(2):
                        k = 2 * q + kk
                        for n, (x, w) in enumerate(((xhi, whi), (xlo, whi), (xhi, wlo))):
                            for half in range(2):
                                at = kk * 1024 + 512 * half
                                mm = pe.matmul(ps[0:m, 2 * pair + half, :], x[:, k, lhs_cols], w[s % RING][:, at:at + 512],
                                               start=(k == 0 and n == 0), stop=(k == KC - 1 and n == 2))
                    if last:
                        mm.then_inc(sig("split_used"), 1)
                if not last:
                    mm.then_inc(sig(tag + "_mm"), 1)

            def column_product(tag, name, u, o, pair):
                s = SPL[(name, u)]
                if o == 0:
                    pe.wait_ge(sig("hi_made"), s + 1)
                    pe.wait_ge(sig("lo_made"), s + 1)
                for k in range(KC):
                    at = k * 256 + o * P
                    for n, (x, w) in enumerate(((xhi, whi), (xlo, whi), (xhi, wlo))):
                        for half in range(2):
                            mm = pe.matmul(ps[:, 2 * pair + half, 0:MOVE], w[s % RING][:, at:at + P],
                                           x[:, k, half * MOVE:(half + 1) * MOVE],
                                           start=(k == 0 and n == 0), stop=(k == KC - 1 and n == 2))
                mm.then_inc(sig("split_used" if o else tag + "_mm"), 1)

            def half_columns(tag, name, half):
                s = SPL[(name, 0)]
                if half == 0:
                    pe.wait_ge(sig("hi_made"), s + 1)
                    pe.wait_ge(sig("lo_made"), s + 1)
                for o in range(2):
                    for k in range(KC):
                        at = k * 256 + o * P
                        for n, (x, w) in enumerate(((xhi, whi), (xlo, whi), (xhi, wlo))):
                            mm = pe.matmul(ps[:, 2 * o + half, 0:MOVE], w[s % RING][:, at:at + P],
                                           x[:, k, half * MOVE:(half + 1) * MOVE],
                                           start=(k == 0 and n == 0), stop=(k == KC - 1 and n == 2))
                    if half:
                        mm.then_inc(sig("split_used" if o else tag + "_mm"), 1)

            def half_logits(l, half):
                if half == 0:
                    pe.wait_ge(sig(f"wr{l}_hi"), past(f"wr{l}_hi") + 1)
                    pe.wait_ge(sig(f"wr{l}_lo"), past(f"wr{l}_lo") + 1)
                for k in range(KC):
                    for n, (x, w) in enumerate(((xhi, wrhi), (xlo, wrhi), (xhi, wrlo))):
                        mm = pe.matmul(ps[0:ROUTE, half, 0:MOVE], w[:, k, :], x[:, k, half * MOVE:(half + 1) * MOVE],
                                       start=(k == 0 and n == 0), stop=(k == KC - 1 and n == 2))
                if half:
                    mm.then_inc(sig(f"lg{l}_mm"), 1)

            def product_then_columns(tag, name, operands_ready, first_half, after_tile=None):
                for t in range(TILES + 1):
                    if t < TILES and (t or not odd(tag)):
                        operands_ready(t)
                        if t >= 2:
                            pe.wait_ge(sig(tag + "_res"), past(tag + "_res") + t - 1)
                        row_product(tag, t, rows(t), cols(t), (t + odd(tag)) % 2, name, t == 0, t == LASTT)
                    if after_tile:
                        after_tile(t)
                    if t == TILES:
                        pe.wait_ge(sig(tag + "_res"), past(tag + "_res") + TILES)
                        pe.wait_ge(sig(tag + "_hi"), past(tag + "_hi") + 3)
                        pe.wait_ge(sig(tag + "_lo"), past(tag + "_lo") + 3)
                        first_half()
                    if t >= 1:
                        to_columns(tag, t - 1, rows(t - 1), h[:, t - 1, :],
                                   lambda: pe.wait_ge(sig(tag + "_row"), past(tag + "_row") + t))

            def small_operands():
                pe.wait_ge(sig("small_landed0"), 16 * N_SMALL[0])
                for g in range(G4):
                    mm = pe.transpose(ps[:, 4, g * P:(g + 1) * P], ws_rows[:, g, :], ident[:, :])
                mm.then_inc(sig("ws_tr"), 1)
                for g in range(G4):
                    mm = pe.transpose(ps[:, 5, g * P:g * P + NB * HIST], pool_rows[:, g * P:(g + 1) * P], ident[0:NB * HIST, 0:NB * HIST])
                mm.then_inc(sig("hist_tr"), 1)

            pe.wait_ge(sig("consts"), 9)
            for m in range(MT):
                to_columns("mem", m, P, mem_rows[:, m, :], lambda: pe.wait_ge(sig("mem_landed"), 16))
            pe.wait_ge(sig("mem_hi"), past("mem_hi") + MT)
            pe.wait_ge(sig("mem_lo"), past("mem_lo") + MT)
            n = 0
            for name in ("wk0", "wv0", "wk1", "wv1"):
                if name == "wv0":
                    small_operands()
                if name == "wv1":
                    pe.wait_ge(sig("ws_copied"), past("ws_copied") + 1)
                    pe.wait_ge(sig("hist_copied"), past("hist_copied") + 1)
                    for t in range(2):
                        to_columns("x", t, P, h[:, t, :], lambda: pe.wait_ge(sig("x_landed"), 32))
                for m in range(MT):
                    if n >= 2:
                        pe.wait_ge(sig("kv_copied"), n - 1)
                    row_product("kv", m, P, slice(m * P, m * P + P), n % 2, name, m == 0, m == MT - 1)
                    n += 1

            for t in range(2, TILES):
                to_columns("x", t, rows(t), h[:, t, :], lambda: pe.wait_ge(sig("x_landed"), 32))
            pe.wait_ge(sig("x_hi"), past("x_hi") + TILES)
            pe.wait_ge(sig("x_lo"), past("x_lo") + TILES)
            pe.wait_ge(sig("kv_copied"), 2 * 2 * DEPTH)
            for u in range(2):
                for o in range(2):
                    if 2 * u + o >= 2:
                        pe.wait_ge(sig("z_copied"), 2 * u + o - 1)
                    column_product("z", "wz", u, o, o)
            pe.wait_ge(sig("z_copied"), 4)

            def mix(t):
                m = rows(t)
                pe.wait_ge(sig("v_row"), past("v_row") + t + 1)
                if t == 0:
                    pe.wait_ge(sig("ws_masked"), 1)
                if t == LASTT:
                    pe.wait_ge(sig("wss_landed"), 16 * NB)
                if t >= 2:
                    pe.wait_ge(sig("gated"), t - 1)
                for g in range(G4):
                    w = wsT[:, g, :] if t < LASTT else wsS[:, g, :]
                    mm = pe.matmul(ps[0:m, 4 + t % 2, g * P:(g + 1) * P], w, uv[t % 2][0:m, 512 + g * P:512 + (g + 1) * P],
                                   start=True, stop=True)
                mm.then_inc(sig("mixed"), 1)

            def gated_columns(t):
                m = rows(t)
                pe.wait_ge(sig("gated"), t + 1)
                if t >= 2:
                    pe.wait_ge(sig("a_lo"), t - 1)
                for g in range(G4):
                    mm = pe.transpose(ps[:, 6 + t % 2, g * P:g * P + m], uv[t % 2][0:m, g * P:(g + 1) * P], ident[0:m, 0:m])
                mm.then_inc(sig("a_tr"), 1)

            def pooled_products():
                for g in range(G4):
                    pe.wait_ge(sig("pooled"), g + 1)
                    if g == 0:
                        pe.wait_ge(sig("uv_gelu"), LASTT)
                    elif g == 1:
                        pe.wait_ge(sig("uv_gelu"), TILES)
                    else:
                        pe.wait_ge(sig("b_lo"), g - 1)
                    bank = 2 * ((g + 1) % 2)
                    pe.matmul(ps[:, bank, :], wp[:, g, :], pz[:, g, 0:SEQ], start=True, stop=True)
                    pe.matmul(ps[:, bank + 1, 0:NS], wp[:, g, :], pz[:, g, SEQ:TOK], start=True, stop=True).then_inc(sig("b_mm"), 1)

            for t in range(TILES + 2):
                if t == TILES:
                    pooled_products()
                if t < TILES:
                    if t >= 2:
                        pe.wait_ge(sig("uv_gelu"), t - 1)
                    row_product("uv", t, rows(t), cols(t), t % 2, "wuv", t == 0, t == LASTT)
                if 1 <= t <= TILES:
                    mix(t - 1)
                if t >= 2:
                    gated_columns(t - 2)
            def last_rows_of_z(t):
                if t == 0:
                    pe.wait_ge(sig("a_lo"), TILES)
                    for g in range(G4):
                        mm = pe.transpose(ps[0:HIST, 4, g * P:(g + 1) * P], zT[:, g, ZW - HIST:ZW], ident[:, :])
                    mm.then_inc(sig("z_back"), 1)
                    pe.wait_ge(sig("z_flat"), 1)
                    for g in range(G4):
                        mm = pe.transpose(ps[0:NS, 5, g * P:(g + 1) * P], flat[:, 0, g, :], ident[:, :])
                    mm.then_inc(sig("z_back"), 1)
                if t == 1:
                    pe.wait_ge(sig("z_back_copied"), 2)

            def out_before(l):
                def waits(t):
                    if l == 0:
                        if t == 0:
                            pe.wait_ge(sig("b_hi"), G4)
                            pe.wait_ge(sig("b_lo"), G4)
                        pe.wait_ge(sig("a_hi"), t + 1)
                        pe.wait_ge(sig("a_lo"), t + 1)
                    else:
                        if t == 0:
                            pe.wait_ge(sig("d_hi"), 1)
                            pe.wait_ge(sig("d_lo"), 1)
                            pe.wait_ge(sig("tails_copied"), 4)
                        if t == 1:
                            pe.wait_ge(sig("c_norm"), LASTT)
                        if t == 2:
                            pe.wait_ge(sig("c_silu"), TILES)
                        pe.wait_ge(sig("c_hi"), t + 1)
                        pe.wait_ge(sig("c_lo"), t + 1)
                return waits

            def attention(l):
                pe.wait_ge(sig(f"out{l}_hi"), past(f"out{l}_hi") + TILES)
                pe.wait_ge(sig(f"out{l}_lo"), past(f"out{l}_lo") + TILES)
                half_columns(f"q{l}", f"wq{l}", 1)
                def key_columns(key, n):
                    i = RAW[key]
                    pe.wait_ge(sig(f"raw_landed{i % RING}"), LANDED[i])
                    rows_ = raw[i % RING][:, :].rearrange("p (m n) -> p m n", m=MT)
                    for m in range(MT):
                        if n:
                            pe.wait_ge(sig(f"kt{l}_{'ab'[m]}"), past(f"kt{l}_{'ab'[m]}") + n)
                        pair = pair_chunks(C_ + m)
                        for k in range(KC):
                            mm = pe.transpose(pair[:, k, :], rows_[:, m, k * P:(k + 1) * P], ident[:, :])
                        mm.then_inc(sig("plain_used" if m else f"kt{l}_tr"), 1)

                for u in range(1, 4):
                    if u == 3:
                        key_columns(("k", l), 0)
                    for o in range(2):
                        j = 2 * u + o
                        if j >= 2:
                            pe.wait_ge(sig(f"q{l}_copied"), past(f"q{l}_copied") + j - 1)
                        column_product(f"q{l}", f"wq{l}", u, o, o)
                pe.wait_ge(sig(f"q{l}_copied"), past(f"q{l}_copied") + KC)

                iv = RAW[("v", l)]
                v_rows = raw[iv % RING][:, :].rearrange("p (m n) -> p m n", m=MT)

                def scores(t):
                    if t == 0:
                        pe.wait_ge(sig(f"kt{l}_a"), past(f"kt{l}_a") + 1)
                        pe.wait_ge(sig(f"kt{l}_b"), past(f"kt{l}_b") + 1)
                    if t >= 2:
                        pe.wait_ge(sig(f"prob{l}_exp"), past(f"prob{l}_exp") + t - 1)
                    pair = pair_flat(t % 2)
                    for j in range(KC):
                        hh, c = j // 2, j % 2
                        mm = pe.matmul(pair[:, hh * NMEM:(hh + 1) * NMEM], qT[:, j, cols(t)], KT[0][:, j, :],
                                       start=(c == 0), stop=(c == 1))
                    mm.then_inc(sig(f"score{l}_mm"), 1)

                def prob_columns(t, m):
                    pe.wait_ge(sig(f"prob{l}_norm"), past(f"prob{l}_norm") + t + 1)
                    if t >= 1:
                        pe.wait_ge(sig(f"pt{l}_copied"), past(f"pt{l}_copied") + t)
                    pair = pair_chunks(C_)
                    for k in range(KC):
                        mm = pe.transpose(pair[:, k, 0:m], prob[0:m, k * P:(k + 1) * P], ident[0:m, 0:m])
                    mm.then_inc(sig(f"prob{l}_tr"), 1)

                def mixed_values(t):
                    pe.wait_ge(sig(f"pt{l}_copied"), past(f"pt{l}_copied") + t + 1)
                    if t == 0:
                        pe.wait_ge(sig(f"raw_landed{iv % RING}"), LANDED[iv])
                    else:
                        pe.wait_ge(sig(f"att{l}_lo"), past(f"att{l}_lo") + t)
                    pair = pair_chunks(D_)
                    for j in range(KC):
                        for m in range(MT):
                            mm = pe.matmul(pair[:, j, :], v_rows[:, m, j * P:(j + 1) * P], probT[:, 2 * (j // 2) + m, :],
                                           start=(m == 0), stop=(m == MT - 1))
                    mm.then_inc(sig("plain_used" if t == LASTT - 1 else f"att{l}_mm"), 1)

                scores(0)
                scores(1)
                for t in range(LASTT):
                    prob_columns(t, P)
                    if t + 2 < LASTT:
                        scores(t + 2)
                    mixed_values(t)
                pe.wait_ge(sig(f"att{l}_lo"), past(f"att{l}_lo") + LASTT)
                key_columns(("ks", l, 0), 1)
                for b in range(NB):
                    if b + 1 < NB:
                        key_columns(("ks", l, b + 1), b + 2)
                    if b == 0:
                        pe.wait_ge(sig(f"q{l}_only"), past(f"q{l}_only") + 1)
                        pe.wait_ge(sig(f"prob{l}_norm"), past(f"prob{l}_norm") + LASTT)
                    pe.wait_ge(sig(f"kt{l}_a"), past(f"kt{l}_a") + b + 2)
                    pe.wait_ge(sig(f"kt{l}_b"), past(f"kt{l}_b") + b + 2)
                    pair = pair_flat(A_)
                    for j in range(KC):
                        hh, c = j // 2, j % 2
                        mm = pe.matmul(pair[0:NS, hh * NMEM:(hh + 1) * NMEM], q_only[:, j, b, :], KT[(b + 1) % 2][:, j, :],
                                       start=(b == 0 and j in (0, 4)), stop=(b == NB - 1 and c == 1), skip_group_check=True)
                    mm.then_inc(sig(f"sscore{l}_mm"), 1)
                pe.wait_ge(sig(f"att{l}_hi"), past(f"att{l}_hi") + LASTT)
                row_product(f"o{l}", 0, P, cols(0), B_, f"wo{l}", True, False)
                prob_columns(LASTT, NS)
                for b in range(NB):
                    if b == 0:
                        pe.wait_ge(sig(f"prob{l}_only"), past(f"prob{l}_only") + 1)
                    i = RAW[("vs", l, b)]
                    pe.wait_ge(sig(f"raw_landed{i % RING}"), LANDED[i])
                    vb = raw[i % RING][:, :].rearrange("p (m n) -> p m n", m=MT)
                    for hh in range(HEADS):
                        for m in range(MT):
                            mm = pe.matmul(pair_flat(A_)[0:NS, hh * HD:(hh + 1) * HD], p_only[:, 2 * hh + m, b, :],
                                           vb[:, m, hh * HD:(hh + 1) * HD],
                                           start=(b == 0 and m == 0 and hh in (0, 2)), stop=(b == NB - 1 and m == 1),
                                           skip_group_check=True)
                    mm.then_inc(sig("plain_used"), 1)

            def o_before(l):
                def waits(t):
                    tiles = LASTT if t < LASTT else TILES
                    pe.wait_ge(sig(f"att{l}_hi"), past(f"att{l}_hi") + tiles)
                    pe.wait_ge(sig(f"att{l}_lo"), past(f"att{l}_lo") + tiles)
                return waits

            def sample_values(l):
                def columns(t):
                    if t == 0:
                        pe.wait_ge(sig(f"os{l}_copied"), past(f"os{l}_copied") + 1)
                        for k in range(KC):
                            mm = pe.transpose(pair_chunks(C_)[:, k, 0:NS], prob[0:NS, k * P:(k + 1) * P], ident[0:NS, 0:NS])
                        mm.then_inc(sig(f"os{l}_tr"), 1)
                    if t == 1:
                        pe.wait_ge(sig(f"att{l}_lo"), past(f"att{l}_lo") + TILES)
                return columns

            def router(l):
                pe.wait_ge(sig(f"o{l}_hi"), past(f"o{l}_hi") + TILES)
                pe.wait_ge(sig(f"o{l}_lo"), past(f"o{l}_lo") + TILES)
                half_logits(l, 1)
                pe.wait_ge(sig(f"lg{l}_copied"), past(f"lg{l}_copied") + 1)
                for t in range(TILES):
                    mm = pe.transpose(ps[:, 2, t * 32:t * 32 + ROUTE], logitT[:, t * P:(t + 1) * P], ident[0:ROUTE, 0:ROUTE])
                mm.then_inc(sig(f"lg{l}_tr"), 1)
                pe.transpose(ps[0:1, 7, 0:1], ident[0:1, 0:1], ident[0:1, 0:1]).then_inc(again(l, "used"), 1)
                pe.wait_ge(sig(f"member{l}"), past(f"member{l}") + 1)
                for t in range(TILES + 1):
                    for tt in range(min(t + 1, TILES)):
                        mm = pe.matmul(ps[:, 3, t * EXPERTS:(t + 1) * EXPERTS], (before if tt == t else ones)[:, :], member[:, tt, :],
                                       start=(tt == 0), stop=(tt == min(t, LASTT)))
                mm.then_inc(sig(f"rank{l}_mm"), 1)

            def experts(l):
                sb_ = MOE_SPL[l]

                def find_tokens(c, i):
                    n = c + 2 * i
                    pe.wait_ge(sig(f"hit{l}"), past(f"hit{l}") + n + 1)
                    if c:
                        pe.wait_ge(sig(f"tok{l}"), past(f"tok{l}") + n)
                    for t in range(TILES):
                        mm = pe.matmul(ps[:, 7, 0:2], hit[c % 2][:, t, :], tok2[:, t, :], start=(t == 0), stop=(t == LASTT))
                    mm.then_inc(sig(f"tok{l}_mm"), 1)

                def gathered_columns(c, i):
                    n = c + 2 * i
                    pe.wait_ge(sig(f"gathered{c % 2}"), 16 * (l * EXPERTS // 2 + c // 2 + 1) + 16 * i)
                    if c:
                        pe.wait_ge(sig(f"xg{l}_lo"), past(f"xg{l}_lo") + n)
                    for k in range(KC):
                        mm = pe.transpose(pair_chunks(C_)[:, k, :], xg[c % 2][:, k * P:(k + 1) * P], ident[:, :])
                    mm.then_inc(sig(f"xg{l}_tr"), 1)

                def expert_product(k0, i, bank, hi, lo, k_unit, nbanks):
                    for q in range(2):
                        s = (sb_ + k0 + q) % RING
                        pe.wait_ge(sig("hi_made"), unit_value(sb_, k0 + q, i))
                        pe.wait_ge(sig("lo_made"), unit_value(sb_, k0 + q, i))
                        for kk in range(k_unit):
                            k = q * k_unit + kk
                            for n, (x, w) in enumerate(((hi, whi), (lo, whi), (hi, wlo))):
                                for half in range(nbanks):
                                    at = (kk * nbanks + half) * 512
                                    mm = pe.matmul(ps[:, bank + half, :], x[:, k, :], w[s][:, at:at + 512],
                                                   start=(k == 0 and n == 0), stop=(k == 2 * k_unit - 1 and n == 2))
                        mm.then_inc(sig("split_used"), 1)

                def step(c, i):
                    n, k = c + 2 * i, first_unit(c)
                    if c < EXPERTS:
                        pe.wait_ge(sig(f"xg{l}_hi"), past(f"xg{l}_hi") + n + 1)
                        pe.wait_ge(sig(f"xg{l}_lo"), past(f"xg{l}_lo") + n + 1)
                        if c:
                            pe.wait_ge(sig(f"hid{l}"), past(f"hid{l}") + n)
                        expert_product(k, i, 0, xgT_hi, xgT_lo, 4, 1)
                        expert_product(k + 2, i, 1, xgT_hi, xgT_lo, 4, 1)
                        k += 4
                    if c < EXPERTS - 1:
                        gathered_columns(c + 1, i)
                    if c:
                        pe.wait_ge(sig(f"hid{l}_hi"), past(f"hid{l}_hi") + n)
                        pe.wait_ge(sig(f"hid{l}_lo"), past(f"hid{l}_lo") + n)
                        if c > 1:
                            pe.wait_ge(sig(f"ye{l}"), past(f"ye{l}") + n - 1)
                        expert_product(k, i, 2, hidT_hi, hidT_lo, 2, 2)
                    if c < EXPERTS:
                        pe.wait_ge(sig(f"hid{l}"), past(f"hid{l}") + n + 1)
                        if c:
                            pe.wait_ge(sig(f"hid{l}_lo"), past(f"hid{l}_lo") + n)
                        for k in range(4):
                            mm = pe.transpose(ps[:, 6, k * P:(k + 1) * P], hid[:, k * P:(k + 1) * P], ident[:, :])
                        mm.then_inc(sig(f"hid{l}_tr"), 1)
                    if c < EXPERTS - 2:
                        find_tokens(c + 2, i)

                pe.wait_ge(sig(f"ranked{l}"), past(f"ranked{l}") + 1)
                find_tokens(0, 0)
                find_tokens(1, 0)
                gathered_columns(0, 0)
                step(0, 0)
                for c in range(1, 3):
                    step(c, 0)
                with pe.Fori(0, EXPERTS // 2 - 3) as i:
                    step(3, i)
                    step(4, i)
                for c in range(EXPERTS - 3, EXPERTS):
                    step(c, 0)
                step(EXPERTS, 0)

            def further(l):
                pe.wait_ge(sig(f"ye{l}"), past(f"ye{l}") + EXPERTS)
                pe.wait_ge(sig(f"hid{l}_lo"), past(f"hid{l}_lo") + EXPERTS)
                pe.wait_ge(sig(f"tok{l}"), past(f"tok{l}") + EXPERTS)
                n = further_blocks(pe, l)
                def one_block(i):
                    pe.wait_ge(again(l, "hit"), 1 + i)
                    for t in range(TILES):
                        mm = pe.matmul(ps[:, 7, 0:2], hit_f[:, t, :], tok2_f[:, t, :], start=(t == 0), stop=(t == LASTT))
                    mm.then_inc(again(l, "tok_mm"), 1)
                    for t in range(TILES):
                        mm = pe.transpose(pair_flat(C_)[:, t * P:(t + 1) * P], hit_f[:, t, :], ident[:, :])
                    mm.then_inc(again(l, "tr"), 1)
                    pe.wait_ge(again(l, "copied"), 1 + 4 * i)
                    pe.wait_ge(again(l, "gathered"), 16 + 16 * i)
                    for k in range(KC):
                        mm = pe.transpose(pair_chunks(C_)[:, k, :], xg[0][:, k * P:(k + 1) * P], ident[:, :])
                    mm.then_inc(again(l, "tr"), 1)
                    pe.wait_ge(again(l, "copied"), 2 + 4 * i)
                    pe.wait_ge(again(l, "added"), 1 + TILES * i)
                    for part in range(2):
                        for q in range(2):
                            pe.wait_ge(again(l, f"landed{q}"), 32 + 48 * i)
                            for kk in range(4):
                                mm = pe.matmul(ps[:, part, :], rowsT[:, 4 * q + kk, :], again_slot(l, 2 * part + q)[:, 512 * kk:512 * kk + 512],
                                               start=(q == 0 and kk == 0), stop=(q == 1 and kk == 3))
                            mm.then_inc(again(l, "used"), 1)
                    pe.wait_ge(again(l, "hid"), 1 + i)
                    for k in range(4):
                        mm = pe.transpose(ps[:, 6, k * P:(k + 1) * P], hid[:, k * P:(k + 1) * P], ident[:, :])
                    mm.then_inc(again(l, "tr"), 1)
                    pe.wait_ge(again(l, "copied"), 3 + 4 * i)
                    for q in range(2):
                        pe.wait_ge(again(l, f"landed{q}"), 48 + 48 * i)
                        for kk in range(2):
                            for half in range(2):
                                at = 1024 * kk + 512 * half
                                mm = pe.matmul(ps[:, 2 + half, :], hidT[:, 2 * q + kk, :], again_slot(l, 4 + q)[:, at:at + 512],
                                               start=(q == 0 and kk == 0), stop=(q == 1 and kk == 1))
                        mm.then_inc(again(l, "used"), 1)
                    pe.wait_ge(again(l, "copied"), 4 + 4 * i)
                    for t in range(TILES):
                        if t >= 2:
                            pe.wait_ge(again(l, "added"), t + TILES * i)
                        m = rows(t)
                        for half in range(2):
                            for y in (y_hi, y_lo):
                                mm = pe.matmul(ps[0:m, 2 * (t % 2) + half, :].rearrange("p (k n) -> p k n", k=2),
                                               hitT[:, t // 2, P * (t % 2):P * (t % 2) + m], y[:, 2 * half:2 * half + 2, :],
                                               start=y is y_hi, stop=y is y_lo)
                        mm.then_inc(again(l, "share_mm"), 1)

                with pe.If(n > 0):
                    one_block(0)
                with pe.If(n > 1):
                    with pe.Fori(1, FURTHER) as i:
                        with pe.If(n > i):
                            one_block(i)

            def combine_columns(l):
                if l == DEPTH - 1:
                    return
                for t in range(TILES):
                    if t == 0:
                        pe.wait_ge(sig(f"xg{l}_lo"), past(f"xg{l}_lo") + EXPERTS)
                        pe.wait_ge(sig(f"hid{l}_lo"), past(f"hid{l}_lo") + EXPERTS)
                    if t == LASTT:
                        pe.wait_ge(sig(f"moe{l}_hi"), past(f"moe{l}_hi") + 3)
                        pe.wait_ge(sig(f"moe{l}_lo"), past(f"moe{l}_lo") + 3)
                        half_columns("glu", "wglu", 0)
                    to_columns(f"moe{l}", t, rows(t), h[:, t, :], lambda: pe.wait_ge(sig(f"moe{l}_row"), past(f"moe{l}_row") + t + 1))

            def conv_layer():
                pe.wait_ge(sig("small_landed1"), 16 * N_SMALL[1])
                pe.wait_ge(sig("moe0_lo"), past("moe0_lo") + TILES)
                for g in range(G4):
                    mm = pe.transpose(ps[:, 4, g * P:g * P + CROWS], tap_rows[:, g * P:(g + 1) * P], ident[0:CROWS, 0:CROWS])
                for g in range(G4):
                    mm = pe.transpose(ps[:, 5, g * P:g * P + NB * HDD], d_rows[:, g * P:(g + 1) * P], ident[0:NB * HDD, 0:NB * HDD])
                for j in range(2):
                    for g in range(G4):
                        mm = pe.transpose(ps[:, 6 + j, g * P:g * P + 4 * HC], c_rows[:, j, g * P:(g + 1) * P], ident[0:4 * HC, 0:4 * HC])
                mm.then_inc(sig("hist1_tr"), 1)
                pe.wait_ge(sig("moe0_hi"), past("moe0_hi") + TILES)
                half_columns("glu", "wglu", 1)
                for g in range(1, G4):
                    if g == 1:
                        pe.wait_ge(sig("hist1_copied"), past("hist1_copied") + 1)
                    else:
                        pe.wait_ge(sig("glu"), g - 1)
                    column_product("glu", "wglu", g, 0, 2 * (g % 2))
                    column_product("glu", "wglu", g, 1, 2 * (g % 2) + 1)
                for g in range(G4):
                    if g < 2:
                        pe.wait_ge(sig("glu"), G4 - 1 + g)
                    else:
                        pe.wait_ge(sig("cx"), g - 1)
                    column_product("cx", "wcx", g, 0, 2 * (g % 2))
                    column_product("cx", "wcx", g, 1, 2 * (g % 2) + 1)
                for u in range(2):
                    pe.wait_ge(sig("cx"), G4 - 1 + u)
                    for o in range(2):
                        column_product("gb", "wgb", u, o, 2 * u + o)
                pe.wait_ge(sig("d_out"), 4)
                pe.wait_ge(sig("flat_ready"), 2)
                for n, (m, src) in enumerate(TAIL_SOURCES):
                    for g in range(G4):
                        mm = pe.transpose(ps[0:m, n, g * P:(g + 1) * P], src(g), ident[:, :])
                    mm.then_inc(sig("tails_tr"), 1)

                def conv_rows(t):
                    if t == 4:
                        pe.wait_ge(sig("c_norm"), 1)
                    for g in range(G4):
                        mm = pe.transpose(ps[0:rows(t), C_ROWS_BANK[t], g * P:(g + 1) * P], acc[:, g, cols(t)], ident[:, :])
                    mm.then_inc(sig("c_rows"), 1)

                def conv_columns(t):
                    m = rows(t)
                    pe.wait_ge(sig("c_norm"), t + 1)
                    if t >= 2:
                        pe.wait_ge(sig("c_silu"), t - 1)
                    for g in range(G4):
                        mm = pe.transpose(ps[:, 6 + t % 2, g * P:g * P + m], ln_rows[t % 2][0:m, g * P:(g + 1) * P], ident[0:m, 0:m])
                    mm.then_inc(sig("c_tr"), 1)

                pe.wait_ge(sig("conv"), G4 - 1)
                pe.wait_ge(sig("conv_pool"), 1)
                pe.wait_ge(sig("tails_copied"), 4)
                for t in range(4):
                    conv_rows(t)
                conv_columns(0)
                conv_rows(4)
                conv_columns(1)

                def rest_of_conv(t):
                    if t == 0:
                        conv_columns(2)
                        conv_columns(3)
                    elif t == 1:
                        conv_columns(4)
                return rest_of_conv

            for l in range(DEPTH):
                after_tile = conv_layer() if l else last_rows_of_z
                product_then_columns(f"out{l}", f"wout{l}", out_before(l), lambda: half_columns(f"q{l}", f"wq{l}", 0), after_tile)
                attention(l)
                product_then_columns(f"o{l}", f"wo{l}", o_before(l), lambda: half_logits(l, 0), sample_values(l))
                router(l)
                experts(l)
                further(l)
                combine_columns(l)

        def ahead(c):
            k, nxt = first_unit(c), first_unit(c + 1)
            own = [k + 3] + ([k + 4, k + 5] if c else [])
            return own, [nxt, nxt + 1] + ([nxt + 2] if c < EXPERTS - 1 else [])

        @block.scalar
        def _(act):
            def make_hi(key):
                i, s = RAW[key], SPL[key]
                act.wait_ge(sig(f"raw_landed{i % RING}"), LANDED[i])
                if s >= RING:
                    act.wait_ge(sig("split_used"), s - RING + 1)
                act.activation(whi[s % RING][:, :], raw[i % RING][:, :], ACT.Copy).then_inc(sig("hi_made"), 1)

            def columns_hi(tag, t, m):
                act.wait_ge(sig(tag + "_tr"), past(tag + "_tr") + t + 1)
                act.activation(xhi[:, :, t * P:t * P + m], pair_chunks(C_ + t % 2)[:, :, 0:m], ACT.Copy).then_inc(sig(tag + "_hi"), 1)

            for m in range(MT):
                columns_hi("mem", m, P)
            for q in range(4):
                make_hi(("wk0", q))
            small = sig("small_landed0")
            act.dma_start(ws_rows, a["w_spatial"][0].rearrange("g t s -> t g s")).then_inc(small, 16)
            act.dma_start(pool_rows, a["state_pool"][0].rearrange("b i n -> (b i) n")).then_inc(small, 16)
            act.dma_start(wp, a["w_pool"][0].rearrange("g c d -> c g d")).then_inc(small, 16)
            with nc.allow_non_contiguous_dma(reason="a few hundred words, once"):
                act.dma_start(b_rows[:, :], a["b_spatial"][0].rearrange("g t -> t g")).then_inc(small, 16)
                act.dma_start(pool_scale[:, :], a["pool_scale"][0].rearrange("(g p) -> p g", p=P)).then_inc(small, 16)
                for b in range(NB):
                    act.dma_start(b_rows_s[b * TS:(b + 1) * TS, :], a["b_spatial"][0][:, 0:TS].rearrange("g t -> t g")).then_inc(small, 16)
            names = ("wk0", "wv0", "wk1", "wv1")
            n = 0
            for w, name in enumerate(names):
                for m in range(MT):
                    if m == 0:
                        act.wait_ge(sig("kv_mm"), w + 1)
                    else:
                        nxt = [(names[w + 1], q) for q in range(4)] if w < 3 else [("wz", 0), ("wz", 1)]
                        for key in nxt:
                            make_hi(key)
                        act.wait_ge(sig("split_used"), SPL[(name, 3)] + 1)
                    if n >= 2:
                        act.wait_ge(sig(f"kv_stored{n % 2}"), 16 * (n // 2))
                    act.activation(kv_rows[n % 2], pair_flat(n % 2), ACT.Copy).then_inc(sig("kv_copied"), 1)
                    n += 1

            for t in range(TILES):
                columns_hi("x", t, rows(t))
            for u in range(2):
                make_hi(("wuv", u))
            act.wait_ge(sig("hist_zeroed"), past("hist_zeroed") + 1)
            for u in range(2):
                for o in range(2):
                    j = 2 * u + o
                    wait_column(act, "z", "wz", u, o)
                    act.activation(zT[:, j, HIST:HIST + MOVE], ps[:, 2 * o, 0:MOVE], ACT.Copy)
                    act.activation(zT[:, j, HIST + MOVE:ZW], ps[:, 2 * o + 1, 0:PB], ACT.Copy)
                    act.activation(zT[:, j, ZW:ZL].rearrange("p (b s) -> p b s", b=NB)[:, :, HIST:],
                                   ps[:, 2 * o + 1, PB:MOVE].rearrange("p (b s) -> p b s", b=NB), ACT.Copy).then_inc(sig("z_copied"), 1)
                make_hi(("wuv", 2 + u))
            def pooled_hi():
                act.wait_ge(sig("small_landed0"), 16 * N_SMALL[0])
                for g in range(G4):
                    bank = 2 * ((g + 1) % 2)
                    act.wait_ge(sig("b_mm"), g + 1)
                    act.activation(xhi[:, G4 + g, 0:SEQ], ps[:, bank, :], ACT.Copy, scale=pool_scale[:, g:g + 1])
                    act.activation(xhi[:, G4 + g, SEQ:TOK], ps[:, bank + 1, 0:NS], ACT.Copy, scale=pool_scale[:, g:g + 1]).then_inc(sig("b_hi"), 1)

            for t in range(TILES + 2):
                if t == TILES:
                    pooled_hi()
                if t < TILES:
                    m = rows(t)
                    if t == LASTT:
                        for q in range(4):
                            make_hi(("wout0", q))
                    wait_product(act, "uv", t, "wuv")
                    if t >= 2:
                        act.wait_ge(sig("a_tr"), t - 1)
                    else:
                        act.wait_ge(sig("ws_copied"), past("ws_copied") + 1)
                    act.activation(uv[t % 2][0:m, :], pair_flat(t % 2)[0:m, :], ACT.Gelu_apprx_tanh).then_inc(sig("uv_gelu"), 1)
                if t >= 2:
                    tt, m = t - 2, rows(t - 2)
                    act.wait_ge(sig("a_tr"), tt + 1)
                    act.activation(xhi[:, 0:G4, cols(tt)], ps[:, 6 + tt % 2, :].rearrange("p (g n) -> p g n", g=G4)[:, :, 0:m],
                                   ACT.Copy).then_inc(sig("a_hi"), 1)
            act.wait_ge(sig("z_back"), 1)
            act.activation(z_tail, ps[0:HIST, 4, :], ACT.Copy).then_inc(sig("z_back_copied"), 1)
            act.wait_ge(sig("z_back"), 2)
            act.activation(z_new, ps[0:NS, 5, :], ACT.Copy).then_inc(sig("z_back_copied"), 1)
            act.wait_ge(sig("z_back_copied"), 2)
            act.dma_start(o_pool_p[0, 0], z_tail).then_inc(sig("tails_stored"), 16)
            for b in range(NB):
                act.dma_start(o_pool_s[0, b, HIST - TS:HIST, :], z_new[b * TS:(b + 1) * TS, :]).then_inc(sig("tails_stored"), 16)

            def out_columns(tag, next_units):
                for t in range(TILES):
                    if t == LASTT - 1:
                        for key in next_units[0:3]:
                            make_hi(key)
                    if t == LASTT:
                        make_hi(next_units[3])
                    columns_hi(tag, t, rows(t))

            def key_copy(l, n):
                dst = KT[0] if n == 0 else KT[n % 2]
                if n == 0:
                    act.wait_ge(sig(f"kt{l}_tr"), past(f"kt{l}_tr") + 1)
                else:
                    act.wait_ge(sig(f"kt{l}_tr"), past(f"kt{l}_tr") + n + 1)
                    if n >= 3:
                        act.wait_ge(sig(f"sscore{l}_mm"), past(f"sscore{l}_mm") + n - 2)
                    elif n == 2:
                        act.wait_ge(sig(f"score{l}_mm"), past(f"score{l}_mm") + LASTT)
                act.activation(dst[:, :, 0:P], pair_chunks(C_), ACT.Copy).then_inc(sig(f"kt{l}_a"), 1)

            def attention(l):
                act.wait_ge(sig("tails_stored"), 16 * (1 + NB + l * (3 + NB)))
                for u in range(4):
                    if u == 3:
                        key_copy(l, 0)
                    for o in range(2):
                        j = 2 * u + o
                        wait_column(act, f"q{l}", f"wq{l}", u, o)
                        act.activation(qT[:, j, :].rearrange("p (b n) -> p b n", b=2), PAIR[o][:, :, 0:MOVE], ACT.Copy).then_inc(sig(f"q{l}_copied"), 1)

                def exponents(t, m):
                    act.wait_ge(sig(f"prob{l}_max"), past(f"prob{l}_max") + t + 1)
                    if t:
                        act.wait_ge(sig(f"prob{l}_tr"), past(f"prob{l}_tr") + t)
                    pair = pair_flat(t % 2)
                    for hh in range(HEADS):
                        e = act.activation(prob[0:m, hh * NMEM:(hh + 1) * NMEM], pair[0:m, hh * NMEM:(hh + 1) * NMEM], ACT.Exp,
                                           bias=smax[0:m, t, hh:hh + 1], scale=QSCALE, accum_out=ssum[0:m, t, hh:hh + 1])
                    e.then_inc(sig(f"prob{l}_exp"), 1)

                exponents(0, P)
                for t in range(LASTT):
                    act.wait_ge(sig(f"prob{l}_tr"), past(f"prob{l}_tr") + t + 1)
                    if t:
                        act.wait_ge(sig(f"att{l}_mm"), past(f"att{l}_mm") + t)
                    act.activation(probT, pair_chunks(C_), ACT.Copy).then_inc(sig(f"pt{l}_copied"), 1)
                    if t + 1 < LASTT:
                        exponents(t + 1, P)
                    if t < LASTT - 1:
                        act.wait_ge(sig(f"att{l}_mm"), past(f"att{l}_mm") + t + 1)
                    else:
                        act.wait_ge(sig("plain_used"), PLAIN[("v", l)] + 1)
                    act.activation(xhi[:, :, cols(t)], pair_chunks(D_), ACT.Copy).then_inc(sig(f"att{l}_hi"), 1)
                for b in range(NB):
                    key_copy(l, b + 1)
                    if b >= 4:
                        make_hi((f"wo{l}", b - 4))
                exponents(LASTT, NS)
                act.wait_ge(sig(f"os{l}_tr"), past(f"os{l}_tr") + 1)
                act.activation(xhi[:, :, cols(LASTT)], pair_chunks(C_)[:, :, 0:NS], ACT.Copy).then_inc(sig(f"att{l}_hi"), 1)

            def make_hi_moe(l, k, i):
                r, s = MOE_RAW[l] + k, MOE_SPL[l] + k
                act.wait_ge(sig(f"raw_landed{r % RING}"), LANDED[r] + 48 * i)
                act.wait_ge(sig("split_used"), s - RING + 1 + 12 * i)
                act.activation(whi[s % RING][:, :], raw[r % RING][:, :], ACT.Copy).then_inc(sig("hi_made"), 1)

            def router(l):
                act.wait_ge(sig(f"lg{l}_mm"), past(f"lg{l}_mm") + 1)
                act.wait_ge(sig(f"lg{l}_zeroed"), past(f"lg{l}_zeroed") + 1)
                act.activation(logitT[:, 0:TOK].rearrange("p (b n) -> p b n", b=2), ps[0:ROUTE, 0:2, 0:MOVE], ACT.Identity,
                               bias=rbias[:, :]).then_inc(sig(f"lg{l}_copied"), 1)
                act.wait_ge(sig(f"group{l}_shift"), past(f"group{l}_shift") + 1)
                act.activation(group_exp, picked[:, :, :], ACT.Exp).then_inc(sig(f"group{l}_exp"), 1)
                act.wait_ge(sig(f"expert{l}_shift"), past(f"expert{l}_shift") + 1)
                act.activation(rt[:, 5, :], rt[:, 4, :], ACT.Exp).then_inc(sig(f"expert{l}_exp"), 1)
                act.wait_ge(sig(f"h_stored"), 32 * (l + 1))
                act.wait_ge(sig(f"o{l}_tr"), past(f"o{l}_tr") + TILES)
                for t in range(TILES):
                    act.activation(h[0:rows(t), t, :], h[0:rows(t), t, :], ACT.Copy, scale=ALPHA).then_inc(sig(f"scaled{l}"), 1)

            def experts(l):
                def gathered_hi(c, i):
                    n = c + 2 * i
                    act.wait_ge(sig(f"xg{l}_tr"), past(f"xg{l}_tr") + n + 1)
                    act.activation(xgT_hi, pair_chunks(C_), ACT.Copy).then_inc(sig(f"xg{l}_hi"), 1)

                def step(c, i):
                    n, k = c + 2 * i, first_unit(c)
                    if c < EXPERTS:
                        own, nxt = ahead(c)
                        for kk in own:
                            make_hi_moe(l, kk, i)
                        act.wait_ge(sig("split_used"), unit_value(MOE_SPL[l], k + 1, i))
                        if c:
                            act.wait_ge(sig(f"hid{l}"), past(f"hid{l}") + n)
                        act.activation(silu, ps[:, 0, :], ACT.Silu).then_inc(sig(f"silu{l}"), 1)
                        for kk in nxt[0:2]:
                            make_hi_moe(l, kk, i)
                        if c < EXPERTS - 1:
                            gathered_hi(c + 1, i)
                        for kk in nxt[2:]:
                            make_hi_moe(l, kk, i)
                    if c:
                        down = k + 5 if c < EXPERTS else k + 1
                        par = (c - 1) % 2
                        act.wait_ge(sig("split_used"), unit_value(MOE_SPL[l], down, i))
                        if c > 2:
                            act.wait_ge(sig(f"y{par}_stored"), 16 * (l * EXPERTS // 2 + (c - 1) // 2) + 16 * i)
                        elif l:
                            act.wait_ge(sig(f"y{par}_stored"), 16 * l * EXPERTS // 2)
                        act.activation(ye[par], pair_flat(B_), ACT.Copy).then_inc(sig(f"ye{l}"), 1)
                    if c < EXPERTS:
                        act.wait_ge(sig(f"hid{l}_tr"), past(f"hid{l}_tr") + n + 1)
                        act.activation(hidT_hi, ps[:, 6, :].rearrange("p (k n) -> p k n", k=4), ACT.Copy).then_inc(sig(f"hid{l}_hi"), 1)
                    if c:
                        act.wait_ge(sig(f"ye{l}"), past(f"ye{l}") + n)
                        e = n - 1
                        dst = y_dram[bass.ds(e * SLOTS, P), :] if not isinstance(e, int) else y_dram[e * SLOTS:e * SLOTS + P, :]
                        act.dma_start(dst, ye[par]).then_inc(sig(f"y{par}_stored"), 16)

                gathered_hi(0, 0)
                step(0, 0)
                for c in range(1, 3):
                    step(c, 0)
                with act.Fori(0, EXPERTS // 2 - 3) as i:
                    step(3, i)
                    step(4, i)
                for c in range(EXPERTS - 3, EXPERTS):
                    step(c, 0)
                step(EXPERTS, 0)

            def further(l):
                act.wait_ge(sig(f"hid{l}"), past(f"hid{l}") + EXPERTS)
                n = further_blocks(act, l)
                def one_block(i):
                    act.wait_ge(again(l, "used"), 3 + 6 * i)
                    act.activation(silu, ps[:, 0, :], ACT.Silu).then_inc(again(l, "silu"), 1)
                    act.wait_ge(again(l, "used"), 7 + 6 * i)
                    act.activation(y_hi, pair_flat(B_).rearrange("p (k n) -> p k n", k=4), ACT.Copy).then_inc(again(l, "y_hi"), 1)

                with act.If(n > 0):
                    one_block(0)
                with act.If(n > 1):
                    with act.Fori(1, FURTHER) as i:
                        with act.If(n > i):
                            one_block(i)

            def conv_small():
                for par in range(2):
                    act.wait_ge(sig(f"y{par}_stored"), 16 * EXPERTS // 2)
                act.wait_ge(sig("moe0_combined"), past("moe0_combined") + TILES)
                small = sig("small_landed1")
                act.dma_start(c_rows, a["state_conv_c"][0].rearrange("(j b) i n -> (b i) j n", j=2)).then_inc(small, 16)
                act.dma_start(d_rows, a["state_conv_d"][0].rearrange("b i n -> (b i) n")).then_inc(small, 16)
                at = 0
                for w in (a["conv_c_w"][0], a["conv_d_w"][0], a["conv_c_b"], a["ln_c_g"], a["ln_c_b"]):
                    act.dma_start(tap_rows[at:at + w.shape[0], :], w).then_inc(small, 16)
                    at += w.shape[0]

            def conv_layer():
                for g in range(G4):
                    wait_column(act, "glu", "wglu", g, 1)
                    if g >= 2:
                        act.wait_ge(sig("glu"), g - 1)
                    else:
                        act.wait_ge(sig("moe0_combined"), past("moe0_combined") + TILES)
                    act.activation(gate_tmp[g % 2].rearrange("p (b n) -> p b n", b=2), PAIR[2 * (g % 2) + 1][:, :, 0:MOVE], ACT.Sigmoid).then_inc(sig("glu_gate"), 1)
                    make_hi(("wcx", g))
                for g in range(G4):
                    act.wait_ge(sig("cx_mm"), g + 1)
                    if g >= 2:
                        act.wait_ge(sig("cx"), g - 1)
                    else:
                        act.wait_ge(sig("glu"), G4 - 1 + g)
                    act.activation(gate_tmp[g % 2].rearrange("p (b n) -> p b n", b=2), PAIR[2 * (g % 2)][:, :, 0:MOVE], ACT.Copy).then_inc(sig("cx_gate"), 1)
                    make_hi(("wgb", g) if g < 2 else ("wout1", g - 2))
                for q in range(2):
                    make_hi(("wout1", 2 + q))
                act.wait_ge(sig("d_out"), 4)
                act.activation(xhi[:, G4:KC, :], cd, ACT.Copy).then_inc(sig("d_hi"), 1)
                act.wait_ge(sig("conv"), G4 - 1)
                for n, (m, _) in enumerate(TAIL_SOURCES):
                    act.wait_ge(sig("tails_tr"), n + 1)
                    act.activation(tails[n][0:m, :], ps[0:m, n, :], ACT.Copy).then_inc(sig("tails_copied"), 1)
                act.wait_ge(sig("tails_copied"), 4)
                act.dma_start(o_cc_p[0, 0], tails[0][0:HC, :]).then_inc(sig("tails_stored"), 16)
                act.dma_start(o_cd_p[0, 0], tails[2][0:HDD, :]).then_inc(sig("tails_stored"), 16)
                act.dma_start(o_cd_s[0].rearrange("b i n -> (b i) n"), tails[3][0:NB * HDD, :]).then_inc(sig("tails_stored"), 16)
                for b in range(NB):
                    act.dma_start(o_cc_s[0, b, HC - TS:HC, :], tails[1][b * TS:(b + 1) * TS, :]).then_inc(sig("tails_stored"), 16)
                for t in range(TILES):
                    m = rows(t)
                    act.wait_ge(sig("c_tr"), t + 1)
                    for g in range(G4):
                        e = act.activation(acc[:, g, cols(t)], ps[:, 6 + t % 2, g * P:g * P + m], ACT.Silu,
                                           scale=ccol[:, g, CROWS - 2:CROWS - 1], bias=ccol[:, g, CROWS - 1:CROWS])
                    e.then_inc(sig("c_silu"), 1)
                    act.wait_ge(sig("c_silu"), t + 1)
                    act.activation(xhi[:, 0:G4, cols(t)], acc[:, :, cols(t)], ACT.Copy).then_inc(sig("c_hi"), 1)

            for l in range(DEPTH):
                if l:
                    conv_layer()
                out_columns(f"out{l}", [(f"wq{l}", q) for q in range(4)])
                attention(l)
                for t in range(TILES):
                    if t == LASTT - 1:
                        act.wait_ge(sig("wr_landed"), 64 * (l + 1))
                        act.activation(wrhi[:, :, :], wr_rows, ACT.Copy).then_inc(sig(f"wr{l}_hi"), 1)
                        for k in range(3):
                            make_hi_moe(l, k, 0)
                    columns_hi(f"o{l}", t, rows(t))
                router(l)
                experts(l)
                further(l)
                if l == DEPTH - 1:
                    return
                for g in range(G4):
                    make_hi(("wglu", g))
                for t in range(TILES):
                    if t == LASTT:
                        conv_small()
                    columns_hi(f"moe{l}", t, rows(t))

        @block.vector
        def _(dve):
            link = chained(dve, "dve_chain")

            def make_lo(key):
                i, s = RAW[key], SPL[key]
                dve.wait_ge(sig("hi_made"), s + 1)
                dve.tensor_tensor(wlo[s % RING][:, :], raw[i % RING][:, :], whi[s % RING][:, :].bitcast(F32), ALU.subtract).then_inc(sig("lo_made"), 1)

            def lo_of(out, full, hi):
                return dve.tensor_tensor(out, full, hi.bitcast(F32), ALU.subtract)

            def columns_lo(tag, t, m):
                dve.wait_ge(sig(tag + "_hi"), past(tag + "_hi") + t + 1)
                lo_of(xlo[:, :, t * P:t * P + m], pair_chunks(C_ + t % 2)[:, :, 0:m], xhi[:, :, t * P:t * P + m]).then_inc(sig(tag + "_lo"), 1)

            def statistics(tag, t, m, pieces):
                for n, piece in enumerate(pieces):
                    ins = dve.bn_stats(bn[0:m, n, :], piece)
                link(ins)
                dve.bn_aggr(mv[0:m, t, :], bn[0:m, 0:len(pieces), :].rearrange("p a n -> p (a n)")).then_inc(sig(tag + "_mv"), 1)

            def normalise(tag, t, m, out, src, gain, load_key):
                dve.wait_ge(sig(tag + "_rstd"), past(tag + "_rstd") + t + 1)
                link(dve.tensor_scalar(out, src, mv[0:m, t, 0:1], rstd[0:m, t:t + 1], ALU.subtract, ALU.mult))
                if t == 0:
                    dve.wait_ge(sig("gb_landed"), GB_LOADS[load_key])
                dve.tensor_tensor(out, out, gain, ALU.mult).then_inc(sig(tag + "_gain"), 1)

            for m in range(MT):
                columns_lo("mem", m, P)
            for q in range(4):
                make_lo(("wk0", q))
            for q in range(4):
                make_lo(("wv0", q))
            dve.wait_ge(sig("ws_tr"), 1)
            dve.tensor_copy(wsT, ps[:, 4, :].rearrange("p (g n) -> p g n", g=G4)).then_inc(sig("ws_copied"), 1)
            dve.wait_ge(sig("hist_tr"), 1)
            for g in range(G4):
                ins = dve.tensor_copy(zT[:, g, ZW:ZL].rearrange("p (b s) -> p b s", b=NB)[:, :, 0:HIST],
                                      ps[:, 5, g * P:g * P + NB * HIST].rearrange("p (b s) -> p b s", b=NB))
            ins.then_inc(sig("hist_copied"), 1)
            dve.memset(zT[:, :, 0:HIST], 0.0).then_inc(sig("hist_zeroed"), 1)
            for name in ("wk1", "wv1"):
                for q in range(4):
                    make_lo((name, q))
            for u in range(2):
                make_lo(("wz", u))

            for t in range(TILES):
                columns_lo("x", t, rows(t))
            for u in range(4):
                make_lo(("wuv", u))

            def pool_group(g):
                cur = zT[:, g, :]
                for lev in range(g + 1):
                    d, new = 2 ** lev, zsum[lev % 2]
                    first = 2 ** (lev + 1) - 1
                    link(dve.tensor_tensor(new[:, first:ZL], cur[:, first:ZL], cur[:, first - d:ZL - d], ALU.add))
                    cur = new
                w = 2 ** (g + 1)
                z_s = zT[:, g, ZW:ZL].rearrange("p (b s) -> p b s", b=NB)[:, :, HIST:]
                s_s = cur[:, ZW:ZL].rearrange("p (b s) -> p b s", b=NB)[:, :, HIST:]
                dve.scalar_tensor_tensor(pz[:, g, w - 1:SEQ], cur[:, HIST + w - 1:ZW], 1.0 / w, zT[:, g, HIST + w - 1:ZW], ALU.mult, ALU.subtract)
                dve.scalar_tensor_tensor(pz[:, g, SEQ:TOK].rearrange("p (b s) -> p b s", b=NB), s_s, 1.0 / w, z_s, ALU.mult, ALU.subtract)
                link(dve.tensor_tensor(pz[:, g, 0:w - 1], cur[:, HIST:HIST + w - 1], inv_count[:, 0:w - 1], ALU.mult))
                dve.tensor_tensor(pz[:, g, 0:w - 1], pz[:, g, 0:w - 1], zT[:, g, HIST:HIST + w - 1], ALU.subtract).then_inc(sig("pooled"), 1)

            def pooled_lo():
                for g in range(G4):
                    bank = 2 * ((g + 1) % 2)
                    dve.wait_ge(sig("b_hi"), g + 1)
                    dve.scalar_tensor_tensor(xlo[:, G4 + g, 0:SEQ], ps[:, bank, :], pool_scale[:, g:g + 1],
                                             xhi[:, G4 + g, 0:SEQ].bitcast(F32), ALU.mult, ALU.subtract)
                    dve.scalar_tensor_tensor(xlo[:, G4 + g, SEQ:TOK], ps[:, bank + 1, 0:NS], pool_scale[:, g:g + 1],
                                             xhi[:, G4 + g, SEQ:TOK].bitcast(F32), ALU.mult, ALU.subtract).then_inc(sig("b_lo"), 1)

            dve.wait_ge(sig("consts"), 9)
            link(dve.reciprocal(inv_count[:, :], inv_count[:, :]))
            for t in range(TILES + 1):
                if t < TILES:
                    m = rows(t)
                    v = uv[t % 2][0:m, 512:1024]
                    dve.wait_ge(sig("uv_gelu"), t + 1)
                    statistics("v", t, m, [v])
                    if t < LASTT:
                        if t == 0:
                            dve.wait_ge(sig("z_copied"), 4)
                            dve.wait_ge(sig("kv_stored0"), 16 * 2 * DEPTH)
                            dve.wait_ge(sig("kv_stored1"), 16 * 2 * DEPTH)
                        pool_group(t)
                    normalise("v", t, m, v, v, gb[0:m, 0, 0:512], "lnv")
                    if t == LASTT:
                        pooled_lo()
                if t >= 1:
                    tt, m = t - 1, rows(t - 1)
                    dve.wait_ge(sig("mixed"), tt + 1)
                    dve.wait_ge(sig("small_landed0"), 16 * N_SMALL[0])
                    bias = b_rows if tt < LASTT else b_rows_s
                    for g in range(G4):
                        u = uv[tt % 2][0:m, g * P:(g + 1) * P]
                        ins = dve.scalar_tensor_tensor(u, ps[0:m, 4 + tt % 2, g * P:(g + 1) * P], bias[0:m, g:g + 1], u, ALU.add, ALU.mult)
                    ins.then_inc(sig("gated"), 1)
                    dve.wait_ge(sig("a_hi"), tt + 1)
                    lo_of(xlo[:, 0:G4, cols(tt)], ps[:, 6 + tt % 2, :].rearrange("p (g n) -> p g n", g=G4)[:, :, 0:m],
                          xhi[:, 0:G4, cols(tt)]).then_inc(sig("a_lo"), 1)
                if t == LASTT:
                    for q in range(2):
                        make_lo(("wout0", q))
            for q in range(2, 4):
                make_lo(("wout0", q))

            def residual_norm(tag, t, psum_ready):
                m = rows(t)
                psum_ready()
                hv = h[0:m, t, :]
                ins = dve.scalar_tensor_tensor(hv, hv, ALPHA, pair_flat((t + odd(tag)) % 2)[0:m, :], ALU.mult, ALU.add)
                ins.then_inc(sig(tag + "_res"), 1)
                dve.wait_ge(sig(tag + "_res"), past(tag + "_res") + t + 1)
                statistics(tag, t, m, [h[0:m, t, 0:512], h[0:m, t, 512:1024]])
                normalise(tag, t, m, hv, hv, gb[0:m, 0, :], tag)

            def out_norm(tag, name, next_lo, last_lo):
                for t in range(TILES):
                    if tag == "out1" and t == 1:
                        conv_lo(LASTT)
                    if t == LASTT:
                        next_lo()
                    residual_norm(tag, t, lambda: wait_product(dve, tag, t, name))
                    if t >= 1:
                        columns_lo(tag, t - 1, rows(t - 1))
                last_lo()
                columns_lo(tag, LASTT, NS)

            def key_copy(l, n):
                key = ("k", l) if n == 0 else ("ks", l, n - 1)
                dst = KT[n % 2]
                dve.wait_ge(sig("plain_used"), PLAIN[key] + 1)
                if n >= 3:
                    dve.wait_ge(sig(f"sscore{l}_mm"), past(f"sscore{l}_mm") + n - 2)
                elif n == 2:
                    dve.wait_ge(sig(f"score{l}_mm"), past(f"score{l}_mm") + LASTT)
                dve.tensor_copy(dst[:, :, P:2 * P], pair_chunks(D_)).then_inc(sig(f"kt{l}_b"), 1)

            def attention(l):
                dve.wait_ge(sig(f"out{l}_row"), past(f"out{l}_row") + TILES)
                link(dve.memset(gb[:, :, :], 0.0))
                key_copy(l, 0)
                dve.wait_ge(sig(f"q{l}_copied"), past(f"q{l}_copied") + KC)
                for b in range(NB):
                    ins = dve.tensor_copy(q_only[:, :, b, b * TS:(b + 1) * TS], qT[:, :, SEQ + b * TS:SEQ + (b + 1) * TS])
                ins.then_inc(sig(f"q{l}_only"), 1)

                def maxima(t, m):
                    if t < LASTT:
                        dve.wait_ge(sig(f"score{l}_mm"), past(f"score{l}_mm") + t + 1)
                    else:
                        dve.wait_ge(sig(f"sscore{l}_mm"), past(f"sscore{l}_mm") + NB)
                    link(dve.tensor_reduce(smax[0:m, t, :], pair_flat(t % 2)[0:m, :].rearrange("p (h n) -> p h n", h=HEADS), AX, ALU.max))
                    dve.tensor_scalar(smax[0:m, t, :], smax[0:m, t, :], -QSCALE, None, ALU.mult).then_inc(sig(f"prob{l}_max"), 1)

                def normal(t, m):
                    dve.wait_ge(sig(f"prob{l}_exp"), past(f"prob{l}_exp") + t + 1)
                    link(dve.reciprocal(ssum[0:m, t, :], ssum[0:m, t, :]))
                    for hh in range(HEADS):
                        v = prob[0:m, hh * NMEM:(hh + 1) * NMEM]
                        ins = dve.tensor_scalar(v, v, ssum[0:m, t, hh:hh + 1], None, ALU.mult)
                    ins.then_inc(sig(f"prob{l}_norm"), 1)

                maxima(0, P)
                maxima(1, P)
                normal(0, P)
                for t in range(LASTT):
                    if t + 2 < LASTT:
                        maxima(t + 2, P)
                    if t + 1 < LASTT:
                        normal(t + 1, P)
                    dve.wait_ge(sig(f"att{l}_hi"), past(f"att{l}_hi") + t + 1)
                    lo_of(xlo[:, :, cols(t)], pair_chunks(D_), xhi[:, :, cols(t)]).then_inc(sig(f"att{l}_lo"), 1)
                dve.wait_ge(sig(f"score{l}_mm"), past(f"score{l}_mm") + LASTT)
                dve.wait_ge(sig(f"q{l}_only"), past(f"q{l}_only") + 1)
                link(dve.memset(p_only, 0.0))
                for b in range(NB):
                    key_copy(l, b + 1)
                    if b >= 4:
                        make_lo((f"wo{l}", b - 4))
                maxima(LASTT, NS)
                normal(LASTT, NS)
                dve.wait_ge(sig(f"prob{l}_tr"), past(f"prob{l}_tr") + LASTT + 1)
                for b in range(NB):
                    ins = dve.tensor_copy(p_only[:, :, b, b * TS:(b + 1) * TS], pair_chunks(C_)[:, :, b * TS:(b + 1) * TS])
                ins.then_inc(sig(f"prob{l}_only"), 1)
                dve.wait_ge(sig("plain_used"), PLAIN[("vs", l, NB - 1)] + 1)
                dve.tensor_copy(prob[0:NS, :], pair_flat(A_)[0:NS, :]).then_inc(sig(f"os{l}_copied"), 1)
                dve.wait_ge(sig(f"att{l}_hi"), past(f"att{l}_hi") + TILES)
                lo_of(xlo[:, :, cols(LASTT)], pair_chunks(C_)[:, :, 0:NS], xhi[:, :, cols(LASTT)]).then_inc(sig(f"att{l}_lo"), 1)

            def make_lo_moe(l, k, i):
                r, s = MOE_RAW[l] + k, MOE_SPL[l] + k
                dve.wait_ge(sig("hi_made"), s + 1 + 12 * i)
                dve.tensor_tensor(wlo[s % RING][:, :], raw[r % RING][:, :], whi[s % RING][:, :].bitcast(F32), ALU.subtract).then_inc(sig("lo_made"), 1)

            def first_of_ties(marks, top):
                link(dve.tensor_tensor(marks, marks, falling[:, :].unsqueeze(1).to_broadcast([P, TILES, 4]), ALU.mult))
                link(dve.tensor_reduce(top, marks, AX, ALU.max))
                link(dve.tensor_tensor(marks, marks, top.unsqueeze(2).to_broadcast([P, TILES, 4]), ALU.is_equal))

            def router(l):
                dve.wait_ge(sig(f"lg{l}_tr"), past(f"lg{l}_tr") + 1)
                link(dve.tensor_copy(lgt[:, :, :], ps[:, 2, 0:32 * TILES].rearrange("p (t n) -> p t n", t=TILES)[:, :, 0:ROUTE]))
                full, square = [P, TILES, 4], [P, TILES, GROUPS, PER]

                def per_token(n):
                    return rt[:, n, :].unsqueeze(2)

                G, og = lgt[:, :, 0:GROUPS], chosen[:, :, 0, :]
                link(dve.tensor_reduce(rt[:, 0, :], G, AX, ALU.max))
                link(dve.tensor_tensor(picked[:, :, :], G, per_token(0).to_broadcast(full), ALU.subtract))
                dve.tensor_scalar(og, picked[:, :, :], 0.0, None, ALU.is_equal).then_inc(sig(f"group{l}_shift"), 1)
                dve.wait_ge(sig(f"group{l}_shift"), past(f"group{l}_shift") + 1)
                first_of_ties(og, rt[:, 6, :])
                by_group = both[:, 0, :, :].rearrange("p t (g k) -> p t g k", g=GROUPS)
                in_group = og.unsqueeze(3).to_broadcast(square)
                link(dve.tensor_tensor(by_group, lgt[:, :, GROUPS:ROUTE].rearrange("p t (g k) -> p t g k", g=GROUPS), in_group, ALU.mult))
                dve.wait_ge(sig(f"group{l}_exp"), past(f"group{l}_exp") + 1)
                link(dve.tensor_reduce(picked[:, :, :], by_group.rearrange("p t g k -> p t k g"), AX, ALU.add))
                link(dve.tensor_reduce(rt[:, 2, :], picked[:, :, :], AX, ALU.max))
                link(dve.tensor_tensor(chosen[:, :, 1, :], picked[:, :, :], per_token(2).to_broadcast(full), ALU.is_equal))
                first_of_ties(chosen[:, :, 1, :], rt[:, 6, :])
                link(dve.scalar_tensor_tensor(picked[:, :, :], chosen[:, :, 1, :], -3.0e38, picked[:, :, :], ALU.mult, ALU.add))
                link(dve.tensor_reduce(rt[:, 3, :], picked[:, :, :], AX, ALU.max))
                link(dve.tensor_tensor(chosen[:, :, 2, :], picked[:, :, :], per_token(3).to_broadcast(full), ALU.is_equal))
                first_of_ties(chosen[:, :, 2, :], rt[:, 6, :])
                link(dve.tensor_tensor(og, og, valid[:, :].unsqueeze(2).to_broadcast(full), ALU.mult))
                for j in range(2):
                    ins = dve.tensor_tensor(both[:, j, :, :].rearrange("p t (g k) -> p t g k", g=GROUPS),
                                            chosen[:, :, 1 + j, :].unsqueeze(2).to_broadcast(square), in_group, ALU.mult)
                link(ins)
                dve.tensor_tensor(member[:, :, :], both[:, 0, :, :], both[:, 1, :, :], ALU.add).then_inc(sig(f"member{l}"), 1)
                dve.tensor_tensor(rt[:, 4, :], rt[:, 3, :], rt[:, 2, :], ALU.subtract).then_inc(sig(f"expert{l}_shift"), 1)
                dve.wait_ge(sig(f"rank{l}_mm"), past(f"rank{l}_mm") + 1)
                dve.wait_ge(sig(f"member{l}"), past(f"member{l}") + 1)
                link(dve.scalar_tensor_tensor(rank[:, :, :], ps[:, 3, 0:TILES * EXPERTS].rearrange("p (t e) -> p t e", t=TILES), 1.0,
                                              member[:, :, :], ALU.add, ALU.mult))
                dve.tensor_scalar(rank[:, :, :], rank[:, :, :], -1.0, None, ALU.add).then_inc(sig(f"ranked{l}"), 1)

            def weights_and_slots(l):
                dve.wait_ge(sig(f"group{l}_exp"), past(f"group{l}_exp") + 1)
                dve.wait_ge(sig(f"expert{l}_exp"), past(f"expert{l}_exp") + 1)
                link(dve.tensor_reduce(rt[:, 1, :], group_exp, AX, ALU.add))
                dve.reciprocal(rt[:, 1, :], rt[:, 1, :])
                link(dve.tensor_scalar(rt[:, 6, :], rt[:, 5, :], 1.0, None, ALU.add))
                link(dve.reciprocal(rt[:, 6, :], rt[:, 6, :]))
                link(dve.tensor_tensor(rw[:, :, 0], rt[:, 6, :], rt[:, 1, :], ALU.mult))
                link(dve.tensor_tensor(rw[:, :, 1], rt[:, 5, :], rw[:, :, 0], ALU.mult))
                by_expert = [P, TILES, EXPERTS]
                dve.tensor_tensor(gates, both[:, 0, :, :], rw[:, :, 0:1].to_broadcast(by_expert), ALU.mult)
                link(dve.tensor_tensor(kept, both[:, 1, :, :], rw[:, :, 1:2].to_broadcast(by_expert), ALU.mult))
                link(dve.tensor_tensor(gates, gates, kept, ALU.add))
                dve.tensor_scalar(kept, rank[:, :, :], SLOTS - 0.5, None, ALU.is_lt)
                link(dve.tensor_tensor(slot_value, rank[:, :, :], slot0[:, :].unsqueeze(1).to_broadcast(by_expert), ALU.add))
                for j in range(2):
                    link(dve.tensor_tensor(both[:, j, :, :], both[:, j, :, :], kept, ALU.mult))
                    link(dve.tensor_reduce(rt[:, 6, :], both[:, j, :, :], AX, ALU.add))
                    link(dve.tensor_tensor(rw[:, :, j], rw[:, :, j], rt[:, 6, :], ALU.mult))
                    link(dve.tensor_tensor(both[:, j, :, :], both[:, j, :, :], slot_value, ALU.mult))
                    link(dve.tensor_reduce(slot_f[:, :, j], both[:, j, :, :], AX, ALU.add))
                dve.tensor_copy(slot_of[:, :, :], slot_f[:, :, :]).then_inc(sig(f"slots{l}"), 1)

            def experts(l):
                def hits(c, i):
                    n = c + 2 * i
                    if c >= 2:
                        dve.wait_ge(sig(f"tok{l}_mm"), past(f"tok{l}_mm") + n - 1)
                    r = rank[:, :, n:n + 1] if isinstance(n, int) else rank[:, :, bass.ds(n, 1)]
                    dve.tensor_tensor(hit[c % 2], iota[:, :].unsqueeze(1).to_broadcast([P, TILES, P]), r.to_broadcast([P, TILES, P]),
                                      ALU.is_equal).then_inc(sig(f"hit{l}"), 1)

                def tokens(c, i):
                    n = c + 2 * i
                    dve.wait_ge(sig(f"tok{l}_mm"), past(f"tok{l}_mm") + n + 1)
                    if c >= 2:
                        dve.wait_ge(sig(f"gathered{c % 2}"), 16 * (l * EXPERTS // 2 + c // 2) + 16 * i)
                    with nc.allow_low_precision(reason="whole numbers below 1024"):
                        dve.tensor_reduce(tok_of[c % 2][:, :], ps[:, 7, 0:2], AX, ALU.add).then_inc(sig(f"tok{l}"), 1)

                def gathered_lo(c, i):
                    n = c + 2 * i
                    dve.wait_ge(sig(f"xg{l}_hi"), past(f"xg{l}_hi") + n + 1)
                    lo_of(xgT_lo, pair_chunks(C_), xgT_hi).then_inc(sig(f"xg{l}_lo"), 1)

                def step(c, i):
                    n, k = c + 2 * i, first_unit(c)
                    own, nxt = ahead(c)
                    if c and c < EXPERTS - 1:
                        tokens(c + 1, i)
                    make_lo_moe(l, own[0], i)
                    if c < EXPERTS - 2:
                        hits(c + 2, i)
                    for kk in own[1:] + nxt[0:2]:
                        make_lo_moe(l, kk, i)
                    dve.wait_ge(sig("split_used"), unit_value(MOE_SPL[l], k + 3, i))
                    dve.wait_ge(sig(f"silu{l}"), past(f"silu{l}") + n + 1)
                    if c:
                        dve.wait_ge(sig(f"hid{l}_tr"), past(f"hid{l}_tr") + n)
                    dve.tensor_tensor(hid, silu, ps[:, 1, :], ALU.mult).then_inc(sig(f"hid{l}"), 1)
                    if c < EXPERTS - 1:
                        gathered_lo(c + 1, i)
                    for kk in nxt[2:]:
                        make_lo_moe(l, kk, i)
                    dve.wait_ge(sig(f"hid{l}_hi"), past(f"hid{l}_hi") + n + 1)
                    lo_of(hidT_lo, ps[:, 6, :].rearrange("p (k n) -> p k n", k=4), hidT_hi).then_inc(sig(f"hid{l}_lo"), 1)

                dve.wait_ge(sig(f"ranked{l}"), past(f"ranked{l}") + 1)
                hits(0, 0)
                hits(1, 0)
                tokens(0, 0)
                tokens(1, 0)
                weights_and_slots(l)
                gathered_lo(0, 0)
                step(0, 0)
                list_blocks(l)
                for c in range(1, 3):
                    step(c, 0)
                with dve.Fori(0, EXPERTS // 2 - 3) as i:
                    step(3, i)
                    step(4, i)
                for c in range(EXPERTS - 3, EXPERTS):
                    step(c, 0)

            def list_blocks(l):
                count = ps[:, 3, TILES * EXPERTS:(TILES + 1) * EXPERTS]
                pad = EXPERTS // 2
                for r in range(LEVELS):
                    dve.tensor_scalar(level[:, r, :], count, SLOTS * (r + 1) + 0.5, None, ALU.is_gt)
                dve.memset(total[0][:, 0:pad], 0.0)
                link(dve.memset(total[1][:, 0:pad], 0.0))
                link(dve.tensor_reduce(total[0][:, pad:], level.rearrange("p r e -> p e r"), AX, ALU.add))
                link(dve.tensor_copy(level[:, 0, :], total[0][:, pad:]))
                for n in range(4):
                    src, dst, d = total[n % 2], total[(n + 1) % 2], 2 ** n
                    link(dve.tensor_tensor(dst[:, pad:], src[:, pad:], src[:, pad - d:pad + EXPERTS - d], ALU.add))
                upto = total[0][:, pad:]
                link(dve.tensor_tensor(level[:, 0, :], upto, level[:, 0, :], ALU.subtract))
                table = [P, FURTHER, EXPERTS]
                number = iota[:, 0:FURTHER].unsqueeze(2).to_broadcast(table)
                start = level[:, 0:1, :].to_broadcast(table)
                link(dve.tensor_tensor(nth, number, start, ALU.is_ge))
                link(dve.tensor_tensor(is_of, number, upto.unsqueeze(1).to_broadcast(table), ALU.is_lt))
                link(dve.tensor_tensor(is_of, is_of, nth, ALU.mult))
                link(dve.tensor_tensor(nth, number, start, ALU.subtract))
                link(dve.tensor_tensor(nth, nth, is_of, ALU.mult))
                link(dve.tensor_reduce(first_rank, nth, AX, ALU.add))
                link(dve.tensor_scalar(first_rank, first_rank, 1.0, float(SLOTS), ALU.add, ALU.mult))
                link(dve.tensor_tensor(nth, is_of, iota[:, 0:EXPERTS].unsqueeze(1).to_broadcast(table), ALU.mult))
                with nc.allow_low_precision(reason="whole numbers below 16"):
                    link(dve.tensor_reduce(block_expert[:, :], nth[0:1, :, :], AX, ALU.add))
                dve.tensor_copy(blocks[:, :], upto[0:1, EXPERTS - 1:EXPERTS]).then_inc(sig(f"listed{l}"), 1)

            def further(l):
                dve.wait_ge(sig(f"scaled{l}"), past(f"scaled{l}") + TILES)
                dve.tensor_copy(tok2_f, tok2[:, :, :]).then_inc(again(l, "added"), 1)
                n = further_blocks(dve, l)
                def one_block(i):
                    done = [0]

                    def step(ins):
                        done[0] += 1
                        ins.then_inc(again(l, "own"), 1)
                        dve.wait_ge(again(l, "own"), done[0] + 6 * i)
                    expert = is_of[:, bass.ds(i, 1), :].to_broadcast([P, TILES, EXPERTS])
                    step(dve.tensor_tensor(own, rank[:, :, :], expert, ALU.mult))
                    step(dve.tensor_reduce(own_rank, own, AX, ALU.add))
                    step(dve.tensor_scalar(own_rank, own_rank, first_rank[:, bass.ds(i, 1)], None, ALU.subtract))
                    step(dve.tensor_tensor(own, gates, expert, ALU.mult))
                    step(dve.tensor_reduce(own_gate, own, AX, ALU.add))
                    marks = [P, TILES, P]
                    dve.tensor_tensor(hit_f, iota[:, :].unsqueeze(1).to_broadcast(marks), own_rank.unsqueeze(2).to_broadcast(marks),
                                      ALU.is_equal).then_inc(again(l, "hit"), 1)
                    dve.wait_ge(again(l, "tok_mm"), 1 + i)
                    with nc.allow_low_precision(reason="whole numbers below 1024"):
                        dve.tensor_reduce(tok_of[0][:, :], ps[:, 7, 0:2], AX, ALU.add).then_inc(again(l, "tok"), 1)
                    dve.wait_ge(again(l, "tr"), 1 + 3 * i)
                    dve.tensor_copy(hitT[:, 0:2, :], ps[:, 4, :].rearrange("p (k n) -> p k n", k=2))
                    dve.tensor_copy(hitT[:, 2, 0:P], ps[:, 5, 0:P]).then_inc(again(l, "copied"), 1)
                    for par in range(2):
                        dve.wait_ge(sig(f"y{par}_stored"), 16 * (l + 1) * EXPERTS // 2)
                    dve.wait_ge(again(l, "tr"), 2 + 3 * i)
                    dve.tensor_copy(rowsT, pair_chunks(C_)).then_inc(again(l, "copied"), 1)
                    dve.wait_ge(again(l, "used"), 5 + 6 * i)
                    dve.wait_ge(again(l, "silu"), 1 + i)
                    dve.tensor_tensor(hid, silu, ps[:, 1, :], ALU.mult).then_inc(again(l, "hid"), 1)
                    dve.wait_ge(again(l, "tr"), 3 + 3 * i)
                    dve.tensor_copy(hidT, ps[:, 6, :].rearrange("p (k n) -> p k n", k=4)).then_inc(again(l, "copied"), 1)
                    dve.wait_ge(again(l, "y_hi"), 1 + i)
                    lo_of(y_lo, pair_flat(B_).rearrange("p (k n) -> p k n", k=4), y_hi).then_inc(again(l, "copied"), 1)
                    for t in range(TILES):
                        hv, m = h[0:rows(t), t, :], rows(t)
                        dve.wait_ge(again(l, "share_mm"), t + 1 + TILES * i)
                        dve.scalar_tensor_tensor(hv, pair_flat(t % 2)[0:m, :], own_gate[0:m, t:t + 1], hv, ALU.mult, ALU.add).then_inc(again(l, "added"), 1)
                    dve.wait_ge(again(l, "added"), 1 + TILES + TILES * i)
                    dve.tensor_copy(spare, own_rank[:, 0:1]).then_inc(again(l, "own"), 1)

                with dve.If(n > 0):
                    one_block(0)
                with dve.If(n > 1):
                    with dve.Fori(1, FURTHER) as i:
                        with dve.If(n > i):
                            one_block(i)

            def combine(l, lo_keys):
                tag = f"moe{l}"
                if lo_keys:
                    make_lo(lo_keys[0])
                for t in range(TILES + 1):
                    if t < TILES:
                        m, hv = rows(t), h[0:rows(t), t, :]
                        dve.wait_ge(sig(f"scaled{l}"), past(f"scaled{l}") + t + 1)
                        dve.wait_ge(sig(f"back_landed{t % 2}"), 32 * (l * len(range(t % 2, TILES, 2)) + t // 2 + 1))
                        link(dve.scalar_tensor_tensor(hv, back[t % 2][0][0:m, :], rw[0:m, t, 0:1], hv, ALU.mult, ALU.add))
                        dve.scalar_tensor_tensor(hv, back[t % 2][1][0:m, :], rw[0:m, t, 1:2], hv, ALU.mult, ALU.add).then_inc(sig(tag + "_combined"), 1)
                        dve.wait_ge(sig(tag + "_combined"), past(tag + "_combined") + t + 1)
                        statistics(tag, t, m, [h[0:m, t, 0:512], h[0:m, t, 512:1024]])
                    if t >= 1:
                        m, hv = rows(t - 1), h[0:rows(t - 1), t - 1, :]
                        normalise(tag, t - 1, m, hv, hv, gb[0:m, 0, :], tag)
                        if t < len(lo_keys):
                            make_lo(lo_keys[t])
                    if lo_keys and t >= 2:
                        columns_lo(tag, t - 2, rows(t - 2))
                if lo_keys:
                    columns_lo(tag, LASTT, NS)

            def conv_layer():
                dve.wait_ge(sig("hist1_tr"), 1)
                link(dve.tensor_copy(ccol[:, :, :], ps[:, 4, :].rearrange("p (g n) -> p g n", g=G4)[:, :, 0:CROWS]))
                for g in range(G4):
                    dve.tensor_copy(cxT[:, g, DW:DL].rearrange("p (b s) -> p b s", b=NB)[:, :, 0:HDD],
                                    ps[:, 5, g * P:g * P + NB * HDD].rearrange("p (b s) -> p b s", b=NB))
                    for j in range(2):
                        dve.tensor_copy(gluT[:, g, CW:CL].rearrange("p (b s) -> p b s", b=NB)[:, 4 * j:4 * j + 4, 0:HC],
                                        ps[:, 6 + j, g * P:g * P + 4 * HC].rearrange("p (b s) -> p b s", b=4))
                dve.memset(gluT[:, :, 0:HC], 0.0)
                link(dve.memset(cxT[:, :, 0:HDD], 0.0))
                dve.tensor_copy(rt[:, 7, :], rt[:, 0, :]).then_inc(sig("hist1_copied"), 1)

                def sequences(x, width, hist, start):
                    return x[:, width:].rearrange("p (b s) -> p b s", b=NB)[:, :, start:start + TS]

                TAPS = [(g, k) for g in range(1, G4) for k in range(POOL_TAPS if g == G4 - 1 else 0, TAPS_C)]
                written = {}

                def taps(first, last):
                    for g, k in TAPS[first:last]:
                        src = gluT[:, g, :]
                        p_in, p_out = src[:, k:k + SEQ], acc[:, g, 0:SEQ]
                        s_in, s_out = sequences(src, CW, HC, k), acc[:, g, SEQ:TOK].rearrange("p (b s) -> p b s", b=NB)
                        w = ccol[:, g, k:k + 1]
                        if (g, k) == TAPS[0] or (g, k - 1) not in TAPS:
                            bias = 0.0 if k else ccol[:, g, TAPS_C + TAPS_D:TAPS_C + TAPS_D + 1]
                            written["p"] = link.mark(dve.tensor_scalar(p_out, p_in, w, bias, ALU.mult, ALU.add))
                            ins = dve.tensor_scalar(s_out, s_in, w, bias, ALU.mult, ALU.add)
                        else:
                            dve.wait_ge(sig("dve_chain"), written["p"])
                            written["p"] = link.mark(dve.scalar_tensor_tensor(p_out, p_in, w, p_out, ALU.mult, ALU.add))
                            dve.wait_ge(sig("dve_chain"), written["s"])
                            ins = dve.scalar_tensor_tensor(s_out, s_in, w, s_out, ALU.mult, ALU.add)
                        if k < TAPS_C - 1:
                            written["s"] = link.mark(ins)
                        elif g < G4 - 1:
                            ins.then_inc(sig("conv"), 1)
                        else:
                            link(ins)
                            dve.wait_ge(sig("conv_pool"), 2)
                            dve.tensor_tensor(acc[:, g, :], acc[:, g, :], conv_rest, ALU.add).then_inc(sig("conv"), 1)

                def to_sequences(dst, width, hist, pair, gate, name):
                    dve.tensor_tensor(dst[:, hist:hist + MOVE], ps[:, 2 * pair, 0:MOVE], gate[:, 0:MOVE], ALU.mult)
                    dve.tensor_tensor(dst[:, hist + MOVE:width], ps[:, 2 * pair + 1, 0:PB], gate[:, MOVE:MOVE + PB], ALU.mult)
                    link(dve.tensor_tensor(sequences(dst, width, hist, hist), ps[:, 2 * pair + 1, PB:MOVE].rearrange("p (b s) -> p b s", b=NB),
                                           gate[:, MOVE + PB:].rearrange("p (b s) -> p b s", b=NB), ALU.mult))
                    dve.tensor_copy(rt[:, 7, :], rt[:, 0, :]).then_inc(sig(name), 1)

                def short_conv(g):
                    for k in range(TAPS_D):
                        src = cxT[:, g, :]
                        p_in, p_out = src[:, k:k + SEQ], cd[:, g, 0:SEQ]
                        s_in, s_out = sequences(src, DW, HDD, k), cd[:, g, SEQ:TOK].rearrange("p (b s) -> p b s", b=NB)
                        w = ccol[:, g, TAPS_C + k:TAPS_C + k + 1]
                        if k == 0:
                            dve.tensor_scalar(p_out, p_in, w, None, ALU.mult)
                            link(dve.tensor_scalar(s_out, s_in, w, None, ALU.mult))
                        else:
                            dve.scalar_tensor_tensor(p_out, p_in, w, p_out, ALU.mult, ALU.add)
                            link(dve.scalar_tensor_tensor(s_out, s_in, w, s_out, ALU.mult, ALU.add))

                done, per_step = 0, 11
                for g in range(G4):
                    dve.wait_ge(sig("glu_gate"), g + 1)
                    dve.wait_ge(sig("glu_mm"), g + 1)
                    to_sequences(gluT[:, g, :], CW, HC, 2 * (g % 2), gate_tmp[g % 2], "glu")
                    make_lo(("wcx", g))
                    if g:
                        taps(done, done + per_step)
                        done += per_step
                for g in range(G4):
                    dve.wait_ge(sig("cx_gate"), g + 1)
                    wait_column(dve, "cx", "wcx", g, 1)
                    to_sequences(cxT[:, g, :], DW, HDD, 2 * (g % 2) + 1, gate_tmp[g % 2], "cx")
                    make_lo(("wgb", g) if g < 2 else ("wout1", g - 2))
                    short_conv(g)
                    taps(done, done + per_step - 2)
                    done += per_step - 2
                for u in range(2):
                    for o in range(2):
                        j = 2 * u + o
                        wait_column(dve, "gb", "wgb", u, o)
                        v = cd[:, j, :].rearrange("p (b n) -> p b n", b=2)
                        dve.tensor_tensor(v, v, PAIR[j][:, :, 0:MOVE], ALU.mult).then_inc(sig("d_out"), 1)
                    make_lo(("wout1", 2 + u))
                taps(done, len(TAPS))
                dve.wait_ge(sig("d_hi"), 1)
                lo_of(xlo[:, G4:KC, :], cd, xhi[:, G4:KC, :]).then_inc(sig("d_lo"), 1)

                def conv_statistics(t):
                    dve.wait_ge(sig("c_rows"), t + 1)
                    statistics("c", t, rows(t), [ps[0:rows(t), C_ROWS_BANK[t], :]])

                def conv_norm(t):
                    m = rows(t)
                    if t >= 2:
                        dve.wait_ge(sig("c_tr"), t - 1)
                    dve.wait_ge(sig("c_rstd"), past("c_rstd") + t + 1)
                    dve.tensor_scalar(ln_rows[t % 2][0:m, :], ps[0:m, C_ROWS_BANK[t], :], mv[0:m, t, 0:1], rstd[0:m, t:t + 1],
                                      ALU.subtract, ALU.mult).then_inc(sig("c_norm"), 1)

                conv_statistics(0)
                conv_norm(0)
                conv_statistics(1)
                conv_norm(1)
                conv_statistics(2)
                conv_lo(0)
                conv_norm(2)
                conv_statistics(3)
                conv_lo(1)
                conv_norm(3)
                conv_statistics(4)
                conv_lo(2)
                conv_norm(4)
                conv_lo(3)

            def conv_lo(t):
                dve.wait_ge(sig("c_hi"), t + 1)
                lo_of(xlo[:, 0:G4, cols(t)], acc[:, :, cols(t)], xhi[:, 0:G4, cols(t)]).then_inc(sig("c_lo"), 1)

            for l in range(DEPTH):
                if l:
                    conv_layer()
                out_norm(f"out{l}", f"wout{l}", lambda: [make_lo((f"wq{l}", q)) for q in range(3)], lambda: make_lo((f"wq{l}", 3)))
                attention(l)
                def router_lo():
                    dve.wait_ge(sig(f"wr{l}_hi"), past(f"wr{l}_hi") + 1)
                    lo_of(wrlo[:, :, :], wr_rows, wrhi[:, :, :]).then_inc(sig(f"wr{l}_lo"), 1)
                    for k in range(3):
                        make_lo_moe(l, k, 0)
                out_norm(f"o{l}", f"wo{l}", router_lo, lambda: None)
                router(l)
                experts(l)
                further(l)
                combine(l, [("wglu", g) for g in range(G4)] if l < DEPTH - 1 else [])

        @block.gpsimd
        def _(pool):
            link = chained(pool, "pool_chain")
            consts = sig("consts")
            link(pool.memset(ident[:, :], 0.0))
            pool.affine_select(out=ident[:, :], in_=ident[:, :], compare_op=ALU.not_equal, fill=1.0, base=0,
                               pattern=[[-1, P]], channel_multiplier=1).then_inc(consts, 1)
            link(pool.memset(before[:, :], 1.0))
            pool.affine_select(out=before[:, :], in_=before[:, :], compare_op=ALU.is_gt, fill=0.0, base=0,
                               pattern=[[1, P]], channel_multiplier=-1).then_inc(consts, 1)
            pool.memset(ones[:, :], 1.0).then_inc(consts, 1)
            pool.iota(iota[:, :], pattern=[[1, P]], base=0, channel_multiplier=0, allow_small_or_imprecise_dtypes=True).then_inc(consts, 1)
            pool.iota(tok2[:, :, 0], pattern=[[P, TILES]], base=0, channel_multiplier=0, allow_small_or_imprecise_dtypes=True)
            pool.iota(tok2[:, :, 1], pattern=[[0, TILES]], base=0, channel_multiplier=1, allow_small_or_imprecise_dtypes=True).then_inc(consts, 1)
            pool.iota(slot0[:, :], pattern=[[SLOTS, EXPERTS]], base=0, channel_multiplier=0, allow_small_or_imprecise_dtypes=True).then_inc(consts, 1)
            pool.iota(inv_count[:, :], pattern=[[1, HIST + 1]], base=1, channel_multiplier=0, allow_small_or_imprecise_dtypes=True).then_inc(consts, 1)
            pool.iota(falling[:, :], pattern=[[-1, 4]], base=4, channel_multiplier=0, allow_small_or_imprecise_dtypes=True)
            pool.memset(minus_half[:, :], -0.5).then_inc(consts, 1)
            link(pool.memset(valid[:, :], 1.0))
            pool.affine_select(out=valid[:, LASTT:TILES], in_=valid[:, LASTT:TILES], compare_op=ALU.is_ge, fill=0.0, base=NS - 1,
                               pattern=[[0, 1]], channel_multiplier=-1).then_inc(consts, 1)

            def load_gb(g, b):
                n = g.shape[0]
                pool.dma_start(gb[:, 0, 0:n], g.partition_broadcast(P)).then_inc(sig("gb_landed"), 16)
                pool.dma_start(gb[:, 1, 0:n], b.partition_broadcast(P)).then_inc(sig("gb_landed"), 16)

            def reciprocal_deviation(tag, t, m):
                pool.wait_ge(sig(tag + "_mv"), past(tag + "_mv") + t + 1)
                link(pool.tensor_scalar(ve[0:m, t:t + 1], mv[0:m, t, 1:2], EPS, None, ALU.add))
                pool.tensor_tensor(rstd[0:m, t:t + 1], ve[0:m, t:t + 1], minus_half[0:m, :], ALU.pow).then_inc(sig(tag + "_rstd"), 1)

            def add_bias(tag, t, m, out, bias):
                pool.wait_ge(sig(tag + "_gain"), past(tag + "_gain") + t + 1)
                pool.tensor_tensor(out, out, bias, ALU.add).then_inc(sig(tag + "_row"), 1)

            load_gb(a["ln_v_g"][0], a["ln_v_b"][0])
            n = 0
            for l in range(DEPTH):
                if l:
                    pool.wait_ge(sig("ws_copied"), past("ws_copied") + 1)
                    pool.affine_select(out=wsT, in_=wsT, compare_op=ALU.is_ge, fill=0.0, base=0,
                                       pattern=[[0, G4], [1, P]], channel_multiplier=-1).then_inc(sig("ws_masked"), 1)
                    link(pool.memset(wsS, 0.0))
                    pool.wait_ge(sig("ws_masked"), 1)
                    for b in range(NB):
                        pool.dma_start(wsS[b * TS:(b + 1) * TS, :, b * TS:(b + 1) * TS], wsT[0:TS, :, 0:TS]).then_inc(sig("wss_landed"), 16)
                for out in (o_memk, o_memv):
                    for m in range(MT):
                        pool.wait_ge(sig("kv_copied"), n + 1)
                        pool.dma_start(out[l, 0, m * P:(m + 1) * P].rearrange("m h c -> m (h c)"), kv_rows[n % 2]).then_inc(sig(f"kv_stored{n % 2}"), 16)
                        n += 1

            for t in range(TILES):
                m = rows(t)
                v = uv[t % 2][0:m, 512:1024]
                reciprocal_deviation("v", t, m)
                if t == 0:
                    pool.wait_ge(sig("gb_landed"), GB_LOADS["lnv"])
                add_bias("v", t, m, v, gb[0:m, 1, 0:512])
            pool.wait_ge(sig("v_row"), past("v_row") + TILES)
            pool.dma_start(o_chunk[0].rearrange("b t n -> (b t) n"), uv[LASTT % 2][0:NS, 512:1024]).then_inc(sig("stored"), 16)
            load_gb(a["ln_g"][0, 0], a["ln_b"][0, 0])
            for g in range(G4):
                ins = pool.tensor_copy(flat[:, 0, g, :].rearrange("p (b s) -> p b s", b=NB), zT[:, g, ZW:ZL].rearrange("p (b s) -> p b s", b=NB)[:, :, HIST:])
            ins.then_inc(sig("z_flat"), 1)
            pool.dma_start(o_pool_s[0][:, 0:HIST - TS, :], a["state_pool"][0][:, TS:HIST, :]).then_inc(sig("stored"), 16)
            pool.wait_ge(sig("stored"), 16 * 2)

            def norm_tiles(tag):
                for t in range(TILES):
                    m = rows(t)
                    reciprocal_deviation(tag, t, m)
                    if t == 0:
                        pool.wait_ge(sig("gb_landed"), GB_LOADS[tag])
                    add_bias(tag, t, m, h[0:m, t, :], gb[0:m, 1, :])

            def next_gb(tag, l, which, after):
                for name, value in after:
                    pool.wait_ge(sig(name), past(name) + value)
                load_gb(a["ln_g"][l, which], a["ln_b"][l, which])

            def experts(l):
                def gather(c, i):
                    n = c + 2 * i
                    pool.wait_ge(sig(f"tok{l}"), past(f"tok{l}") + n + 1)
                    if c >= 2:
                        pool.wait_ge(sig(f"xg{l}_tr"), past(f"xg{l}_tr") + n - 1)
                    if l or c:
                        pool.wait_ge(sig("marked"), l * EXPERTS + n)
                    pool.tensor_tensor(wait_mark[:, 0:1], minus_half[0:1, :], minus_half[0:1, :], ALU.add).then_inc(sig("marked"), 1)
                    pool.indirect_dma_start(xg[c % 2], None, h_dram, bass.IndirectOffsetOnAxis(tok_of[c % 2][:, 0:1], 0)).then_inc(sig(f"gathered{c % 2}"), 16)

                def step(c, i):
                    if c < EXPERTS - 1:
                        gather(c + 1, i)

                pool.wait_ge(sig("h_stored"), 32 * (l + 1))
                gather(0, 0)
                gather(1, 0)
                for c in range(1, 3):
                    step(c, 0)
                with pool.Fori(0, EXPERTS // 2 - 3) as i:
                    step(3, i)
                    step(4, i)
                for c in range(EXPERTS - 3, EXPERTS - 1):
                    step(c, 0)

            def further(l):
                pool.wait_ge(sig(f"xg{l}_tr"), past(f"xg{l}_tr") + EXPERTS)
                pool.tensor_tensor(wait_mark[:, 1 + l:2 + l], minus_half[0:1, :], minus_half[0:1, :], ALU.add).then_inc(again(l, "marked"), 1)
                n = further_blocks(pool, l)
                def one_block(i):
                    pool.wait_ge(again(l, "tok"), 1 + i)
                    pool.wait_ge(again(l, "marked"), 1 + i)
                    pool.tensor_tensor(wait_mark[:, 1 + l:2 + l], minus_half[0:1, :], minus_half[0:1, :], ALU.add).then_inc(again(l, "marked"), 1)
                    pool.indirect_dma_start(xg[0], None, h_dram, bass.IndirectOffsetOnAxis(tok_of[0][:, 0:1], 0)).then_inc(again(l, "gathered"), 16)

                with pool.If(n > 0):
                    one_block(0)
                with pool.If(n > 1):
                    with pool.Fori(1, FURTHER) as i:
                        with pool.If(n > i):
                            one_block(i)

            def combine(l):
                tag = f"moe{l}"
                pool.wait_ge(sig(f"slots{l}"), past(f"slots{l}") + 1)
                for par in range(2):
                    pool.wait_ge(sig(f"y{par}_stored"), 16 * (l + 1) * EXPERTS // 2)

                def fetch(t):
                    m = rows(t)
                    if t >= 2:
                        pool.wait_ge(sig(tag + "_combined"), past(tag + "_combined") + t - 1)
                    for j in range(2):
                        pool.indirect_dma_start(back[t % 2][j][0:m, :], None, y_dram, bass.IndirectOffsetOnAxis(slot_of[0:m, t, j:j + 1], 0)).then_inc(sig(f"back_landed{t % 2}"), 16)
                fetch(0)
                fetch(1)
                for t in range(TILES + 1):
                    if t < TILES:
                        reciprocal_deviation(tag, t, rows(t))
                    if t + 2 < TILES:
                        fetch(t + 2)
                    if t == 0:
                        pool.wait_ge(sig("gb_landed"), GB_LOADS[tag])
                        continue
                    m = rows(t - 1)
                    add_bias(tag, t - 1, m, h[0:m, t - 1, :], gb[0:m, 1, :])
                    if l == DEPTH - 1:
                        pool.wait_ge(sig(tag + "_row"), past(tag + "_row") + t)
                        out = y_prompt[0, (t - 1) * P:t * P, :] if t - 1 < LASTT else y_sample.rearrange("b t n -> (b t) n")
                        pool.dma_start(out, h[0:m, t - 1, :]).then_inc(sig("stored"), 16)

            def conv_chunk():
                pool.wait_ge(sig("hist1_copied"), past("hist1_copied") + 1)
                pool.wait_ge(sig("moe0_gain"), past("moe0_gain") + TILES)
                pool.wait_ge(sig("moe0_row"), past("moe0_row") + TILES)
                n = 0
                for g, last, dst in ((0, TAPS_C, acc[:, 0, :]), (G4 - 1, POOL_TAPS, conv_rest)):
                    pool.wait_ge(sig("glu"), g + 1)
                    src, dst_s = gluT[:, g, :], dst[:, SEQ:TOK].rearrange("p (b s) -> p b s", b=NB)
                    for k in range(last):
                        w, bias = ccol[:, g, k:k + 1], ccol[:, g, TAPS_C + TAPS_D:TAPS_C + TAPS_D + 1]
                        part = conv_part[k % 2]
                        part_s = part[:, SEQ:TOK].rearrange("p (b s) -> p b s", b=NB)
                        src_p, src_s = src[:, k:k + SEQ], src[:, CW:].rearrange("p (b s) -> p b s", b=NB)[:, :, k:k + TS]
                        if k == 0:
                            pool.tensor_scalar(dst[:, 0:SEQ], src_p, w, bias, ALU.mult, ALU.add)
                            link(pool.tensor_scalar(dst_s, src_s, w, bias, ALU.mult, ALU.add))
                            continue
                        pool.tensor_tensor(part[:, 0:SEQ], src_p, w.to_broadcast([P, SEQ]), ALU.mult)
                        link(pool.tensor_tensor(part_s, src_s, w.unsqueeze(2).to_broadcast([P, NB, TS]), ALU.mult))
                        ins = pool.tensor_tensor(dst, dst, part, ALU.add)
                        if k < last - 1:
                            link(ins)
                    ins.then_inc(sig("conv_pool"), 1)

            def conv_layer():
                conv_chunk()
                for t in range(TILES):
                    if t == 0:
                        pool.wait_ge(sig("cx"), G4)
                        for g in range(G4):
                            ins = pool.tensor_copy(flat[:, 0, g, :].rearrange("p (b s) -> p b s", b=NB), gluT[:, g, CW:CL].rearrange("p (b s) -> p b s", b=NB)[:, :, HC:])
                        ins.then_inc(sig("flat_ready"), 1)
                        for g in range(G4):
                            ins = pool.tensor_copy(flat[:, 1, g, 0:NB * HDD].rearrange("p (b s) -> p b s", b=NB), cxT[:, g, DW:DL].rearrange("p (b s) -> p b s", b=NB)[:, :, DSW - HDD:])
                        ins.then_inc(sig("flat_ready"), 1)
                    reciprocal_deviation("c", t, rows(t))
                pool.dma_start(o_cc_s[0][:, 0:HC - TS, :], a["state_conv_c"][0][:, TS:HC, :]).then_inc(sig("stored"), 16)
            stores = 2
            for l in range(DEPTH):
                if l:
                    conv_layer()
                    stores += 1
                    next_gb("out1", 1, 0, [("tails_stored", 16 * (1 + NB + 3 + NB))])
                norm_tiles(f"out{l}")
                if l:
                    pool.wait_ge(sig("lg0_copied"), past("lg0_copied") + 1)
                pool.dma_start(wr_rows[:, :, 0:GROUPS], a["w_group"][l].rearrange("(k p) n -> p k n", p=P)).then_inc(sig("wr_landed"), 16)
                pool.dma_start(wr_rows[:, :, GROUPS:ROUTE], a["w_router"][l].rearrange("(k p) n -> p k n", p=P)).then_inc(sig("wr_landed"), 16)
                with nc.allow_non_contiguous_dma(reason="20 words"):
                    pool.dma_start(rbias[0:GROUPS, :], a["b_group"][l].rearrange("(g o) -> g o", o=1)).then_inc(sig("wr_landed"), 16)
                    pool.dma_start(rbias[GROUPS:ROUTE, :], a["b_router"][l].rearrange("(g o) -> g o", o=1)).then_inc(sig("wr_landed"), 16)
                next_gb(f"o{l}", l, 1, [(f"sscore{l}_mm", NB)])
                norm_tiles(f"o{l}")
                pool.wait_ge(sig(f"o{l}_row"), past(f"o{l}_row") + TILES)
                pool.dma_start(h_dram[0:SEQ, :].rearrange("(t p) n -> p t n", p=P), h[:, 0:LASTT, :]).then_inc(sig("h_stored"), 16)
                pool.dma_start(h_dram[SEQ:TOK, :], h[0:NS, LASTT, :]).then_inc(sig("h_stored"), 16)
                next_gb(f"moe{l}", l, 2, [])
                pool.wait_ge(sig(f"o{l}_lo"), past(f"o{l}_lo") + TILES)
                pool.memset(logitT[:, TOK:TILES * P], 0.0).then_inc(sig(f"lg{l}_zeroed"), 1)
                experts(l)
                further(l)
                combine(l)
            pool.wait_ge(sig("stored"), 16 * (stores + TILES))
            for par in range(2):
                pool.wait_ge(sig(f"kv_stored{par}"), 16 * 4)


_INS = ["x_prompt", "x_sample", "cache_mem_k", "cache_mem_v", "state_pool", "state_conv_c", "state_conv_d", "mem_prompt",
        "w_in_ab", "ln_v_g", "ln_v_b", "w_spatial", "b_spatial", "w_pool", "pool_scale", "w_out_ab", "w_in_cd", "conv_c_w",
        "conv_c_b", "ln_c_g", "ln_c_b", "conv_d_w", "w_out_cd", "w_q", "w_k", "w_v", "w_o", "w_group", "b_group",
        "w_router", "b_router", "w_gate", "w_up", "w_down", "ln_g", "ln_b"]


def _out_shapes(x):
    depth, batch, n_mem = x["w_q"].shape[0], x["x_prompt"].shape[0], x["mem_prompt"].shape[1]
    heads, head_dim = x["cache_mem_k"].shape[3:]
    db, ts = x["x_sample"].shape[:2]
    ne, no = x["state_pool"].shape[0], x["state_conv_c"].shape[0]
    half = x["state_pool"].shape[3]
    return [x["x_prompt"].shape, x["x_sample"].shape, (depth, batch, n_mem, heads, head_dim), (depth, batch, n_mem, heads, head_dim),
            (ne, batch) + x["state_pool"].shape[2:], (no, batch) + x["state_conv_c"].shape[2:], (no, batch) + x["state_conv_d"].shape[2:],
            (ne, db, ts, half), x["state_pool"].shape, x["state_conv_c"].shape, x["state_conv_d"].shape]


def kernel(**inputs):
    import numpy as _np
    import concourse.bacc as _bacc
    from concourse import mybir as _mybir
    from concourse.bass_utils import run_bass_kernel_spmd as _run

    nc = _bacc.Bacc("TRN2", target_bir_lowering=False, num_devices=1)
    arrays, ins, outs = {}, {}, []
    for name in _INS:
        x = _np.ascontiguousarray(inputs[name])
        arrays[f"in_{name}_dram"] = x
        ins[name] = nc.dram_tensor(f"in_{name}_dram", x.shape, _mybir.dt.from_np(x.dtype), kind="ExternalInput").ap()
    shapes = _out_shapes(arrays and {n: arrays[f"in_{n}_dram"] for n in _INS})
    for i, shape in enumerate(shapes):
        outs.append(nc.dram_tensor(f"out_{i}_dram", tuple(shape), _mybir.dt.float32, kind="ExternalOutput").ap())
    trunk_kernel(nc, ins, outs)
    r = _run(nc, [arrays], core_ids=[0])
    return tuple(r.results[0][f"out_{i}_dram"] for i in range(len(shapes)))
```
